# Optimizing a Trainium2 kernel written in Bass

```python
import jax, jax.numpy as jnp
from jax import lax
import numpy as np

D_MODEL = 1024
BATCH = 1
SEQ = 512
DEPTH = 2

N_EVEN = (DEPTH + 1) // 2
N_ODD = DEPTH // 2

HEAD_DIM = 64
D_CONV_A = D_MODEL // 2
N_FOX_HEADS = (D_MODEL // 2) // HEAD_DIM
D_FOX = N_FOX_HEADS * HEAD_DIM
SHORT_CONV_WIDTH = 3
CONFORMER_CONV_WIDTH = 31
BLOCK_Q = 128
_FF_RAW = -(-8 * D_MODEL // 3)
D_FF = -(-_FF_RAW // 256) * 256
RMS_EPS = 1e-6
LN_EPS = 1e-5

OFF_GB = 0
OFF_GC = OFF_GB + D_CONV_A
OFF_XA = OFF_GC + D_CONV_A
OFF_Q = OFF_XA + D_CONV_A
OFF_K = OFF_Q + D_FOX
OFF_V = OFF_K + D_FOX
OFF_F = OFF_V + D_FOX
D_IN_EVEN = OFF_F + N_FOX_HEADS


def rms_norm(x, g):
    xf = x.astype(jnp.float32)
    y = xf * lax.rsqrt(jnp.mean(xf * xf, axis=-1, keepdims=True) + RMS_EPS)
    return (y * g.astype(jnp.float32)).astype(x.dtype)

def layer_norm(x, g, b):
    xf = x.astype(jnp.float32)
    mu = jnp.mean(xf, axis=-1, keepdims=True)
    xc = xf - mu
    var = jnp.mean(xc * xc, axis=-1, keepdims=True)
    y = xc * lax.rsqrt(var + LN_EPS)
    return (y * g.astype(jnp.float32) + b.astype(jnp.float32)).astype(x.dtype)

def causal_depthwise_conv(x, w):
    k_width, ch = w.shape
    return lax.conv_general_dilated(
        x, w[:, None, :].astype(x.dtype), window_strides=(1,),
        padding=[(k_width - 1, 0)], dimension_numbers=("NWC", "WIO", "NWC"),
        feature_group_count=ch)

def forgetting_attention(q, k, v, log_f):
    seq = q.shape[1]
    c = jnp.cumsum(log_f, axis=1).transpose(0, 2, 1)
    scale = HEAD_DIM ** -0.5
    outs = []
    for start in range(0, seq, BLOCK_Q):
        end = start + BLOCK_Q
        s = jnp.einsum("bqhd,bkhd->bhqk", q[:, start:end], k[:, :end],
                       preferred_element_type=jnp.float32) * scale
        bias = c[:, :, start:end, None] - c[:, :, None, :end]
        mask = (start + jnp.arange(BLOCK_Q))[:, None] >= jnp.arange(end)[None, :]
        s = jnp.where(mask, s + bias, -jnp.inf)
        p = jax.nn.softmax(s, axis=-1)
        outs.append(jnp.einsum("bhqk,bkhd->bqhd", p.astype(v.dtype), v[:, :end]))
    return jnp.concatenate(outs, axis=1)

def shortconv_fox_mixer(h, w_in, b_f, conv_w, w_out):
    bsz, seq, _ = h.shape
    proj = h @ w_in
    gate_b = proj[..., OFF_GB:OFF_GC]
    gate_c = proj[..., OFF_GC:OFF_XA]
    xa = proj[..., OFF_XA:OFF_Q]
    y_a = gate_b * causal_depthwise_conv(gate_c * xa, conv_w)
    q = proj[..., OFF_Q:OFF_K].reshape(bsz, seq, N_FOX_HEADS, HEAD_DIM)
    k = proj[..., OFF_K:OFF_V].reshape(bsz, seq, N_FOX_HEADS, HEAD_DIM)
    v = proj[..., OFF_V:OFF_F].reshape(bsz, seq, N_FOX_HEADS, HEAD_DIM)
    log_f = jax.nn.log_sigmoid((proj[..., OFF_F:] + b_f).astype(jnp.float32))
    y_b = forgetting_attention(q, k, v, log_f).reshape(bsz, seq, D_FOX)
    return jnp.concatenate([y_a, y_b.astype(h.dtype)], axis=-1) @ w_out

def conformer_conv_module(h, w_pw1, b_pw1, w_dw, b_dw, ln_g, ln_b, w_pw2, b_pw2):
    a, g = jnp.split(h @ w_pw1 + b_pw1, 2, axis=-1)
    u = a * jax.nn.sigmoid(g)
    u = causal_depthwise_conv(u, w_dw) + b_dw
    u = jax.nn.silu(layer_norm(u, ln_g, ln_b))
    return u @ w_pw2 + b_pw2

def swiglu_ffn(h, w_ffn_in, w_ffn_out):
    g, u = jnp.split(h @ w_ffn_in, 2, axis=-1)
    return (jax.nn.silu(g) * u) @ w_ffn_out

def first_inputs(seed: int = 0) -> dict:
    key = jax.random.key(seed)
    ks = jax.random.split(key, 20)
    f32 = jnp.float32
    nrm = lambda k, shape, s: (jax.random.normal(k, shape, f32) * s)
    gain = lambda k, shape: 1.0 + 0.05 * jax.random.normal(k, shape, f32)
    return {
        "x": jax.random.normal(ks[0], (BATCH, SEQ, D_MODEL), f32),
        "norm_mix_pre": gain(ks[1], (DEPTH, D_MODEL)),
        "norm_mix_post": gain(ks[2], (DEPTH, D_MODEL)),
        "norm_ffn_pre": gain(ks[3], (DEPTH, D_MODEL)),
        "norm_ffn_post": gain(ks[4], (DEPTH, D_MODEL)),
        "w_in": nrm(ks[5], (N_EVEN, D_MODEL, D_IN_EVEN), D_MODEL ** -0.5),
        "b_forget": 1.0 + 3.0 * jax.random.uniform(ks[6], (N_EVEN, N_FOX_HEADS), f32),
        "w_short_conv": nrm(ks[7], (N_EVEN, SHORT_CONV_WIDTH, D_CONV_A), SHORT_CONV_WIDTH ** -0.5),
        "w_out": nrm(ks[8], (N_EVEN, D_CONV_A + D_FOX, D_MODEL), (D_CONV_A + D_FOX) ** -0.5),
        "w_pw1": nrm(ks[9], (N_ODD, D_MODEL, 2 * D_MODEL), D_MODEL ** -0.5),
        "b_pw1": nrm(ks[10], (N_ODD, 2 * D_MODEL), 0.02),
        "w_dw": nrm(ks[11], (N_ODD, CONFORMER_CONV_WIDTH, D_MODEL), CONFORMER_CONV_WIDTH ** -0.5),
        "b_dw": nrm(ks[12], (N_ODD, D_MODEL), 0.02),
        "ln_g": gain(ks[13], (N_ODD, D_MODEL)),
        "ln_b": nrm(ks[14], (N_ODD, D_MODEL), 0.02),
        "w_pw2": nrm(ks[15], (N_ODD, D_MODEL, D_MODEL), D_MODEL ** -0.5),
        "b_pw2": nrm(ks[16], (N_ODD, D_MODEL), 0.02),
        "w_ffn_in": nrm(ks[17], (DEPTH, D_MODEL, 2 * D_FF), D_MODEL ** -0.5),
        "w_ffn_out": nrm(ks[18], (DEPTH, D_FF, D_MODEL), D_FF ** -0.5),
    }

def first_block(x, norm_mix_pre, norm_mix_post, norm_ffn_pre, norm_ffn_post,
              w_in, b_forget, w_short_conv, w_out,
              w_pw1, b_pw1, w_dw, b_dw, ln_g, ln_b, w_pw2, b_pw2,
              w_ffn_in, w_ffn_out):
    h = x
    for layer in range(DEPTH):
        j = layer // 2
        u = rms_norm(h, norm_mix_pre[layer])
        if layer % 2 == 0:
            m = shortconv_fox_mixer(u, w_in[j], b_forget[j], w_short_conv[j], w_out[j])
        else:
            m = conformer_conv_module(u, w_pw1[j], b_pw1[j], w_dw[j], b_dw[j],
                                      ln_g[j], ln_b[j], w_pw2[j], b_pw2[j])
        h = h + rms_norm(m, norm_mix_post[layer])
        f = swiglu_ffn(rms_norm(h, norm_ffn_pre[layer]), w_ffn_in[layer], w_ffn_out[layer])
        h = h + rms_norm(f, norm_ffn_post[layer])
    return h


N_A_LAYERS = DEPTH // 2
N_B_LAYERS = DEPTH - N_A_LAYERS
HG_EXPAND = 128
HG_HEADS = D_MODEL // HG_EXPAND
HG_DV = D_MODEL // HG_HEADS
HG_CHUNK = 32
ATT_HEAD_DIM = 64
ATT_Q_HEADS = D_MODEL // ATT_HEAD_DIM
ATT_KV_HEADS = 2
ATT_GROUP = ATT_Q_HEADS // ATT_KV_HEADS
WINDOW = 128
D_FF_2 = 2816
CONV_WIDTH = 3
EPS = 1e-6


F32 = jnp.float32

def rms_norm_2(x, g):
    xf = x.astype(F32)
    xf = xf * lax.rsqrt(jnp.mean(xf * xf, axis=-1, keepdims=True) + EPS)
    return (xf * g.astype(F32)).astype(x.dtype)

def alibi_slopes(n_heads):
    return jnp.asarray(2.0 ** (-8.0 * np.arange(1, n_heads + 1) / n_heads), F32)

def hgrn2_chunked(q, k, v, logf):
    b_, s_, h_, dk = q.shape
    dv = v.shape[-1]
    n_chunks = s_ // HG_CHUNK

    def to_chunks(t):
        return t.reshape(b_, n_chunks, HG_CHUNK, h_, t.shape[-1]).transpose(1, 0, 3, 2, 4)

    qc, kc, vc, gc = to_chunks(q), to_chunks(k), to_chunks(v), to_chunks(logf)
    causal = jnp.tril(jnp.ones((HG_CHUNK, HG_CHUNK), bool))[:, :, None]

    def step(state, inp):
        qb, kb, vb, gb = inp
        cum = jnp.cumsum(gb, axis=2)
        o_inter = jnp.einsum('bhtk,bhkv->bhtv', qb * jnp.exp(cum), state)
        rel = cum[:, :, :, None, :] - cum[:, :, None, :, :]
        decay = jnp.exp(jnp.where(causal, rel, -jnp.inf))
        scores = jnp.einsum('bhtk,bhsk,bhtsk->bhts', qb, kb, decay)
        o_intra = jnp.einsum('bhts,bhsv->bhtv', scores, vb)
        last = cum[:, :, -1:, :]
        new_state = (jnp.exp(last[:, :, 0, :])[..., None] * state
                     + jnp.einsum('bhsk,bhsv->bhkv', kb * jnp.exp(last - cum), vb))
        return new_state, o_inter + o_intra

    s0 = jnp.zeros((b_, h_, dk, dv), F32)
    _, o = lax.scan(step, s0, (qc, kc, vc, gc))
    return o.transpose(1, 0, 3, 2, 4).reshape(b_, s_, h_, dv)

def hgrn2_mixer(x, w_in, lower_bound, out_norm, w_out):
    b_, s_, _ = x.shape
    q, f, i, g = jnp.split(x @ w_in, 4, axis=-1)
    q = jax.nn.silu(q.astype(F32)) * HG_EXPAND ** -0.5
    forget = lower_bound + (1.0 - lower_bound) * jax.nn.sigmoid(f.astype(F32))
    logf = jnp.log(forget)
    k = 1.0 - forget
    heads = lambda t: t.reshape(b_, s_, HG_HEADS, -1)
    o = hgrn2_chunked(heads(q), heads(k), heads(i.astype(F32)), heads(logf))
    o = rms_norm_2(o, out_norm) * jax.nn.silu(heads(g.astype(F32)))
    return o.reshape(b_, s_, D_MODEL).astype(x.dtype) @ w_out

def shared_kv(h, kv_norm, w_kv):
    b_, s_, _ = h.shape
    k, v = jnp.split(rms_norm_2(h, kv_norm) @ w_kv, 2, axis=-1)
    return (k.reshape(b_, s_, ATT_KV_HEADS, ATT_HEAD_DIM),
            v.reshape(b_, s_, ATT_KV_HEADS, ATT_HEAD_DIM))

def swa_sink_attention(x, k, v, w_q, sinks, w_o):
    b_, s_, _ = x.shape
    nb = s_ // WINDOW
    q = (x @ w_q).reshape(b_, nb, WINDOW, ATT_KV_HEADS, ATT_GROUP, ATT_HEAD_DIM)

    def band(t):
        tb = t.reshape(b_, nb, WINDOW, ATT_KV_HEADS, ATT_HEAD_DIM)
        prev = jnp.pad(tb[:, :-1], ((0, 0), (1, 0), (0, 0), (0, 0), (0, 0)))
        return jnp.concatenate([prev, tb], axis=2)

    kb, vb = band(k), band(v)
    scores = jnp.einsum('bnqkgd,bnskd->bnkgqs', q.astype(F32), kb.astype(F32)) * ATT_HEAD_DIM ** -0.5
    q_idx = jnp.arange(WINDOW)[:, None] + WINDOW
    k_idx = jnp.arange(2 * WINDOW)[None, :]
    dist = q_idx - k_idx
    key_abs = (jnp.arange(nb) * WINDOW)[:, None] + jnp.arange(2 * WINDOW)[None, :] - WINDOW
    valid = ((dist >= 0) & (dist < WINDOW))[None] & (key_abs >= 0)[:, None, :]
    slopes = alibi_slopes(ATT_Q_HEADS).reshape(ATT_KV_HEADS, ATT_GROUP)
    scores = scores - slopes[:, :, None, None] * dist.astype(F32)
    scores = jnp.where(valid[None, :, None, None], scores, -jnp.inf)
    sink = sinks.astype(F32).reshape(ATT_KV_HEADS, ATT_GROUP)[None, None, :, :, None, None]
    m = jnp.maximum(jnp.max(scores, axis=-1, keepdims=True), sink)
    e = jnp.exp(scores - m)
    probs = e / (jnp.sum(e, axis=-1, keepdims=True) + jnp.exp(sink - m))
    out = jnp.einsum('bnkgqs,bnskd->bnqkgd', probs, vb.astype(F32))
    return out.reshape(b_, s_, ATT_Q_HEADS * ATT_HEAD_DIM).astype(x.dtype) @ w_o

def conv_ffn(x, w_up, conv_w, conv_b, w_down):
    s_ = x.shape[1]
    gate, val = jnp.split(x @ w_up, 2, axis=-1)
    gp = jnp.pad(gate, ((0, 0), (CONV_WIDTH - 1, 0), (0, 0)))
    conv = conv_b
    for j in range(CONV_WIDTH):
        conv = conv + conv_w[j] * gp[:, j:j + s_]
    return (jax.nn.silu(conv) * val) @ w_down

def second_inputs(seed: int = 0) -> dict:
    key = jax.random.key(seed)
    ks = jax.random.split(key, 18)
    D = D_MODEL
    HQD = ATT_Q_HEADS * ATT_HEAD_DIM
    KVD = ATT_KV_HEADS * ATT_HEAD_DIM

    def w(k, shape, fan_in):
        return jax.random.normal(k, shape, F32) * fan_in ** -0.5

    def gain(k, shape):
        return 1.0 + 0.02 * jax.random.normal(k, shape, F32)

    return {
        'x': jax.random.normal(ks[0], (BATCH, SEQ, D), F32),
        'hg_norm': gain(ks[1], (N_A_LAYERS, D)),
        'hg_w_in': w(ks[2], (N_A_LAYERS, D, 4 * D), D),
        'hg_lb_logits': 0.1 * jax.random.normal(ks[3], (N_A_LAYERS + 1, D), F32),
        'hg_out_norm': gain(ks[4], (N_A_LAYERS, HG_DV)),
        'hg_w_out': w(ks[5], (N_A_LAYERS, D, D), D),
        'kv_norm': gain(ks[6], (D,)),
        'w_kv': w(ks[7], (D, 2 * KVD), D),
        'attn_norm': gain(ks[8], (N_B_LAYERS, D)),
        'attn_w_q': w(ks[9], (N_B_LAYERS, D, HQD), D),
        'attn_sinks': 0.5 * jax.random.normal(ks[10], (N_B_LAYERS, ATT_Q_HEADS), F32),
        'attn_w_o': w(ks[11], (N_B_LAYERS, HQD, D), HQD),
        'ffn_norm': gain(ks[12], (DEPTH, D)),
        'ffn_w_up': w(ks[13], (DEPTH, D, 2 * D_FF_2), D),
        'ffn_conv_w': w(ks[14], (DEPTH, CONV_WIDTH, D_FF_2), CONV_WIDTH),
        'ffn_conv_b': 0.02 * jax.random.normal(ks[15], (DEPTH, D_FF_2), F32),
        'ffn_w_down': w(ks[16], (DEPTH, D_FF_2, D), D_FF_2),
        'final_norm': gain(ks[17], (D,)),
    }

def second_block(x, hg_norm, hg_w_in, hg_lb_logits, hg_out_norm, hg_w_out, kv_norm, w_kv,
              attn_norm, attn_w_q, attn_sinks, attn_w_o, ffn_norm, ffn_w_up, ffn_conv_w,
              ffn_conv_b, ffn_w_down, final_norm):
    lower_bounds = jnp.cumsum(jax.nn.softmax(hg_lb_logits.astype(F32), axis=0), axis=0)
    h = x
    k_sh, v_sh = None, None
    for layer in range(DEPTH):
        if layer < N_A_LAYERS:
            a = layer
            h = h + hgrn2_mixer(rms_norm_2(h, hg_norm[a]), hg_w_in[a], lower_bounds[a],
                                hg_out_norm[a], hg_w_out[a])
        else:
            bi = layer - N_A_LAYERS
            if bi == 0:
                k_sh, v_sh = shared_kv(h, kv_norm, w_kv)
            h = h + swa_sink_attention(rms_norm_2(h, attn_norm[bi]), k_sh, v_sh,
                                       attn_w_q[bi], attn_sinks[bi], attn_w_o[bi])
        h = h + conv_ffn(rms_norm_2(h, ffn_norm[layer]), ffn_w_up[layer], ffn_conv_w[layer],
                         ffn_conv_b[layer], ffn_w_down[layer])
    return rms_norm_2(h, final_norm)


def setup_inputs(seed=0):
    out = dict(first_inputs(seed))
    for name, value in second_inputs(seed + 1).items():
        if name != "x":
            out[name + "_2"] = value
    return out


def reference(
    x, norm_mix_pre, norm_mix_post, norm_ffn_pre, norm_ffn_post, w_in, b_forget, w_short_conv,
    w_out, w_pw1, b_pw1, w_dw, b_dw, ln_g, ln_b, w_pw2, b_pw2, w_ffn_in, w_ffn_out, hg_norm_2,
    hg_w_in_2, hg_lb_logits_2, hg_out_norm_2, hg_w_out_2, kv_norm_2, w_kv_2, attn_norm_2,
    attn_w_q_2, attn_sinks_2, attn_w_o_2, ffn_norm_2, ffn_w_up_2, ffn_conv_w_2, ffn_conv_b_2,
    ffn_w_down_2, final_norm_2,
):
    x = first_block(
        x, norm_mix_pre, norm_mix_post, norm_ffn_pre, norm_ffn_post, w_in, b_forget,
        w_short_conv, w_out, w_pw1, b_pw1, w_dw, b_dw, ln_g, ln_b, w_pw2, b_pw2, w_ffn_in,
        w_ffn_out,
    )
    return second_block(
        x, hg_norm_2, hg_w_in_2, hg_lb_logits_2, hg_out_norm_2, hg_w_out_2, kv_norm_2, w_kv_2,
        attn_norm_2, attn_w_q_2, attn_sinks_2, attn_w_o_2, ffn_norm_2, ffn_w_up_2, ffn_conv_w_2,
        ffn_conv_b_2, ffn_w_down_2, final_norm_2,
    )


_drawn_inputs = setup_inputs


def setup_inputs(seed=0):
    import zlib

    import numpy as np

    out = dict(_drawn_inputs(seed))
    spreads = {}
    factors = {'b_pw1': 4.04,
     'ln_b': 4.315,
     'hg_norm_2': 6.962,
     'hg_lb_logits_2': 8.0,
     'hg_out_norm_2': 8.0,
     'kv_norm_2': 8.0,
     'attn_norm_2': 8.0,
     'attn_sinks_2': 8.0,
     'ffn_norm_2': 5.213,
     'ffn_conv_b_2': 8.0,
     'final_norm_2': 2.837}
    for name, (base, spread) in spreads.items():
        noise = np.random.default_rng([zlib.crc32(name.encode()), seed]).standard_normal(out[name].shape)
        drawn = base * np.exp(spread * noise) if base else spread * noise
        out[name] = __import__('jax').numpy.asarray(drawn.astype(out[name].dtype))
    for name, factor in factors.items():
        out[name] = (out[name] * factor).astype(out[name].dtype)
    return out
```

```python
from contextlib import ExitStack

import concourse.bass as bass
from concourse import mybir

F32 = mybir.dt.float32
F32R = mybir.dt.float32r
U32 = mybir.dt.uint32
ALU = mybir.AluOpType
ACT = mybir.ActivationFunctionType
AX_X = mybir.AxisListType.X

P = 128
T = 512
D = 1024
KC = D // P
TT = T // P
FF = 2816
FC = FF // P
FOX_HEADS, FOX_DIM = 8, 64
HG_HEADS = 8
SWA_HEADS, SWA_DIM, WINDOW = 16, 64, 128
SHORT_TAPS, LONG_TAPS, FFN_TAPS = 3, 31, 3
RMS_EPS, LN_EPS = 1e-6, 1e-5
NEVER = -1e30
LEVELS = (1, 2, 4, 8, 16, 32, 64)

SLOT_PARTS = (
    ("a_q", 4), ("a_k", 4), ("a_v", 4), ("a_conv", 12), ("a_out", 8), ("a_ffn_in", 2 * FC), ("a_ffn_out", FC),
    ("b_in", 16), ("b_out", 8), ("b_ffn_in", 2 * FC), ("b_ffn_out", FC),
    ("c_fq", 16), ("c_i", 8), ("c_g", 8), ("c_out", 8), ("c_ffn_in", 2 * FC), ("c_ffn_out", FC),
    ("d_kv", 2), ("d_q", 8), ("d_out", 8), ("d_ffn_in", 2 * FC), ("d_ffn_out", FC),
)


def starts(parts):
    at, out = 0, {}
    for name, n in parts:
        out[name] = at
        at += n
    return out, at


SLOT, N_SLOTS = starts(SLOT_PARTS)

VEC_PARTS = (
    ("mix_pre", 16), ("mix_post", 16), ("ffn_pre", 16), ("ffn_post", 16),
    ("w_forget", KC * FOX_HEADS), ("b_forget", 1), ("short_conv", SHORT_TAPS * 4),
    ("b_pw1", 16), ("w_dw", LONG_TAPS * KC), ("b_dw", KC), ("ln_g", KC), ("ln_b", KC), ("b_pw2", KC),
    ("hg_norm", KC), ("lb_logits", 2 * KC), ("hg_out_norm", 1), ("kv_norm", KC), ("attn_norm", KC),
    ("sinks", SWA_HEADS), ("ffn_norm_2", 2 * KC), ("ffn_conv_w", 2 * FFN_TAPS * FC), ("ffn_conv_b", 2 * FC),
    ("final_norm", KC),
)
VEC, N_VEC = starts(VEC_PARTS)

STATS = ("a_pre", "a_post", "a_fpre", "a_fpost", "b_pre", "b_var", "b_post", "b_fpre", "b_fpost",
         "c_pre", "c_head", "c_fpre", "d_pre", "d_fpre", "final")
SQ, _ = starts([(s, KC) for s in STATS])
RS, _ = starts([(s, HG_HEADS if s == "c_head" else 1) for s in STATS])
SPLITS = ("a_pre", "a_gate", "a_fpre", "b_pre", "b_ln", "b_fpre", "c_pre", "c_out", "c_fpre", "d_kv", "d_q", "d_fpre")
SPLIT, _ = starts([(s, 4 if s == "a_gate" else KC) for s in SPLITS])
RESID, _ = starts([(s, KC) for s in ("a_mix", "a_ffn", "b_mix", "b_ffn", "c_mix", "c_ffn", "d_mix", "d_ffn")])
MADE, _ = starts([(s, KC) for s in ("a_mix", "a_ffn", "b_mix", "b_ffn")])
FULL, _ = starts([(s, KC - 1) for s in "abcd"])
HID, _ = starts([(s, FC) for s in "abcd"])
CONVG, _ = starts([(s, 2 * FC) for s in "cd"])


def build(nc, weights, vectors, squares, select_d, masks_d, x_t, out_t):
    with ExitStack() as ctx:
        def sb(name, shape, dt, where=ctx):
            return where.enter_context(nc.sbuf_tensor(name, shape, dt))

        def sem(name):
            return ctx.enter_context(nc.semaphore(name))

        h = sb("h", [P, KC, T], F32)
        with ExitStack() as one:
            m = sb("m", [P, KC, T], F32, one)
        u_hi = sb("u_hi", [P, KC, T], F32R)
        u_lo = sb("u_lo", [P, KC, T], F32R)
        raw = sb("raw", [P, 2, D], F32)
        w_hi = sb("w_hi", [P, 2, D], F32R)
        w_lo = sb("w_lo", [P, 2, D], F32R)
        sq = sb("sq", [P, 2, T], F32)
        ut = sb("ut", [P, 2, T], F32)
        rs = sb("rs", [P, T], F32)
        vec = sb("vec", [P, N_VEC], F32)
        consts = sb("consts", [P, 2 * P + 2 * WINDOW], F32)
        ident, causal, dist = consts[:, 0:P], consts[:, P:2 * P], consts[:, 2 * P:]
        ones = sb("ones", [P, P], F32)
        small = sb("small", [P, 64], F32)
        eps = sb("eps", [P, 2], F32)

        with ExitStack() as fox:
            aq = sb("aq", [P, 4, T], F32, fox)
            ak = sb("ak", [P, 4, T], F32, fox)
            av = sb("av", [P, TT, 512], F32, fox)
            az = sb("az", [P, 4, T + SHORT_TAPS - 1], F32, fox)
            agc = sb("agc", [P, T], F32, fox)
            ay = sb("ay", [P, T], F32, fox)
            ap = sb("ap", [P, TT, T], F32, fox)
            apt = sb("apt", [P, TT, T], F32, fox)
            ac = sb("ac", [FOX_HEADS, T], F32, fox)
            select = sb("select", [FOX_HEADS, FOX_HEADS, P], F32, fox)
            acat_hi = sb("acat_hi", [P, KC, T], F32R, fox)
            acat_lo = sb("acat_lo", [P, KC, T], F32R, fox)
        with ExitStack() as conf:
            bz = sb("bz", [P, KC, T + LONG_TAPS - 1], F32, conf)
            ba = sb("ba", [P, 2, T], F32, conf)
            by = sb("by", [P, KC, T], F32, conf)
            bmean = sb("bmean", [P, T], F32, conf)
            by_hi = sb("by_hi", [P, KC, T], F32R, conf)
            by_lo = sb("by_lo", [P, KC, T], F32R, conf)
        with ExitStack() as hgrn:
            with ExitStack() as qk:
                cq = sb("cq", [P, HG_HEADS, T], F32, qk)
                ck = sb("ck", [P, HG_HEADS, T], F32, qk)
            ccat_hi = sb("ccat_hi", [P, KC, T], F32R, hgrn)
            ccat_lo = sb("ccat_lo", [P, KC, T], F32R, hgrn)
            cf = sb("cf", [P, HG_HEADS, T], F32, hgrn)
            cv = sb("cv", [P, TT, D], F32, hgrn)
            cg = sb("cg", [P, KC, T], F32, hgrn)
            ca = sb("ca", [P, 4, T], F32, hgrn)
            ct1 = sb("ct1", [P, 4, T // 2], F32, hgrn)
            ct2 = sb("ct2", [P, 4, T // 4], F32, hgrn)
            cmask = sb("cmask", [P, len(LEVELS), P], F32, hgrn)
        with ExitStack() as swa:
            dq = sb("dq", [P, KC, T], F32, swa)
            dk = sb("dk", [P, 2, T], F32, swa)
            dv = sb("dv", [P, TT, P], F32, swa)
            ds_ = sb("ds", [P, TT, 2, 2 * WINDOW], F32, swa)
            dpt = sb("dpt", [P, TT, T], F32, swa)
            dcat_hi = sb("dcat_hi", [P, KC, T], F32R, swa)
            dcat_lo = sb("dcat_lo", [P, KC, T], F32R, swa)
        with ExitStack() as ffn:
            hid_hi = sb("hid_hi", [P, FC, T], F32R, ffn)
            hid_lo = sb("hid_lo", [P, FC, T], F32R, ffn)
            gate = sb("gate", [P, 2, T], F32, ffn)
            gconv = sb("gconv", [P, 2, T], F32, ffn)

        bank = [ctx.enter_context(nc.psum_tensor(f"bank{i}", [P, T], F32)) for i in range(8)]
        STAT = bank[4]

        raw_landed = [sem("raw_landed0"), sem("raw_landed1")]
        hi_ready, w_ready, slot_done = sem("hi_ready"), sem("w_ready"), sem("slot_done")
        x_landed, consts_landed, mask_landed = sem("x_landed"), sem("consts_landed"), sem("mask_landed")
        consts_made = sem("consts_made")
        sq_ready, sq_used, rs_ln, rs_ready = sem("sq_ready"), sem("sq_used"), sem("rs_ln"), sem("rs_ready")
        ut_ready, uh_ready, u_ready = sem("ut_ready"), sem("uh_ready"), sem("u_ready")
        made_ready, normed, h_ready = sem("made_ready"), sem("normed"), sem("h_ready")
        out_full = sem("out_full")
        gate_ready, ht_ready, hh_ready, hid_ready = sem("gate_ready"), sem("ht_ready"), sem("hh_ready"), sem("hid_ready")
        gconv0_ready, gconv_ready = sem("gconv0_ready"), sem("gconv_ready")
        y_ready, y_stored = sem("y_ready"), sem("y_stored")
        a_evac, f_full, f_read, f_exp, f_ln, logf, c_ready = (sem(n) for n in (
            "a_evac", "f_full", "f_read", "f_exp", "f_ln", "logf", "c_ready"))
        gc_evac, z_ready, sconv = sem("gc_evac"), sem("z_ready"), sem("sconv")
        scores_ready, max_ready, exp_ready, inv_ready, p_ready = (sem(n) for n in (
            "scores_ready", "max_ready", "exp_ready", "inv_ready", "p_ready"))
        pt_full, pt_ready, o_ready, oh_ready, ol_ready = (sem(n) for n in (
            "pt_full", "pt_ready", "o_ready", "oh_ready", "ol_ready"))
        b_a, b_sig, bz_ready, taps, mean_full, mean_ready, xc_ready, yn_ready = (sem(n) for n in (
            "b_a", "b_sig", "bz_ready", "taps", "mean_full", "mean_ready", "xc_ready", "yn_ready"))
        lb_step, c_sig, c_qkf, i_evac, g_sig, g_ready = (sem(n) for n in (
            "lb_step", "c_sig", "c_qkf", "i_evac", "g_sig", "g_ready"))
        level_full, level_kept, upd, pv_part, far_full, far_kept, co_full, co_evac, cg_mul = (sem(n) for n in (
            "level_full", "level_kept", "upd", "pv_part", "far_full", "far_kept", "co_full", "co_evac", "cg_mul"))
        d_kv_evac, d_q_evac = sem("d_kv_evac"), sem("d_q_evac")
        ds_full, ds_ready, ds_max, ds_m, ds_nm, ds_exp, ds_sink, ds_den, ds_p = (sem(n) for n in (
            "ds_full", "ds_ready", "ds_max", "ds_m", "ds_nm", "ds_exp", "ds_sink", "ds_den", "ds_p"))
        dpt_full, dpt_ready, do_ready, doh_ready, dol_ready = (sem(n) for n in (
            "dpt_full", "dpt_ready", "do_ready", "doh_ready", "dol_ready"))

        def col(name, i=0, n=1):
            return vec[:, VEC[name] + i:VEC[name] + i + n]

        def window_bank(n, e):
            return bank[4 + 2 * e + n // 2][:, 2 * WINDOW * (n % 2):2 * WINDOW * (n % 2 + 1)]

        def after(eng, s, n):
            if not (isinstance(n, int) and n <= 0):
                eng.wait_ge(s, n)

        block = ctx.enter_context(nc.Block())

        @block.sync
        def _(sp):
            sp.dma_start(h[:, :, :], x_t).then_inc(x_landed, 16)
            for j in range(2):
                sp.dma_start(raw[:, j, :], weights[j]).then_inc(raw_landed[j], 16)
            sp.dma_start(vec[:, :], vectors).then_inc(consts_landed, 16)
            sp.dma_start(consts[:, :], squares).then_inc(consts_landed, 16)
            sp.dma_start(select[:, :, :], select_d).then_inc(consts_landed, 16)
            with sp.Fori(1, N_SLOTS // 2) as i:
                for j in range(2):
                    sp.wait_ge(w_ready, 2 * i + j - 1)
                    sp.dma_start(raw[:, j, :], weights[bass.ds(2 * i + j, 1)].rearrange("o p n -> p (o n)"))\
                      .then_inc(raw_landed[j], 16)
            for c in range(KC):
                sp.wait_ge(y_ready, c + 1)
                sp.dma_start(out_t[:, c, :], m[:, c, :]).then_inc(y_stored, 16)
            sp.wait_ge(y_stored, 16 * KC)

        @block.gpsimd
        def _(pool):
            def low_part(s, j):
                pool.wait_ge(hi_ready, s + 1)
                pool.tensor_tensor(w_lo[:, j, :], raw[:, j, :], w_hi[:, j, :].bitcast(F32), ALU.subtract)\
                    .then_inc(w_ready, 1)

            with pool.Fori(0, N_SLOTS // 2) as i:
                for j in range(2):
                    low_part(2 * i + j, j)

        @block.tensor
        def _(pe):
            def product(out, wh, wl, xh, xl, start, stop):
                pe.matmul(out, wh, xh, start=start, stop=False)
                pe.matmul(out, wh, xl, start=False, stop=False)
                return pe.matmul(out, wl, xh, start=False, stop=stop)

            def weight(part, j, k, n=P):
                return part[:, j, k * n:(k + 1) * n]

            def chunk(s, j, out, xh, xl, ready=None):
                pe.wait_ge(w_ready, s + 1)
                for k in range(KC):
                    if ready:
                        ready(k)
                    last = product(out, weight(w_hi, j, k), weight(w_lo, j, k), xh[:, k, :], xl[:, k, :],
                                   k == 0, k == KC - 1)
                last.then_inc(slot_done, 1)

            def token_major(s, j, banks, first, final, free=None):
                pe.wait_ge(w_ready, s + 1)
                for t in range(TT):
                    if free:
                        free(t)
                    for k in range(2):
                        xs = slice(t * P, (t + 1) * P)
                        kk = 2 * first + k
                        last = product(banks[t][:, :], u_hi[:, kk, xs], u_lo[:, kk, xs],
                                       weight(w_hi, j, k, 512), weight(w_lo, j, k, 512),
                                       kk == 0, final and k == 1)
                last.then_inc(slot_done, 1)

            def mean_square(name, ready=None):
                for c in range(KC):
                    if c == 0 and ready:
                        ready()
                    sum_squares(name, c)

            def sum_squares(name, c):
                pe.wait_ge(sq_ready, SQ[name] + c + 1)
                pe.matmul(STAT[:, :], ones[:, :], sq[:, c % 2, :], start=(c == 0), stop=(c == KC - 1)).then_inc(sq_used, 1)

            def normed_input(name):
                return lambda k: pe.wait_ge(u_ready, SPLIT[name] + k + 1)

            def out_chunks(part, stat, xh, xl, free, ready=None):
                for n in range(KC):
                    free(n)
                    chunk(SLOT[part] + n, n % 2, bank[n % 4][:, :], xh, xl, ready if n == 0 else None)
                    if n:
                        sum_squares(stat, n - 1)
                sum_squares(stat, KC - 1)

            def consumed(made):
                def free(n):
                    if n >= 4:
                        pe.wait_ge(made_ready, MADE[made] + n - 3)
                return free

            def added(resid):
                def free(n):
                    if n >= 4:
                        pe.wait_ge(h_ready, RESID[resid] + n - 3)
                return free

            def feed_forward(l):
                s0, s1 = SLOT[f"{l}_ffn_in"], SLOT[f"{l}_ffn_out"]
                name = f"{l}_fpre"

                def pairs(i, first):
                    for b in range(2):
                        if not first:
                            pe.wait_ge(ht_ready, HID[l] + 2 * i + b - 1)
                        for e in range(2):
                            chunk(s0 + 4 * i + 2 * b + e, e, bank[2 * b + e][:, :], u_hi, u_lo,
                                  normed_input(name) if first and b == 0 and e == 0 else None)

                pairs(0, True)
                with pe.Fori(1, FC // 2) as i:
                    pairs(i, False)

                def back(k, j, first=False, final=False):
                    pe.wait_ge(w_ready, s1 + k + 1)
                    pe.wait_ge(hid_ready, HID[l] + k + 1)
                    for n in range(KC):
                        if first and n == 4:
                            pe.wait_ge(ht_ready, HID[l] + FC)
                        xh = hid_hi[:, k, :] if isinstance(k, int) else hid_hi[:, bass.ds(k, 1), :].rearrange("p o t -> p (o t)")
                        xl = hid_lo[:, k, :] if isinstance(k, int) else hid_lo[:, bass.ds(k, 1), :].rearrange("p o t -> p (o t)")
                        last = product(bank[(n + 4) % 8][:, :], weight(w_hi, j, n), weight(w_lo, j, n), xh, xl,
                                       first, final)
                        if final and n < KC - 1:
                            last.then_inc(out_full, 1)
                    last.then_inc(slot_done, 1)

                back(0, 0, first=True)
                back(1, 1)
                with pe.Fori(1, FC // 2 - 1) as i:
                    for j in range(2):
                        back(2 * i + j, j)
                back(FC - 2, 0)
                back(FC - 1, 1, final=True)

            pe.wait_ge(consts_landed, 48)
            pe.wait_ge(consts_made, 2)

            mean_square("a_pre")
            for n in range(8):
                if n >= 4:
                    pe.wait_ge(a_evac, n - 3)
                chunk(n, n % 2, bank[n % 4][:, :], u_hi, u_lo, normed_input("a_pre") if n == 0 else None)
            for k in range(KC):
                pe.wait_ge(u_ready, SPLIT["a_pre"] + KC)
                wf = vec[:, VEC["w_forget"] + k * FOX_HEADS:VEC["w_forget"] + (k + 1) * FOX_HEADS]
                pe.matmul(bank[4][0:FOX_HEADS, :], wf, u_hi[:, k, :].bitcast(F32), start=(k == 0), stop=False)
                last = pe.matmul(bank[4][0:FOX_HEADS, :], wf, u_lo[:, k, :].bitcast(F32), start=False,
                                 stop=(k == KC - 1))
            last.then_inc(f_full, 1)
            for n in range(4):
                token_major(SLOT["a_v"] + n, n % 2, bank, n, n == 3,
                            (lambda t: pe.wait_ge(a_evac, 5 + t)) if n == 0 else None)

            def scores(hd):
                r, c = slice(64 * (hd % 2), 64 * (hd % 2) + 64), hd // 2
                for qb in range(TT):
                    w = (qb + 1) * P
                    if hd > 0:
                        pe.wait_ge(pt_ready, 4 * hd)
                    s = bank[4 + qb]
                    pe.matmul(s[:, 0:w], aq[r, c, qb * P:w], ak[r, c, 0:w], start=True, stop=False)
                    pe.matmul(s[:, 0:w], select[:, hd, :], ac[:, 0:w], start=False, stop=False)
                    pe.matmul(s[:, qb * P:w], ident, causal, start=False, stop=True).then_inc(scores_ready, 1)

            def attend(hd):
                r = slice(64 * (hd % 2), 64 * (hd % 2) + 64)
                pe.wait_ge(p_ready, 4 * hd + 4)
                for kt in range(TT):
                    for qb in range(kt, TT):
                        last = pe.transpose(bank[4 + kt][:, qb * P:(qb + 1) * P], ap[:, qb, kt * P:(kt + 1) * P], ident)
                    last.then_inc(pt_full, 1)
                if hd % 2 == 0 and hd >= 2:
                    pe.wait_ge(ol_ready, hd // 2)
                for kt in range(TT):
                    pe.wait_ge(pt_ready, 4 * hd + kt + 1)
                    last = pe.matmul(bank[3][r, kt * P:T], av[:, kt, hd * FOX_DIM:(hd + 1) * FOX_DIM],
                                     apt[:, kt, kt * P:T], start=(kt == 0), stop=(kt == TT - 1))
                last.then_inc(o_ready, 1)

            def conv_slot(n):
                c, kind = n // 3, n % 3
                if n < 3:
                    pe.wait_ge(a_evac, 12)
                elif kind == 0:
                    pe.wait_ge(gc_evac, c)
                elif kind == 1:
                    pe.wait_ge(z_ready, c)
                else:
                    pe.wait_ge(ut_ready, SPLIT["a_gate"] + c)
                chunk(SLOT["a_conv"] + n, n % 2, bank[kind][:, :], u_hi, u_lo)

            pe.wait_ge(c_ready, 1)
            pe.wait_ge(a_evac, 12)
            for hd in range(FOX_HEADS):
                scores(hd)
                for n in range(hd * 12 // 8, (hd + 1) * 12 // 8):
                    conv_slot(n)
                attend(hd)

            def fox_ready(k):
                if k < 4:
                    pe.wait_ge(u_ready, SPLIT["a_gate"] + k + 1)
                else:
                    pe.wait_ge(ol_ready, k - 3)

            out_chunks("a_out", "a_post", acat_hi, acat_lo, consumed("a_mix"), fox_ready)
            mean_square("a_fpre")
            feed_forward("a")
            mean_square("a_fpost")

            mean_square("b_pre")
            for n in range(16):
                if n >= 4:
                    c = (n - 4) // 2
                    pe.wait_ge(b_a if n % 2 == 0 else b_sig, c + 1)
                chunk(SLOT["b_in"] + n, n % 2, bank[n % 4][:, :], u_hi, u_lo, normed_input("b_pre") if n == 0 else None)
            for c in range(KC):
                pe.wait_ge(taps, LONG_TAPS * (c + 1))
                last = pe.matmul(STAT[:, :], ones[:, :], by[:, c, :], start=(c == 0), stop=(c == KC - 1))
            last.then_inc(mean_full, 1)
            mean_square("b_var", lambda: pe.wait_ge(mean_ready, 1))
            out_chunks("b_out", "b_post", by_hi, by_lo, consumed("b_mix"), normed_input("b_ln"))
            mean_square("b_fpre")
            feed_forward("b")
            mean_square("b_fpost")

            mean_square("c_pre")
            for n in range(16):
                c = n // 2
                if n >= 4:
                    if n % 2 == 0:
                        pe.wait_ge(c_sig, 2 * c - 3)
                    else:
                        pe.wait_ge(c_qkf, 3 * (c - 1))
                chunk(SLOT["c_fq"] + n, n % 2, bank[n % 4][:, :], u_hi, u_lo, normed_input("c_pre") if n == 0 else None)

            def value_slot(n):
                def free(t):
                    if n == 0:
                        pe.wait_ge(c_qkf, 3 * KC)
                    elif n == 4:
                        pe.wait_ge(i_evac, t + 1)
                token_major(SLOT["c_i"] + n, n % 2, bank, n % 4, n % 4 == 3, free if n in (0, 4) else None)

            def gate_slot(n):
                if n < 4:
                    pe.wait_ge(i_evac, KC)
                    pe.wait_ge(co_evac, n + 1)
                else:
                    pe.wait_ge(g_ready, n - 3)
                chunk(SLOT["c_g"] + n, n % 2, bank[n % 4][:, :], u_hi, u_lo)

            N_LEVEL = 1 + len(LEVELS)
            PER_HEAD = 1 + 3 * 8
            for g in range(2):
                for lv in range(N_LEVEL):
                    for e in range(4):
                        hd = 4 * g + e
                        if lv == 0:
                            after(pe, c_qkf, 3 * KC)
                            if g:
                                pe.wait_ge(far_kept, 8)
                        else:
                            pe.wait_ge(upd, upd_count(g, lv, e))
                            pe.wait_ge(level_kept, 4 * (N_LEVEL * g + lv - 1) + e + 1)
                        for t in range(TT):
                            s = slice(t * P, (t + 1) * P)
                            last = pe.matmul(bank[4 + e][:, s], ck[:, hd, s], cq[:, hd, s], start=True, stop=True)
                        last.then_inc(level_full, 1)
                    (gate_slot if g else value_slot)(lv)
                for e in range(4):
                    hd = 4 * g + e
                    pe.wait_ge(level_kept, 4 * (N_LEVEL * g + N_LEVEL - 1) + e + 1)
                    if g == 0:
                        pe.wait_ge(i_evac, KC)
                    else:
                        pe.wait_ge(g_ready, KC)
                    for t in range(TT):
                        last = pe.matmul(bank[e][:, t * P:(t + 1) * P], cv[:, t, hd * P:(hd + 1) * P],
                                         ca[:, e, t * P:(t + 1) * P], start=(t == 0), stop=False, skip_group_check=True)
                    last.then_inc(pv_part, 1)
                for far in range(2):
                    for e in range(4):
                        hd = 4 * g + e
                        pe.wait_ge(upd, upd_count(g, N_LEVEL + far, e))
                        if far:
                            pe.wait_ge(far_kept, 8 * g + e + 1)
                        if far == 0:
                            for i in range(2):
                                last = pe.matmul(bank[4 + e][:, i * P:(i + 1) * P], ck[:, hd, 2 * i * P:(2 * i + 1) * P],
                                                 cq[:, hd, (2 * i + 1) * P:(2 * i + 2) * P], start=True, stop=True)
                        else:
                            for i in range(2):
                                last = pe.matmul(bank[4 + e][:, 2 * i * P:2 * (i + 1) * P], ck[:, hd, i * P:(i + 1) * P],
                                                 cq[:, hd, 2 * P:4 * P], start=True, stop=True)
                        last.then_inc(far_full, 1)
                    for e in range(4):
                        hd = 4 * g + e
                        pe.wait_ge(far_kept, 8 * g + 4 * far + e + 1)
                        for i in range(2):
                            if far == 0:
                                last = pe.matmul(bank[e][:, (2 * i + 1) * P:(2 * i + 2) * P],
                                                 cv[:, 2 * i, hd * P:(hd + 1) * P], ca[:, e, i * P:(i + 1) * P],
                                                 start=False, stop=False, skip_group_check=True)
                            else:
                                last = pe.matmul(bank[e][:, 2 * P:4 * P], cv[:, i, hd * P:(hd + 1) * P],
                                                 ca[:, e, 2 * i * P:2 * (i + 1) * P], start=False, stop=(i == 1),
                                                 skip_group_check=True)
                        last.then_inc(pv_part if far == 0 else co_full, 1)
            for hd in range(HG_HEADS):
                pe.wait_ge(sq_ready, SQ["c_head"] + hd + 1)
                if hd >= 2:
                    pe.wait_ge(rs_ready, RS["c_head"] + hd - 1)
                pe.matmul(bank[4 + hd % 2][:, :], ones[:, :], sq[:, hd % 2, :], start=True, stop=True).then_inc(sq_used, 1)
            out_chunks("c_out", "c_fpre", ccat_hi, ccat_lo, added("c_mix"), normed_input("c_out"))
            feed_forward("c")

            mean_square("d_pre", lambda: pe.wait_ge(h_ready, RESID["c_ffn"] + 1))
            chunk(SLOT["d_kv"], 0, bank[0][:, :], u_hi, u_lo, normed_input("d_kv"))
            pe.wait_ge(w_ready, SLOT["d_kv"] + 2)
            for t in range(TT):
                for k in range(KC):
                    ts = slice(t * P, (t + 1) * P)
                    last = product(bank[1][:, ts], u_hi[:, k, ts], u_lo[:, k, ts], weight(w_hi, 1, k), weight(w_lo, 1, k),
                                   k == 0, k == KC - 1)
            last.then_inc(slot_done, 1)

            def window_scores(c):
                kv = c // 4
                for n in range(TT):
                    lo = 0 if n else P
                    if c > 0:
                        pe.wait_ge(dpt_ready, 4 * c)
                    for e in range(2):
                        r = slice(64 * e, 64 * e + 64)
                        last = pe.matmul(window_bank(n, e)[:, lo:],
                                         dq[r, c, n * P:(n + 1) * P], dk[r, kv, (n - 1) * P + lo:(n + 1) * P],
                                         start=True, stop=True)
                    last.then_inc(ds_full, 1)

            def window_attend(c):
                kv = c // 4
                for n in range(TT):
                    pe.wait_ge(ds_p, 8 * c + 2 * n + 2)
                    for kt in range(0 if n else 1, 2):
                        for e in range(2):
                            last = pe.transpose(bank[4 + n][:, (2 * kt + e) * P:(2 * kt + e + 1) * P],
                                                ds_[:, n, e, kt * P:(kt + 1) * P], ident)
                    last.then_inc(dpt_full, 1)
                if c >= 2:
                    pe.wait_ge(dol_ready, c - 1)
                o = bank[2 + c % 2]
                for n in range(TT):
                    pe.wait_ge(dpt_ready, 4 * c + n + 1)
                    for e in range(2):
                        first = 0 if n else 1
                        for kt in range(first, 2):
                            last = pe.matmul(o[64 * e:64 * e + 64, n * P:(n + 1) * P],
                                             dv[:, n - 1 + kt, 64 * kv:64 * kv + 64],
                                             dpt[:, n, (2 * kt + e) * P:(2 * kt + e + 1) * P],
                                             start=(kt == first), stop=(kt == 1))
                last.then_inc(do_ready, 1)

            def query_slot(n):
                if n >= 2:
                    pe.wait_ge(d_q_evac, n - 1)
                else:
                    pe.wait_ge(d_kv_evac, 5)
                chunk(SLOT["d_q"] + n, n % 2, bank[n % 2][:, :], u_hi, u_lo, normed_input("d_q") if n == 0 else None)

            query_slot(0)
            for c in range(KC):
                pe.wait_ge(d_q_evac, c + 1)
                window_scores(c)
                if c + 1 < KC:
                    query_slot(c + 1)
                window_attend(c)
            out_chunks("d_out", "d_fpre", dcat_hi, dcat_lo, added("d_mix"), lambda k: pe.wait_ge(dol_ready, k + 1))
            feed_forward("d")
            mean_square("final", lambda: pe.wait_ge(h_ready, RESID["d_ffn"] + 1))

        @block.scalar
        def _(act):
            def high_part(s, j, done=None):
                if done is not None:
                    act.wait_ge(slot_done, done)
                act.wait_ge(raw_landed[j], 16 * ((s - j) // 2 + 1) if isinstance(s, int) else 8 * (s - j) + 16)
                act.activation(w_hi[:, j, :], raw[:, j, :], ACT.Copy).then_inc(hi_ready, 1)

            def slot_over(s, j):
                if isinstance(s, int) and s + 2 >= N_SLOTS:
                    act.wait_ge(slot_done, s + 1)
                else:
                    high_part(s + 2, j, s + 1)

            def square(name, c, src, **kw):
                n = SQ[name] + c
                after(act, sq_used, n - 1)
                act.activation(sq[:, n % 2, :], src, ACT.Square, **kw).then_inc(sq_ready, 1)

            def root(name, i=0, src=STAT, scale=1.0 / D, e=0):
                n = RS[name] + i
                act.activation(rs[:, :], src[:, :], ACT.Ln, bias=eps[:, e:e + 1], scale=scale).then_inc(rs_ln, 1)
                act.wait_ge(rs_ln, n + 1)
                act.activation(rs[:, :], rs[:, :], ACT.Exp, scale=-0.5).then_inc(rs_ready, 1)

            def stat_of_h(name, resid):
                for c in range(KC):
                    if resid is None:
                        act.wait_ge(x_landed, 16)
                    else:
                        act.wait_ge(h_ready, RESID[resid] + c + 1)
                    square(name, c, h[:, c, :])
                act.wait_ge(sq_used, SQ[name] + KC)
                root(name)

            def high_of(name, c, dst):
                act.wait_ge(ut_ready, SPLIT[name] + c + 1)
                act.activation(dst, ut[:, (SPLIT[name] + c) % 2, :], ACT.Copy).then_inc(uh_ready, 1)

            def split_input(name):
                for c in range(KC):
                    high_of(name, c, u_hi[:, c, :])

            def square_out(part, stat, made=None, resid=None):
                for n in range(KC):
                    slot_over(SLOT[part] + n, n % 2)
                    if made:
                        act.wait_ge(made_ready, MADE[made] + n + 1)
                        square(stat, n, m[:, n, :])
                    else:
                        act.wait_ge(h_ready, RESID[resid] + n + 1)
                        square(stat, n, h[:, n, :])
                act.wait_ge(sq_used, SQ[stat] + KC)
                root(stat)

            def feed_forward(l, second):
                s0, s1 = SLOT[f"{l}_ffn_in"], SLOT[f"{l}_ffn_out"]

                def pairs(i):
                    for b in range(2):
                        j = 2 * i + b
                        slot_over(s0 + 2 * j, 0)
                        if second is not None:
                            if not isinstance(j, int) or j >= 2:
                                act.wait_ge(gate_ready, HID[l] + j - 1)
                            one = lambda name, at: vec[:, bass.ds(VEC[name] + at + j, 1)] if not isinstance(j, int) else vec[:, VEC[name] + at + j:VEC[name] + at + j + 1]
                            act.activation(gconv[:, b, :], bank[2 * b][:, :], ACT.Identity,
                                           bias=one("ffn_conv_b", second * FC),
                                           scale=one("ffn_conv_w", (second * FFN_TAPS + 2) * FC)).then_inc(gconv0_ready, 1)
                        slot_over(s0 + 2 * j + 1, 1)
                        if second is not None:
                            act.wait_ge(gconv_ready, CONVG[l] + 2 * j + 2)
                        if not isinstance(j, int) or j >= 2:
                            act.wait_ge(ht_ready, HID[l] + j - 1)
                        act.activation(gate[:, b, :], bank[2 * b][:, :] if second is None else gconv[:, b, :], ACT.Silu)\
                           .then_inc(gate_ready, 1)

                pairs(0)
                with act.Fori(1, FC // 2) as i:
                    pairs(i)
                with act.Fori(0, FC // 2 - 1) as i:
                    for j in range(2):
                        slot_over(s1 + 2 * i + j, j)
                slot_over(s1 + FC - 2, 0)

            def ffn_square_out(l, stat):
                slot_over(SLOT[f"{l}_ffn_out"] + FC - 1, 1)
                for n in range(KC):
                    act.wait_ge(made_ready, MADE[f"{l}_ffn"] + n + 1)
                    square(stat, n, m[:, n, :])
                act.wait_ge(sq_used, SQ[stat] + KC)
                root(stat)

            for j in range(2):
                high_part(j, j)
            act.wait_ge(consts_landed, 48)
            act.wait_ge(consts_made, 2)

            stat_of_h("a_pre", None)
            split_input("a_pre")
            for n in range(8):
                slot_over(n, n % 2)
                act.activation((aq if n < 4 else ak)[:, n % 4, :], bank[n % 4][:, :], ACT.Copy,
                               scale=FOX_DIM ** -0.5 if n < 4 else 1.0).then_inc(a_evac, 1)
            act.wait_ge(f_read, 1)
            f8 = slice(0, FOX_HEADS)
            act.activation(ap[f8, 1, :], ap[f8, 0, :], ACT.Abs).then_inc(f_exp, 1)
            act.wait_ge(f_exp, 1)
            act.activation(ap[f8, 1, :], ap[f8, 1, :], ACT.Exp, scale=-1.0).then_inc(f_exp, 1)
            act.wait_ge(f_exp, 2)
            act.activation(ap[f8, 1, :], ap[f8, 1, :], ACT.Ln, bias=1.0).then_inc(f_ln, 1)
            for n in range(4):
                slot_over(SLOT["a_v"] + n, n % 2)
            for t in range(TT):
                act.activation(av[:, t, :], bank[t][:, :], ACT.Copy).then_inc(a_evac, 1)
            nmax, rsum = small[:, 0:8], small[:, 8:16]
            for hd in range(FOX_HEADS):
                for qb in range(TT):
                    w, i = (qb + 1) * P, 4 * (hd % 2) + qb
                    act.wait_ge(max_ready, 4 * hd + qb + 1)
                    after(act, pt_full, 4 * hd)
                    act.activation(ap[:, qb, 0:w], bank[4 + qb][:, 0:w], ACT.Exp, bias=nmax[:, i:i + 1],
                                   accum_out=rsum[:, i:i + 1]).then_inc(exp_ready, 1)
                for n in range(hd * 12 // 8, (hd + 1) * 12 // 8):
                    c, kind = n // 3, n % 3
                    slot_over(SLOT["a_conv"] + n, n % 2)
                    if kind == 0:
                        after(act, z_ready, c)
                        act.activation(agc[:, :], bank[0][:, :], ACT.Copy).then_inc(gc_evac, 1)
                    if kind == 2:
                        high_of("a_gate", c, acat_hi[:, c, :])
                for kt in range(TT):
                    act.wait_ge(pt_full, 4 * hd + kt + 1)
                    after(act, o_ready, hd)
                    act.activation(apt[:, kt, kt * P:T], bank[4 + kt][:, kt * P:T], ACT.Copy).then_inc(pt_ready, 1)
                if hd % 2:
                    act.wait_ge(o_ready, hd + 1)
                    act.activation(acat_hi[:, 4 + hd // 2, :], bank[3][:, :], ACT.Copy).then_inc(oh_ready, 1)
            square_out("a_out", "a_post", made="a_mix")
            stat_of_h("a_fpre", "a_mix")
            split_input("a_fpre")
            feed_forward("a", None)
            ffn_square_out("a", "a_fpost")

            stat_of_h("b_pre", "a_ffn")
            split_input("b_pre")
            for n in range(16):
                c = n // 2
                slot_over(SLOT["b_in"] + n, n % 2)
                after(act, bz_ready, c - 1 if n % 2 == 0 else c)
                if n % 2 == 0:
                    act.activation(ba[:, 0, :], bank[n % 4][:, :], ACT.Identity, bias=col("b_pw1", c)).then_inc(b_a, 1) \
                        if c == 0 else (act.wait_ge(bz_ready, c), act.activation(
                            ba[:, 0, :], bank[n % 4][:, :], ACT.Identity, bias=col("b_pw1", c)).then_inc(b_a, 1))
                else:
                    act.activation(ba[:, 1, :], bank[n % 4][:, :], ACT.Sigmoid, bias=col("b_pw1", KC + c)).then_inc(b_sig, 1)
            act.wait_ge(mean_full, 1)
            act.activation(bmean[:, :], STAT[:, :], ACT.Copy, scale=1.0 / D).then_inc(mean_ready, 1)
            for c in range(KC):
                act.wait_ge(xc_ready, c + 1)
                square("b_var", c, by[:, c, :])
            act.wait_ge(sq_used, SQ["b_var"] + KC)
            root("b_var", e=1)
            for c in range(KC):
                n = SPLIT["b_ln"] + c
                act.wait_ge(yn_ready, c + 1)
                act.wait_ge(u_ready, n - 1)
                act.activation(ut[:, n % 2, :], by[:, c, :], ACT.Silu, bias=col("ln_b", c), scale=col("ln_g", c))\
                   .then_inc(ut_ready, 1)
                act.wait_ge(ut_ready, n + 1)
                act.activation(by_hi[:, c, :], ut[:, n % 2, :], ACT.Copy).then_inc(uh_ready, 1)
            square_out("b_out", "b_post", made="b_mix")
            stat_of_h("b_fpre", "b_mix")
            split_input("b_fpre")
            feed_forward("b", None)
            ffn_square_out("b", "b_fpost")

            act.dma_start(cmask[:, :, :], masks_d).then_inc(mask_landed, 16)
            stat_of_h("c_pre", "b_ffn")
            split_input("c_pre")
            act.wait_ge(lb_step, 3)
            act.activation(small[:, 16:32], small[:, 16:32], ACT.Exp).then_inc(lb_step, 1)
            for n in range(16):
                slot_over(SLOT["c_fq"] + n, n % 2)
                act.activation((cq if n % 2 else cf)[:, n // 2, :], bank[n % 4][:, :], ACT.Sigmoid).then_inc(c_sig, 1)

            def value_over(n):
                slot_over(SLOT["c_i"] + n, n % 2)
                if n % 4 == 3:
                    half = slice(512 * (n // 4), 512 * (n // 4) + 512)
                    for t in range(TT):
                        act.activation(cv[:, t, half], bank[t][:, :], ACT.Copy).then_inc(i_evac, 1)

            def gate_over(n):
                slot_over(SLOT["c_g"] + n, n % 2)
                act.activation(cg[:, n, :], bank[n % 4][:, :], ACT.Sigmoid).then_inc(g_sig, 1)

            for g in range(2):
                for lv in range(8):
                    (gate_over if g else value_over)(lv)
                for far in range(2):
                    for e in range(4):
                        w = T if far else 2 * P
                        act.wait_ge(far_full, 8 * g + 4 * far + e + 1)
                        act.wait_ge(pv_part, 8 * g + 4 * far + e + 1)
                        act.activation(ca[:, e, 0:w], bank[4 + e][:, 0:w], ACT.Copy).then_inc(far_kept, 1)
                for e in range(4):
                    act.wait_ge(co_full, 4 * g + e + 1)
                    act.activation(cf[:, 4 * g + e, :], bank[e][:, :], ACT.Copy).then_inc(co_evac, 1)
            for hd in range(HG_HEADS):
                act.wait_ge(co_evac, hd + 1)
                square("c_head", hd, cf[:, hd, :])
                act.wait_ge(sq_used, SQ["c_head"] + hd + 1)
                if hd:
                    act.wait_ge(ut_ready, SPLIT["c_out"] + hd)
                root("c_head", hd, bank[4 + hd % 2], 1.0 / P)
                high_of("c_out", hd, ccat_hi[:, hd, :])
            square_out("c_out", "c_fpre", resid="c_mix")
            split_input("c_fpre")
            feed_forward("c", 0)
            slot_over(SLOT["c_ffn_out"] + FC - 1, 1)

            stat_of_h("d_pre", "c_ffn")
            split_input("d_kv")
            slot_over(SLOT["d_kv"], 0)
            for kv in range(2):
                for half in range(2):
                    act.activation(dk[64 * half:64 * half + 64, kv, :], bank[0][64 * kv:64 * kv + 64, :], ACT.Copy)\
                       .then_inc(d_kv_evac, 1)
            slot_over(SLOT["d_kv"] + 1, 1)
            act.activation(dv[:, :, :], bank[1][:, :].rearrange("p (t n) -> p t n", t=TT), ACT.Copy).then_inc(d_kv_evac, 1)
            split_input("d_q")

            def query_over(n):
                slot_over(SLOT["d_q"] + n, n % 2)
                act.activation(dq[:, n, :], bank[n % 2][:, :], ACT.Copy, scale=SWA_DIM ** -0.5).then_inc(d_q_evac, 1)

            query_over(0)
            nm, den = small[:, 32:40], small[:, 40:48]
            for c in range(KC):
                act.wait_ge(ds_nm, 2 * c + 2)
                act.activation(small[:, 56:64], small[:, 56:64], ACT.Exp).then_inc(ds_sink, 1)
                for n in range(TT):
                    lo = 0 if n else P
                    for e in range(2):
                        i = 2 * n + e
                        act.activation(ds_[:, n, e, lo:], ds_[:, n, e, lo:], ACT.Exp, bias=nm[:, i:i + 1],
                                       accum_out=den[:, i:i + 1]).then_inc(ds_exp, 1)
                if c + 1 < KC:
                    query_over(c + 1)
                for n in range(TT):
                    lo = 0 if n else 2 * P
                    act.wait_ge(dpt_full, 4 * c + n + 1)
                    after(act, do_ready, c)
                    act.activation(dpt[:, n, lo:], bank[4 + n][:, lo:], ACT.Copy).then_inc(dpt_ready, 1)
                act.wait_ge(do_ready, c + 1)
                act.activation(dcat_hi[:, c, :], bank[2 + c % 2][:, :], ACT.Copy).then_inc(doh_ready, 1)
            square_out("d_out", "d_fpre", resid="d_mix")
            split_input("d_fpre")
            feed_forward("d", 1)
            slot_over(SLOT["d_ffn_out"] + FC - 1, 1)
            stat_of_h("final", "d_ffn")

        @block.vector
        def _(dve):
            def split_value(name, c, make):
                n = SPLIT[name] + c
                after(dve, u_ready, n - 1)
                make(ut[:, n % 2, :]).then_inc(ut_ready, 1)

            def low_of(name, c, dst, hi):
                n = SPLIT[name] + c
                dve.wait_ge(uh_ready, n + 1)
                dve.tensor_tensor(dst, ut[:, n % 2, :], hi.bitcast(F32), ALU.subtract).then_inc(u_ready, 1)

            def norm_input(name, stat, gain, at):
                dve.wait_ge(rs_ready, RS[stat] + 1)
                for c in range(KC + 1):
                    if c < KC:
                        split_value(name, c, lambda dst: dve.scalar_tensor_tensor(
                            out=dst, in0=h[:, c, :], scalar=col(gain, at + c), in1=rs[:, :], op0=ALU.mult, op1=ALU.mult))
                    if c:
                        low_of(name, c - 1, u_lo[:, c - 1, :], u_hi[:, c - 1, :])

            def norm_add(made, resid, stat, gain, at):
                dve.wait_ge(rs_ready, RS[stat] + 1)
                for c in range(KC + 1):
                    if c < KC:
                        dve.wait_ge(made_ready, MADE[made] + c + 1)
                        dve.tensor_tensor(m[:, c, :], m[:, c, :], rs[:, :], ALU.mult).then_inc(normed, 1)
                    if c:
                        dve.wait_ge(normed, MADE[made] + c)
                        dve.scalar_tensor_tensor(out=h[:, c - 1, :], in0=m[:, c - 1, :], scalar=col(gain, at + c - 1),
                                                 in1=h[:, c - 1, :], op0=ALU.mult, op1=ALU.add).then_inc(h_ready, 1)

            def keep_out(part, bias=None):
                for n in range(KC):
                    dve.wait_ge(slot_done, SLOT[part] + n + 1)
                    if bias:
                        dve.tensor_scalar(m[:, n, :], bank[n % 4][:, :], bias(n), None, ALU.add).then_inc(made_ready, 1)
                    else:
                        dve.tensor_copy(m[:, n, :], bank[n % 4][:, :]).then_inc(made_ready, 1)

            def ffn_full(l, n):
                if n < KC - 1:
                    dve.wait_ge(out_full, FULL[l] + n + 1)
                else:
                    dve.wait_ge(slot_done, SLOT[f"{l}_ffn_out"] + FC)

            def add_out(part, l):
                for n in range(KC):
                    if part:
                        dve.wait_ge(slot_done, SLOT[part] + n + 1)
                    else:
                        ffn_full(l, n)
                    src = bank[n % 4] if part else bank[(n + 4) % 8]
                    dve.tensor_tensor(h[:, n, :], h[:, n, :], src[:, :], ALU.add).then_inc(h_ready, 1)

            def feed_forward(l, second):
                s0 = SLOT[f"{l}_ffn_in"]

                def at(t, j):
                    return t[:, j, :] if isinstance(j, int) else t[:, bass.ds(j, 1), :].rearrange("p o t -> p (o t)")

                def pairs(i):
                    for b in range(2):
                        j = 2 * i + b
                        if second is not None:
                            dve.wait_ge(gconv0_ready, HID[l] - HID["c"] + j + 1)
                            for tap in (1, 0):
                                back = 2 - tap
                                base = VEC["ffn_conv_w"] + (second * FFN_TAPS + tap) * FC
                                w = vec[:, bass.ds(base + j, 1)] if not isinstance(j, int) else vec[:, base + j:base + j + 1]
                                if tap == 0:
                                    dve.wait_ge(gconv_ready, CONVG[l] + 2 * j + 1)
                                dve.scalar_tensor_tensor(out=gconv[:, b, back:], in0=bank[2 * b][:, 0:T - back], scalar=w,
                                                         in1=gconv[:, b, back:], op0=ALU.mult, op1=ALU.add)\
                                   .then_inc(gconv_ready, 1)
                        dve.wait_ge(slot_done, s0 + 2 * j + 2)
                        dve.wait_ge(gate_ready, HID[l] + j + 1)
                        if not isinstance(j, int) or j >= 2:
                            dve.wait_ge(hid_ready, HID[l] + j - 1)
                        dve.tensor_tensor(gate2[:, b, :], gate[:, b, :], bank[2 * b + 1][:, :], ALU.mult).then_inc(ht_ready, 1)
                        dve.wait_ge(ht_ready, HID[l] + j + 1)
                        dve.tensor_scalar(at(hid_hi, j), gate2[:, b, :], 1.0, None, ALU.mult).then_inc(hh_ready, 1)
                        dve.wait_ge(hh_ready, HID[l] + j + 1)
                        dve.tensor_tensor(at(hid_lo, j), gate2[:, b, :], at(hid_hi, j).bitcast(F32), ALU.subtract)\
                           .then_inc(hid_ready, 1)

                gate2 = ut
                pairs(0)
                with dve.Fori(1, FC // 2) as i:
                    pairs(i)

            def keep_ffn(l):
                for n in range(KC):
                    ffn_full(l, n)
                    dve.tensor_copy(m[:, n, :], bank[(n + 4) % 8][:, :]).then_inc(made_ready, 1)

            dve.memset(ones[:, :], 1.0).then_inc(consts_made, 1)
            dve.memset(eps[:, 0:1], RMS_EPS)
            dve.memset(eps[:, 1:2], LN_EPS).then_inc(consts_made, 1)
            dve.memset(az[:, :, 0:SHORT_TAPS - 1], 0.0)
            dve.wait_ge(consts_landed, 48)
            dve.wait_ge(x_landed, 16)

            norm_input("a_pre", "a_pre", "mix_pre", 0)
            f8 = slice(0, FOX_HEADS)
            dve.wait_ge(f_full, 1)
            dve.tensor_scalar(ap[f8, 0, :], bank[4][f8, :], vec[f8, VEC["b_forget"]:VEC["b_forget"] + 1], None, ALU.add)\
               .then_inc(f_read, 1)
            dve.wait_ge(f_ln, 1)
            dve.wait_ge(f_read, 1)
            dve.scalar_tensor_tensor(out=ap[f8, 2, :], in0=ap[f8, 0, :], scalar=0.0, in1=ap[f8, 1, :],
                                     op0=ALU.min, op1=ALU.subtract).then_inc(logf, 1)
            dve.memset(ap[f8, 3, :], 1.0).then_inc(logf, 1)
            dve.wait_ge(logf, 2)
            dve.tensor_tensor_scan(ac[:, :], ap[f8, 3, :], ap[f8, 2, :], 0.0, ALU.mult, ALU.add).then_inc(c_ready, 1)
            nmax, rsum, rinv = small[:, 0:8], small[:, 8:16], small[:, 48:56]
            dve.wait_ge(c_ready, 1)
            for hd in range(FOX_HEADS):
                o4 = 4 * (hd % 2)
                for qb in range(TT):
                    dve.wait_ge(scores_ready, 4 * hd + qb + 1)
                    dve.tensor_reduce(nmax[:, o4 + qb:o4 + qb + 1], bank[4 + qb][:, 0:(qb + 1) * P], AX_X, ALU.max,
                                      negate=True).then_inc(max_ready, 1)
                dve.wait_ge(exp_ready, 4 * hd + 4)
                dve.reciprocal(rinv[:, o4:o4 + 4], rsum[:, o4:o4 + 4]).then_inc(inv_ready, 1)
                dve.wait_ge(inv_ready, hd + 1)
                for qb in range(TT):
                    w = (qb + 1) * P
                    dve.tensor_scalar(ap[:, qb, 0:w], ap[:, qb, 0:w], rinv[:, o4 + qb:o4 + qb + 1], None, ALU.mult)\
                       .then_inc(p_ready, 1)
                for n in range(hd * 12 // 8, (hd + 1) * 12 // 8):
                    c, kind = n // 3, n % 3
                    dve.wait_ge(slot_done, SLOT["a_conv"] + n + 1)
                    if kind == 1:
                        dve.wait_ge(gc_evac, c + 1)
                        dve.tensor_tensor(az[:, c, SHORT_TAPS - 1:], agc[:, :], bank[1][:, :], ALU.mult).then_inc(z_ready, 1)
                        dve.wait_ge(z_ready, c + 1)
                        after(dve, ut_ready, SPLIT["a_gate"] + c if c else 0)
                        for i, tap in enumerate((2, 1, 0)):
                            w = col("short_conv", tap * 4 + c)
                            if i == 0:
                                ins = dve.tensor_scalar(ay[:, :], az[:, c, tap:tap + T], w, None, ALU.mult)
                            else:
                                dve.wait_ge(sconv, 3 * c + i)
                                ins = dve.scalar_tensor_tensor(out=ay[:, :], in0=az[:, c, tap:tap + T], scalar=w,
                                                               in1=ay[:, :], op0=ALU.mult, op1=ALU.add)
                            ins.then_inc(sconv, 1)
                    if kind == 2:
                        dve.wait_ge(sconv, 3 * c + 3)
                        split_value("a_gate", c, lambda dst: dve.tensor_tensor(dst, ay[:, :], bank[2][:, :], ALU.mult))
                        low_of("a_gate", c, acat_lo[:, c, :], acat_hi[:, c, :])
                if hd % 2:
                    c = 4 + hd // 2
                    dve.wait_ge(oh_ready, hd // 2 + 1)
                    dve.tensor_tensor(acat_lo[:, c, :], bank[3][:, :], acat_hi[:, c, :].bitcast(F32), ALU.subtract)\
                       .then_inc(ol_ready, 1)
            keep_out("a_out")
            norm_add("a_mix", "a_mix", "a_post", "mix_post", 0)
            norm_input("a_fpre", "a_fpre", "ffn_pre", 0)
            feed_forward("a", None)
            keep_ffn("a")
            norm_add("a_ffn", "a_ffn", "a_fpost", "ffn_post", 0)

            norm_input("b_pre", "b_pre", "mix_pre", KC)
            dve.memset(bz[:, :, 0:LONG_TAPS - 1], 0.0)
            for c in range(KC):
                dve.wait_ge(b_a, c + 1)
                dve.wait_ge(b_sig, c + 1)
                dve.tensor_tensor(bz[:, c, LONG_TAPS - 1:], ba[:, 0, :], ba[:, 1, :], ALU.mult).then_inc(bz_ready, 1)
                dve.wait_ge(bz_ready, c + 1)
                for tap in range(LONG_TAPS):
                    w = col("w_dw", tap * KC + c)
                    if tap == 0:
                        ins = dve.tensor_scalar(by[:, c, :], bz[:, c, 0:T], w, col("b_dw", c), ALU.mult, ALU.add)
                    else:
                        dve.wait_ge(taps, LONG_TAPS * c + tap)
                        ins = dve.scalar_tensor_tensor(out=by[:, c, :], in0=bz[:, c, tap:tap + T], scalar=w, in1=by[:, c, :],
                                                       op0=ALU.mult, op1=ALU.add)
                    ins.then_inc(taps, 1)
            dve.wait_ge(mean_ready, 1)
            for c in range(KC):
                dve.tensor_tensor(by[:, c, :], by[:, c, :], bmean[:, :], ALU.subtract).then_inc(xc_ready, 1)
            dve.wait_ge(rs_ready, RS["b_var"] + 1)
            for c in range(KC):
                dve.tensor_tensor(by[:, c, :], by[:, c, :], rs[:, :], ALU.mult).then_inc(yn_ready, 1)
            for c in range(KC):
                low_of("b_ln", c, by_lo[:, c, :], by_hi[:, c, :])
            keep_out("b_out", lambda n: col("b_pw2", n))
            norm_add("b_mix", "b_mix", "b_post", "mix_post", KC)
            norm_input("b_fpre", "b_fpre", "ffn_pre", KC)
            feed_forward("b", None)
            keep_ffn("b")
            norm_add("b_ffn", "b_ffn", "b_fpost", "ffn_post", KC)

            l0, l1, e0, e1 = col("lb_logits", 0, KC), col("lb_logits", KC, KC), small[:, 16:24], small[:, 24:32]
            lb, rest, top = small[:, 0:8], small[:, 8:16], small[:, 32:40]
            dve.tensor_tensor(top, l0, l1, ALU.max).then_inc(lb_step, 1)
            dve.wait_ge(lb_step, 1)
            dve.tensor_tensor(e0, l0, top, ALU.subtract).then_inc(lb_step, 1)
            dve.tensor_tensor(e1, l1, top, ALU.subtract).then_inc(lb_step, 1)
            norm_input("c_pre", "c_pre", "hg_norm", 0)
            dve.wait_ge(lb_step, 4)
            dve.tensor_tensor(top, e0, e1, ALU.add).then_inc(lb_step, 1)
            dve.wait_ge(lb_step, 5)
            dve.reciprocal(top, top).then_inc(lb_step, 1)
            dve.wait_ge(lb_step, 6)
            dve.tensor_tensor(lb, e0, top, ALU.mult).then_inc(lb_step, 1)
            dve.wait_ge(lb_step, 7)
            dve.tensor_scalar(rest, lb, -1.0, 1.0, ALU.mult, ALU.add).then_inc(lb_step, 1)
            dve.wait_ge(lb_step, 8)
            for c in range(KC):
                dve.wait_ge(c_sig, 2 * c + 1)
                dve.tensor_scalar(cf[:, c, :], cf[:, c, :], rest[:, c:c + 1], lb[:, c:c + 1], ALU.mult, ALU.add)\
                   .then_inc(c_qkf, 1)
                dve.wait_ge(c_qkf, 3 * c + 1)
                dve.tensor_scalar(ck[:, c, :], cf[:, c, :], -1.0, 1.0, ALU.mult, ALU.add).then_inc(c_qkf, 1)
                dve.wait_ge(c_sig, 2 * c + 2)
                dve.scalar_tensor_tensor(out=cq[:, c, :], in0=cq[:, c, :], scalar=P ** -0.5, in1=bank[(2 * c + 1) % 4][:, :],
                                         op0=ALU.mult, op1=ALU.mult).then_inc(c_qkf, 1)
            dve.wait_ge(c_qkf, 3 * KC)
            dve.wait_ge(mask_landed, 16)

            def keep_level(g, lv, e):
                dve.wait_ge(level_full, 4 * (8 * g + lv) + e + 1)
                if g and lv == 0:
                    dve.wait_ge(co_full, e + 1)
                kept = ca[:, e, :].rearrange("p (t s) -> p t s", t=TT)
                found = bank[4 + e][:, :].rearrange("p (t s) -> p t s", t=TT)
                if lv == 0:
                    mask = ident.unsqueeze(1).to_broadcast([P, TT, P])
                    dve.tensor_tensor(kept, found, mask, ALU.mult).then_inc(level_kept, 1)
                else:
                    dve.wait_ge(level_kept, 4 * (8 * g + lv - 1) + e + 1)
                    mask = cmask[:, lv - 1, :].bitcast(U32).unsqueeze(1).to_broadcast([P, TT, P])
                    dve.copy_predicated(kept, mask, found).then_inc(level_kept, 1)

            def products(level, hd, e):
                if level == 0:
                    return cf[:, hd, :]
                return (ct1 if level % 2 else ct2)[:, e, 0:T >> level]

            def decay(g, lv, e):
                hd = 4 * g + e
                if lv == 1:
                    dve.tensor_tensor(cq[:, hd, :], cq[:, hd, :], cf[:, hd, :], ALU.mult).then_inc(upd, 1)
                    return
                mm = 1 << (lv - 2)
                nb = T // (2 * mm)
                dve.wait_ge(upd, upd_count(g, lv - 1, e) + (0 if lv == 2 else 1))
                prod = products(lv - 2, hd, e).rearrange("p (b two) -> p b two", two=2)
                q = cq[:, hd, :].rearrange("p (b two s) -> p b two s", two=2, s=mm)[:, :, 1, :]
                k = ck[:, hd, :].rearrange("p (b two s) -> p b two s", two=2, s=mm)[:, :, 0, :]
                even = prod[:, :, 0].unsqueeze(2).to_broadcast([P, nb, mm])
                odd = prod[:, :, 1].unsqueeze(2).to_broadcast([P, nb, mm])
                dve.tensor_tensor(q, q, even, ALU.mult).then_inc(upd, 1)
                dve.tensor_tensor(k, k, odd, ALU.mult).then_inc(upd, 1)
                dve.tensor_tensor(products(lv - 1, hd, e), prod[:, :, 0], prod[:, :, 1], ALU.mult).then_inc(upd, 1)

            def gate_product(n):
                dve.wait_ge(g_sig, n + 1)
                dve.tensor_tensor(cg[:, n, :], cg[:, n, :], bank[n % 4][:, :], ALU.mult).then_inc(g_ready, 1)

            for g in range(2):
                for lv in range(1, 9):
                    for e in range(4):
                        keep_level(g, lv - 1, e)
                        decay(g, lv, e)
                    if g:
                        gate_product(lv - 1)
                for e in range(4):
                    dve.wait_ge(far_full, 8 * g + e + 1)
                    decay(g, 9, e)
            for hd in range(HG_HEADS):
                n = SPLIT["c_out"] + hd
                dve.wait_ge(sq_ready, SQ["c_head"] + hd + 1)
                dve.wait_ge(g_ready, KC)
                dve.scalar_tensor_tensor(out=cg[:, hd, :], in0=cf[:, hd, :], scalar=col("hg_out_norm"), in1=cg[:, hd, :],
                                         op0=ALU.mult, op1=ALU.mult).then_inc(cg_mul, 1)
                dve.wait_ge(cg_mul, hd + 1)
                dve.wait_ge(rs_ready, RS["c_head"] + hd + 1)
                split_value("c_out", hd, lambda dst: dve.tensor_tensor(dst, cg[:, hd, :], rs[:, :], ALU.mult))
                low_of("c_out", hd, ccat_lo[:, hd, :], ccat_hi[:, hd, :])
            add_out("c_out", None)
            norm_input("c_fpre", "c_fpre", "ffn_norm_2", 0)
            feed_forward("c", 0)
            add_out(None, "c")

            norm_input("d_kv", "d_pre", "kv_norm", 0)
            dve.wait_ge(slot_done, SLOT["d_q"])
            norm_input("d_q", "d_pre", "attn_norm", 0)
            top, nm, den, es = small[:, 0:8], small[:, 32:40], small[:, 40:48], small[:, 56:64]
            for c in range(KC):
                sink2 = col("sinks", 2 * c, 2).unsqueeze(1).to_broadcast([P, TT, 2])
                per = lambda s: s.rearrange("p (n e) -> p n e", e=2)
                for n in range(TT):
                    lo = 0 if n else P
                    dve.wait_ge(ds_full, 4 * c + 2 * (n // 2) + 2)
                    if c:
                        dve.wait_ge(dpt_full, 4 * c)
                    for e in range(2):
                        slope = 2.0 ** (-8.0 * (2 * c + e + 1) / SWA_HEADS)
                        dve.scalar_tensor_tensor(out=ds_[:, n, e, lo:], in0=dist[:, lo:], scalar=-slope,
                                                 in1=window_bank(n, e)[:, lo:],
                                                 op0=ALU.mult, op1=ALU.add).then_inc(ds_ready, 1)
                    dve.wait_ge(ds_ready, 8 * c + 2 * n + 2)
                    dve.tensor_reduce(top[:, 2 * n:2 * n + 2], ds_[:, n, :, lo:], AX_X, ALU.max).then_inc(ds_max, 1)
                dve.wait_ge(ds_max, 4 * c + 4)
                dve.tensor_tensor(per(top), per(top), sink2, ALU.max).then_inc(ds_m, 1)
                dve.wait_ge(ds_m, c + 1)
                dve.tensor_scalar(nm, top, -1.0, None, ALU.mult).then_inc(ds_nm, 1)
                dve.tensor_tensor(per(es), sink2, per(top), ALU.subtract).then_inc(ds_nm, 1)
                dve.wait_ge(ds_sink, c + 1)
                dve.wait_ge(ds_exp, 8 * c + 8)
                dve.tensor_tensor(den, den, es, ALU.add).then_inc(ds_den, 1)
                dve.wait_ge(ds_den, 2 * c + 1)
                dve.reciprocal(den, den).then_inc(ds_den, 1)
                dve.wait_ge(ds_den, 2 * c + 2)
                for n in range(TT):
                    lo = 0 if n else P
                    for e in range(2):
                        i = 2 * n + e
                        dve.tensor_scalar(ds_[:, n, e, lo:], ds_[:, n, e, lo:], den[:, i:i + 1], None, ALU.mult)\
                           .then_inc(ds_p, 1)
                dve.wait_ge(doh_ready, c + 1)
                dve.tensor_tensor(dcat_lo[:, c, :], bank[2 + c % 2][:, :], dcat_hi[:, c, :].bitcast(F32), ALU.subtract)\
                   .then_inc(dol_ready, 1)
            add_out("d_out", None)
            norm_input("d_fpre", "d_fpre", "ffn_norm_2", KC)
            feed_forward("d", 1)
            add_out(None, "d")
            dve.wait_ge(rs_ready, RS["final"] + 1)
            for c in range(KC):
                dve.scalar_tensor_tensor(out=m[:, c, :], in0=h[:, c, :], scalar=col("final_norm", c), in1=rs[:, :],
                                         op0=ALU.mult, op1=ALU.mult).then_inc(y_ready, 1)


def upd_count(g, lv, e):
    per_group = 4 + 8 * 12
    before = 0 if lv <= 1 else 4 + 12 * (lv - 2)
    return per_group * g + before + (e + 1 if lv == 1 else 3 * e + 2)


def kernel(**inputs):
    import numpy as np
    import concourse.bacc as bacc
    from concourse.bass_utils import run_bass_kernel_spmd

    a = {k: np.ascontiguousarray(v) for k, v in inputs.items()}

    def feature_slots(w):
        return w.reshape(KC, P, -1, P).transpose(2, 1, 0, 3).reshape(-1, P, D)

    def token_slots(w):
        return w.reshape(4, 2, P, -1, 512).transpose(3, 0, 2, 1, 4).reshape(-1, P, D)

    def woven(*parts):
        return np.stack(parts, 1).reshape(-1, P, D)

    def ffn(w_in, w_out):
        return [woven(feature_slots(w_in[:, :FF]), feature_slots(w_in[:, FF:])), w_out.reshape(FC, P, D)]

    w_in, w_hg, w_kv = a["w_in"][0], a["hg_w_in_2"][0], a["w_kv_2"]
    w_pw1 = a["w_pw1"][0]
    part = [w_in[:, 512 * i:512 * (i + 1)] for i in range(6)]
    hg = [w_hg[:, D * i:D * (i + 1)] for i in range(4)]
    slots = [feature_slots(part[3]), feature_slots(part[4]), token_slots(part[5]),
             woven(feature_slots(part[1]), feature_slots(part[2]), feature_slots(part[0])),
             feature_slots(a["w_out"][0]), *ffn(a["w_ffn_in"][0], a["w_ffn_out"][0]),
             woven(feature_slots(w_pw1[:, :D]), feature_slots(w_pw1[:, D:])), feature_slots(a["w_pw2"][0]),
             *ffn(a["w_ffn_in"][1], a["w_ffn_out"][1]),
             woven(feature_slots(hg[1]), feature_slots(hg[0])), token_slots(hg[2]), feature_slots(hg[3]),
             feature_slots(a["hg_w_out_2"][0]), *ffn(a["ffn_w_up_2"][0], a["ffn_w_down_2"][0]),
             feature_slots(w_kv), feature_slots(a["attn_w_q_2"][0]), feature_slots(a["attn_w_o_2"][0]),
             *ffn(a["ffn_w_up_2"][1], a["ffn_w_down_2"][1])]
    weights = np.concatenate(slots)
    assert weights.shape == (N_SLOTS, P, D)

    def columns(v):
        return v.reshape(-1, P).T

    forget = w_in[:, 3072:].reshape(KC, P, FOX_HEADS).transpose(1, 0, 2).reshape(P, -1)
    b_forget = np.zeros((P, 1), np.float32)
    b_forget[:FOX_HEADS, 0] = a["b_forget"][0]
    vectors = np.concatenate([
        columns(a["norm_mix_pre"]), columns(a["norm_mix_post"]), columns(a["norm_ffn_pre"]), columns(a["norm_ffn_post"]),
        forget, b_forget, columns(a["w_short_conv"][0]), columns(a["b_pw1"]), columns(a["w_dw"][0]), columns(a["b_dw"]),
        columns(a["ln_g"]), columns(a["ln_b"]), columns(a["b_pw2"]), columns(a["hg_norm_2"]), columns(a["hg_lb_logits_2"]),
        columns(a["hg_out_norm_2"]), columns(a["kv_norm_2"]), columns(a["attn_norm_2"]),
        np.broadcast_to(a["attn_sinks_2"], (P, SWA_HEADS)), columns(a["ffn_norm_2"]), columns(a["ffn_conv_w_2"]),
        columns(a["ffn_conv_b_2"]), columns(a["final_norm_2"])], 1)
    assert vectors.shape == (P, N_VEC)

    row, colm = np.arange(P)[:, None], np.arange(P)[None, :]
    far = row + WINDOW - np.arange(2 * WINDOW)[None, :]
    squares = np.concatenate([np.eye(P), np.where(colm <= row, 0.0, NEVER),
                              np.where((far >= 0) & (far < WINDOW), far, -NEVER)], 1).astype(np.float32)
    select = np.zeros((FOX_HEADS, FOX_HEADS, P), np.float32)
    for hd in range(FOX_HEADS):
        select[hd, hd] = -1.0
    masks = np.stack([(row // (2 * n) == colm // (2 * n)) & (row // n % 2 == 0) & (colm // n % 2 == 1) for n in LEVELS], 1)
    arrays = {
        "weights": weights, "vectors": vectors, "squares": squares, "select": select, "masks": masks.astype(np.float32),
        "x_t": a["x"][0].T.reshape(KC, P, T).transpose(1, 0, 2),
    }
    nc = bacc.Bacc("TRN2", target_bir_lowering=False, num_devices=1)
    args = []
    for name, v in arrays.items():
        arrays[name] = v = np.ascontiguousarray(v)
        args.append(nc.dram_tensor(f"{name}_dram", v.shape, mybir.dt.from_np(v.dtype), kind="ExternalInput").ap())
    args.append(nc.dram_tensor("out_dram", (P, KC, T), F32, kind="ExternalOutput").ap())
    build(nc, *args)
    r = run_bass_kernel_spmd(nc, [{f"{k}_dram": v for k, v in arrays.items()}], core_ids=[0])
    out = r.results[0]["out_dram"]
    return np.ascontiguousarray(out.transpose(1, 0, 2).reshape(D, T).T)[None]
```

```python
from contextlib import ExitStack

import concourse.bass as bass
from concourse import mybir

F32 = mybir.dt.float32
F32R = mybir.dt.float32r
U32 = mybir.dt.uint32
ALU = mybir.AluOpType
ACT = mybir.ActivationFunctionType
AX_X = mybir.AxisListType.X

P = 128
T = 512
D = 1024
KC = D // P
TT = T // P
FF = 2816
FC = FF // P
FOX_HEADS, FOX_DIM = 8, 64
HG_HEADS = 8
SWA_HEADS, SWA_DIM, WINDOW = 16, 64, 128
SHORT_TAPS, LONG_TAPS, FFN_TAPS = 3, 31, 3
RMS_EPS, LN_EPS = 1e-6, 1e-5
NEVER = -1e30
LEVELS = (1, 2, 4, 8, 16, 32, 64)
RING = 4
AHEAD = 3
HALF = FC // 2
PE_CHUNKS = (6, 7)

SLOT_PARTS = (
    ("a_q", 4), ("a_k", 4), ("a_v", 4), ("a_conv", 12), ("a_out", 8), ("a_ffn_in", 2 * FC), ("a_ffn_out", FC),
    ("b_in", 16), ("b_out", 8), ("b_ffn_in", 2 * FC), ("b_ffn_out", FC),
    ("c_fq", 16), ("c_i", 8), ("c_g", 8), ("c_out", 8), ("c_ffn_in", 2 * FC), ("c_ffn_out", FC),
    ("d_kv", 2), ("d_q", 8), ("d_out", 8), ("d_ffn_in", 2 * FC), ("d_ffn_out", FC),
)


def starts(parts):
    at, out = 0, {}
    for name, n in parts:
        out[name] = at
        at += n
    return out, at


SLOT, N_SLOTS = starts(SLOT_PARTS)

VEC_PARTS = (
    ("mix_pre", 16), ("mix_post", 16), ("ffn_pre", 16), ("ffn_post", 16),
    ("w_forget", KC * FOX_HEADS), ("b_forget", 1), ("short_conv", SHORT_TAPS * 4),
    ("b_pw1", 16), ("w_dw", LONG_TAPS * KC), ("b_dw", KC), ("ln_g", KC), ("ln_b", KC), ("b_pw2", KC),
    ("hg_norm", KC), ("lb_logits", 2 * KC), ("hg_out_norm", 1), ("kv_norm", KC), ("attn_norm", KC),
    ("sinks", SWA_HEADS), ("ffn_norm_2", 2 * KC), ("ffn_conv_w", 2 * FFN_TAPS * FC), ("ffn_conv_b", 2 * FC),
    ("final_norm", KC),
)
VEC, N_VEC = starts(VEC_PARTS)

STATS = ("a_pre", "a_post", "a_fpre", "a_fpost", "b_pre", "b_post", "b_fpre", "b_fpost",
         "c_pre", "c_fpre", "d_pre", "d_fpre", "final")
DIRECT = ("b_var", "c_head")
ORDER = STATS[:5] + ("b_var",) + STATS[5:9] + ("c_head",) + STATS[9:]
SQ, _ = starts([(s, KC) for s in ORDER])
ACC, _ = starts([(s, KC - 1) for s in STATS])
SUM, _ = starts([(s, 1) for s in STATS])
USED, _ = starts([(s, KC) for s in DIRECT])
RS, _ = starts([(s, HG_HEADS if s == "c_head" else 1) for s in ORDER])
SPLITS = ("a_pre", "a_gate", "a_fpre", "b_pre", "b_ln", "b_fpre", "c_pre", "c_out", "c_fpre", "d_kv", "d_q", "d_fpre")
SPLIT, _ = starts([(s, 4 if s == "a_gate" else KC) for s in SPLITS])
VALUE, _ = starts([(s, 4 if s == "a_gate" else KC) for s in SPLITS if not s.endswith("fpre")])
RESID, _ = starts([(s, KC) for s in ("a_mix", "a_ffn", "b_mix", "b_ffn", "c_mix", "c_ffn", "d_mix", "d_ffn")])
MADE, _ = starts([(s, KC) for s in ("a_mix", "a_ffn", "b_mix", "b_ffn")])
FULL, _ = starts([(s, 6) for s in "abcd"])
HID, _ = starts([(s, FC) for s in "abcd"])
CONVG, _ = starts([(s, 2 * FC) for s in "cd"])


def tap_order():
    todo = [c for c in range(KC) if c not in PE_CHUNKS]
    items, done, nxt, at = [], {}, 0, 0
    left = {c: 0 for c in todo}
    per_chunk = 15
    while nxt < KC or any(left[c] < LONG_TAPS for c in todo):
        if nxt < KC:
            items.append(("gated", nxt))
            nxt += 1
        for n in range(per_chunk if nxt < KC else 10 ** 6):
            live = [c for c in todo if c < nxt and left[c] < LONG_TAPS][:2]
            if not live:
                break
            c = min(live, key=lambda c: done.get((c, left[c] - 1), 0))
            items.append(("tap", c, left[c]))
            at += 1
            done[c, left[c]] = at
            left[c] += 1
    for c in PE_CHUNKS:
        items.insert(items.index(("gated", c)) + 6 + 4 * PE_CHUNKS.index(c), ("low", c))
    return items, done


def build(nc, weights, vectors, squares, select_d, masks_d, x_t, out_t):
    with ExitStack() as ctx:
        def sb(name, shape, dt, where=ctx):
            return where.enter_context(nc.sbuf_tensor(name, shape, dt))

        def sem(name):
            return ctx.enter_context(nc.semaphore(name))

        h = sb("h", [P, KC, T], F32)
        with ExitStack() as one:
            m = sb("m", [P, KC, T], F32, one)
        u_hi = sb("u_hi", [P, KC, T], F32R)
        u_lo = sb("u_lo", [P, KC, T], F32R)
        with ExitStack() as landing:
            raw = sb("raw", [P, RING, D], F32, landing)
        w_lo = sb("w_lo", [P, RING, D], F32R)
        w_hi = sb("w_hi", [P, RING, D], F32R)
        sq = sb("sq", [P, 2, T], F32)
        ut = sb("ut", [P, 2, T], F32)
        acc = sb("acc", [P, T], F32)
        rs = sb("rs", [P, T], F32)
        vec = sb("vec", [P, N_VEC], F32)
        identity = sb("identity", [P, P], F32)
        ident = identity[:, :]
        ones = sb("ones", [P, P], F32)
        small = sb("small", [P, 64], F32)
        eps = sb("eps", [P, 2], F32)

        with ExitStack() as fox:
            aq = sb("aq", [P, 4, T], F32, fox)
            ak = sb("ak", [P, 4, T], F32, fox)
            av = sb("av", [P, TT, 512], F32, fox)
            az = sb("az", [P, 4, T + SHORT_TAPS - 1], F32, fox)
            agc = sb("agc", [P, T], F32, fox)
            ay = sb("ay", [P, T], F32, fox)
            ap = sb("ap", [P, TT, T], F32, fox)
            apt = sb("apt", [P, TT, T], F32, fox)
            ac = sb("ac", [FOX_HEADS, T], F32, fox)
            causal = sb("causal", [P, P], F32, fox)
            wf_hi = sb("wf_hi", [P, KC, P // FOX_HEADS, FOX_HEADS], F32R, fox)
            wf_lo = sb("wf_lo", [P, KC, P // FOX_HEADS, FOX_HEADS], F32R, fox)
            select = sb("select", [FOX_HEADS, FOX_HEADS, P], F32, fox)
            acat_hi = sb("acat_hi", [P, KC, T], F32R, fox)
            acat_lo = sb("acat_lo", [P, KC, T], F32R, fox)
        with ExitStack() as conf:
            bz = sb("bz", [P, KC, T + LONG_TAPS - 1], F32, conf)
            ba = sb("ba", [P, 2, 2, T], F32, conf)
            bz_hi = sb("bz_hi", [P, len(PE_CHUNKS), T + LONG_TAPS - 1], F32R, conf)
            bz_lo = sb("bz_lo", [P, len(PE_CHUNKS), T + LONG_TAPS - 1], F32R, conf)
            dg_hi = sb("dg_hi", [P, 4, P], F32R, conf)
            dg_lo = sb("dg_lo", [P, 4, P], F32R, conf)
            wt_hi = sb("wt_hi", [P, LONG_TAPS * KC], F32R, conf)
            wt_lo = sb("wt_lo", [P, LONG_TAPS * KC], F32, conf)
            by = sb("by", [P, KC, T], F32, conf)
            bmean = sb("bmean", [P, T], F32, conf)
            by_hi = sb("by_hi", [P, KC, T], F32R, conf)
            by_lo = sb("by_lo", [P, KC, T], F32R, conf)
        with ExitStack() as hgrn:
            with ExitStack() as qk:
                cq = sb("cq", [P, HG_HEADS, T], F32, qk)
                ck = sb("ck", [P, HG_HEADS, T], F32, qk)
            ccat_hi = sb("ccat_hi", [P, KC, T], F32R, hgrn)
            ccat_lo = sb("ccat_lo", [P, KC, T], F32R, hgrn)
            cf = sb("cf", [P, HG_HEADS, T], F32, hgrn)
            cv = sb("cv", [P, TT, D], F32, hgrn)
            cg = sb("cg", [P, KC, T], F32, hgrn)
            ca = sb("ca", [P, 4, T], F32, hgrn)
            ct1 = sb("ct1", [P, 4, T // 2], F32, hgrn)
            ct2 = sb("ct2", [P, 4, T // 4], F32, hgrn)
            cmask = sb("cmask", [P, len(LEVELS), P // 2], F32, hgrn)
        with ExitStack() as swa:
            dq = sb("dq", [P, KC, T], F32, swa)
            dk = sb("dk", [P, 2, T], F32, swa)
            dv = sb("dv", [P, TT, P], F32, swa)
            ds_ = sb("ds", [P, 2, TT, 2, 2 * WINDOW], F32, swa)
            dist = sb("dist", [P, 2 * WINDOW], F32, swa)
            dpt = sb("dpt", [P, TT, T], F32, swa)
            dcat_hi = sb("dcat_hi", [P, KC, T], F32R, swa)
            dcat_lo = sb("dcat_lo", [P, KC, T], F32R, swa)
        with ExitStack() as ffn:
            hid_hi = sb("hid_hi", [P, FC, T], F32R, ffn)
            hid_lo = sb("hid_lo", [P, FC, T], F32R, ffn)
            gconv = sb("gconv", [P, 2, T], F32, ffn)

        bank = [ctx.enter_context(nc.psum_tensor(f"bank{i}", [P, T], F32)) for i in range(8)]
        STAT = bank[4]

        raw_landed = [sem(f"raw_landed{j}") for j in range(RING)]
        hi_ready, w_ready, slot_done = sem("hi_ready"), sem("w_ready"), sem("slot_done")
        x_landed = [sem(f"x_landed{c}") for c in range(KC)]
        vec_landed, consts_landed, mask_landed, dist_landed = (sem(n) for n in (
            "vec_landed", "consts_landed", "mask_landed", "dist_landed"))
        acc_ready, sum_full, scaled_ready, t2_ready = sem("acc_ready"), sem("sum_full"), sem("scaled_ready"), sem("t2_ready")
        wf_ready, wt_ready, zh_ready, zl_ready, dg_ready, dg_used, tap_full, tap_evac = (sem(n) for n in (
            "wf_ready", "wt_ready", "zh_ready", "zl_ready", "dg_ready", "dg_used", "tap_full", "tap_evac"))
        consts_made = sem("consts_made")
        sq_ready, sq_used, rs_ln, rs_ready = sem("sq_ready"), sem("sq_used"), sem("rs_ln"), sem("rs_ready")
        ut_ready, uh_ready, u_ready = sem("ut_ready"), sem("uh_ready"), sem("u_ready")
        made_ready, normed, h_ready = sem("made_ready"), sem("normed"), sem("h_ready")
        out_full = sem("out_full")
        gate_ready, ht_ready, hh_ready, hid_ready = sem("gate_ready"), sem("ht_ready"), sem("hh_ready"), sem("hid_ready")
        gconv0_ready, gconv_ready = sem("gconv0_ready"), sem("gconv_ready")
        y_ready, y_stored = sem("y_ready"), sem("y_stored")
        a_evac, f_full, f_read, f_exp, f_ln, logf, c_ready = (sem(n) for n in (
            "a_evac", "f_full", "f_read", "f_exp", "f_ln", "logf", "c_ready"))
        gc_evac, z_ready, sconv = sem("gc_evac"), sem("z_ready"), sem("sconv")
        scores_ready, max_ready, exp_ready, inv_ready, p_ready = (sem(n) for n in (
            "scores_ready", "max_ready", "exp_ready", "inv_ready", "p_ready"))
        pt_full, pt_ready, o_ready, oh_ready, ol_ready = (sem(n) for n in (
            "pt_full", "pt_ready", "o_ready", "oh_ready", "ol_ready"))
        b_a, b_sig, bz_ready, taps, mean_full, mean_ready, xc_ready, yn_ready = (sem(n) for n in (
            "b_a", "b_sig", "bz_ready", "taps", "mean_full", "mean_ready", "xc_ready", "yn_ready"))
        lb_step, c_sig, c_qkf, i_evac, g_sig, g_ready = (sem(n) for n in (
            "lb_step", "c_sig", "c_qkf", "i_evac", "g_sig", "g_ready"))
        level_full, level_kept, upd, pv_part, far_full, far_kept, co_full, co_evac, cg_mul = (sem(n) for n in (
            "level_full", "level_kept", "upd", "pv_part", "far_full", "far_kept", "co_full", "co_evac", "cg_mul"))
        d_kv_evac, d_q_evac = sem("d_kv_evac"), sem("d_q_evac")
        ds_full, ds_ready, ds_max, ds_m, ds_nm, ds_exp, ds_sink, ds_den, ds_p = (sem(n) for n in (
            "ds_full", "ds_ready", "ds_max", "ds_m", "ds_nm", "ds_exp", "ds_sink", "ds_den", "ds_p"))
        dpt_full, dpt_ready, do_ready, doh_ready, dol_ready = (sem(n) for n in (
            "dpt_full", "dpt_ready", "do_ready", "doh_ready", "dol_ready"))

        def col(name, i=0, n=1):
            return vec[:, VEC[name] + i:VEC[name] + i + n]

        def window_bank(n, e):
            return bank[4 + 2 * e + n // 2][:, 2 * WINDOW * (n % 2):2 * WINDOW * (n % 2 + 1)]

        def window_small(c):
            at = 32 * (c % 2)
            return tuple(small[:, at + 8 * i:at + 8 * i + 8] for i in range(4))

        def ffn_gain(l, c):
            return col("ffn_pre" if l in "ab" else "ffn_norm_2", KC * (l in "bd") + c)

        wf = vec[:, VEC["w_forget"]:VEC["w_forget"] + KC * FOX_HEADS].rearrange("p (k n) -> p k n", k=KC)\
            .unsqueeze(2).to_broadcast([P, KC, P // FOX_HEADS, FOX_HEADS])
        TAP_ITEMS, TAP_DONE = tap_order()

        def after(eng, s, n):
            if not (isinstance(n, int) and n <= 0):
                eng.wait_ge(s, n)

        block = ctx.enter_context(nc.Block())

        @block.sync
        def _(sp):
            sp.dma_start(vec[:, :], vectors).then_inc(vec_landed, 16)
            for c in range(KC):
                sp.dma_start(h[:, c, :], x_t[:, c, :]).then_inc(x_landed[c], 16)

            def load(s, j, n):
                sp.dma_start(raw[:, j, :], weights[n]).then_inc(raw_landed[j], 16)

            for j in range(RING):
                load(j, j, j)
            sp.dma_start(identity[:, :], squares[:, 0:P]).then_inc(consts_landed, 16)
            sp.dma_start(causal[:, :], squares[:, P:2 * P]).then_inc(consts_landed, 16)
            sp.dma_start(select[:, :, :], select_d).then_inc(consts_landed, 16)
            with sp.Fori(1, N_SLOTS // RING) as i:
                for j in range(RING):
                    sp.wait_ge(slot_done, RING * (i - 1) + j + 1)
                    sp.dma_start(raw[:, j, :], weights[bass.ds(RING * i + j, 1)].rearrange("o p n -> p (o n)"))\
                      .then_inc(raw_landed[j], 16)
            for n in range(N_SLOTS - N_SLOTS % RING, N_SLOTS):
                sp.wait_ge(slot_done, n - RING + 1)
                load(n, n % RING, n)
            for c in range(KC):
                sp.wait_ge(y_ready, c + 1)
                sp.dma_start(out_t[:, c, :], m[:, c, :]).then_inc(y_stored, 16)
            sp.wait_ge(y_stored, 16 * KC)

        @block.gpsimd
        def _(pool):
            def low_part(s, j):
                pool.wait_ge(hi_ready, s + 1)
                pool.tensor_tensor(w_lo[:, j, :], raw[:, j, :], w_hi[:, j, :].bitcast(F32), ALU.subtract)\
                    .then_inc(w_ready, 1)

            with pool.Fori(0, N_SLOTS // RING) as i:
                for j in range(RING):
                    low_part(RING * i + j, j)
            for n in range(N_SLOTS - N_SLOTS % RING, N_SLOTS):
                low_part(n, n % RING)

        @block.tensor
        def _(pe):
            def product(out, wh, wl, xh, xl, start, stop):
                pe.matmul(out, wh, xh, start=start, stop=False)
                pe.matmul(out, wh, xl, start=False, stop=False)
                return pe.matmul(out, wl, xh, start=False, stop=stop)

            def weight(part, j, k, n=P):
                return part[:, j, k * n:(k + 1) * n]

            def chunk(s, i, out, xh, xl, ready=None):
                j = s % RING
                pe.wait_ge(w_ready, s + RING * i + 1)
                for k in range(KC):
                    if ready:
                        ready(k)
                    last = product(out, weight(w_hi, j, k), weight(w_lo, j, k), xh[:, k, :], xl[:, k, :],
                                   k == 0, k == KC - 1)
                last.then_inc(slot_done, 1)

            def two_chunks(s, outs, xh, xl, ready):
                pe.wait_ge(w_ready, s + 2)
                for k in range(KC):
                    ready(k)
                    for e in range(2):
                        j = (s + e) % RING
                        last = product(outs[e][:, :], weight(w_hi, j, k), weight(w_lo, j, k), xh[:, k, :], xl[:, k, :],
                                       k == 0, k == KC - 1)
                        if k == KC - 1:
                            last.then_inc(slot_done, 1)

            def token_major(s, banks, first, final, free=None):
                j = s % RING
                pe.wait_ge(w_ready, s + 1)
                for t in range(TT):
                    if free:
                        free(t)
                    for k in range(2):
                        xs = slice(t * P, (t + 1) * P)
                        kk = 2 * first + k
                        last = product(banks[t][:, :], u_hi[:, kk, xs], u_lo[:, kk, xs],
                                       weight(w_hi, j, k, 512), weight(w_lo, j, k, 512),
                                       kk == 0, final and k == 1)
                last.then_inc(slot_done, 1)

            def mean_square(name):
                pe.wait_ge(acc_ready, ACC[name] + KC - 1)
                pe.matmul(STAT[:, :], ones[:, :], acc[:, :], start=True, stop=True).then_inc(sum_full, 1)

            def normed_input(name):
                return lambda k: pe.wait_ge(u_ready, SPLIT[name] + k + 1)

            def out_chunks(part, xh, xl, free, ready):
                s = SLOT[part]
                two_chunks(s, bank[0:2], xh, xl, ready)
                for n in range(2, KC):
                    free(n)
                    chunk(s + n, 0, bank[n % 4][:, :], xh, xl)

            def consumed(made):
                def free(n):
                    if n >= 4:
                        pe.wait_ge(made_ready, MADE[made] + n - 3)
                return free

            def added(resid):
                def free(n):
                    if n >= 4:
                        pe.wait_ge(h_ready, RESID[resid] + n - 3)
                return free

            def feed_forward(l):
                s0, s1 = SLOT[f"{l}_ffn_in"], SLOT[f"{l}_ffn_out"]

                def gates(i, b):
                    after(pe, scaled_ready, HID[l] + 2 * i + b - 1 if not isinstance(i, int) or i else 0)
                    chunk(s0 + 2 * b, i, bank[2 * b][:, :], u_hi, u_lo)

                def values(i, b):
                    after(pe, ht_ready, HID[l] + 2 * i + b - 1 if not isinstance(i, int) or i else 0)
                    chunk(s0 + 2 * b + 1, i, bank[2 * b + 1][:, :], u_hi, u_lo)

                two_chunks(s0, bank[0:2], u_hi, u_lo, normed_input(f"{l}_fpre"))
                gates(0, 1)
                mean_square(f"{l}_fpre")
                values(0, 1)
                with pe.Fori(1, FC // 2) as i:
                    for b in range(2):
                        gates(i, b)
                        values(i, b)

                def back(half, n, i=0, first=False, final=False):
                    s = s1 + HALF * half + n
                    j = s % RING
                    pe.wait_ge(w_ready, s + RING * i + 1)
                    if half == 0:
                        pe.wait_ge(hid_ready, HID[l] + 2 * n + 2 * RING * i + 2)
                    for c in range(4):
                        for kk in range(2):
                            xs = [x[:, 2 * n + kk, :] if isinstance(i, int) else
                                  x[:, bass.ds(2 * RING * i + 2 * n + kk, 1), :].rearrange("p o t -> p (o t)")
                                  for x in (hid_hi, hid_lo)]
                            ws = [w[:, j, 512 * kk + P * c:512 * kk + P * (c + 1)] for w in (w_hi, w_lo)]
                            last = product(bank[4 * (1 - half) + c][:, :], *ws, *xs, first and kk == 0, final and kk == 1)
                        if final and c < 3:
                            last.then_inc(out_full, 1)
                    last.then_inc(slot_done, 1)

                for half in range(2):
                    if half:
                        pe.wait_ge(ht_ready, HID[l] + FC)
                    back(half, 0, first=True)
                    with pe.Fori(0, 2) as i:
                        for n in range(1, 1 + RING):
                            back(half, n, i)
                    back(half, 9)
                    back(half, 10, final=True)

            pe.wait_ge(consts_made, 2)

            mean_square("a_pre")
            two_chunks(0, bank[0:2], u_hi, u_lo, normed_input("a_pre"))
            for n in range(2, 8):
                if n >= 4:
                    pe.wait_ge(a_evac, n - 3)
                chunk(n, 0, bank[n % 4][:, :], u_hi, u_lo)
            pe.wait_ge(wf_ready, 2)
            for k in range(KC):
                wide = [w[:, k, :, :].rearrange("p r n -> p (r n)") for w in (wf_hi, wf_lo)]
                last = product(bank[4][:, :], *wide, u_hi[:, k, :], u_lo[:, k, :], k == 0, k == KC - 1)
            last.then_inc(f_full, 1)
            for n in range(4):
                token_major(SLOT["a_v"] + n, bank, n, n == 3, (lambda t: pe.wait_ge(a_evac, 5 + t)) if n == 0 else None)
            pe.wait_ge(consts_landed, 48)

            def scores(hd):
                r, c = slice(64 * (hd % 2), 64 * (hd % 2) + 64), hd // 2
                for qb in range(TT):
                    w = (qb + 1) * P
                    if hd > 0:
                        pe.wait_ge(pt_ready, 4 * hd)
                    s = bank[4 + qb]
                    pe.matmul(s[:, 0:w], aq[r, c, qb * P:w], ak[r, c, 0:w], start=True, stop=False)
                    pe.matmul(s[:, 0:w], select[:, hd, :], ac[:, 0:w], start=False, stop=False)
                    pe.matmul(s[:, qb * P:w], ident, causal[:, :], start=False, stop=True).then_inc(scores_ready, 1)

            def attend(hd):
                r = slice(64 * (hd % 2), 64 * (hd % 2) + 64)
                pe.wait_ge(p_ready, 4 * hd + 4)
                for kt in range(TT):
                    for qb in range(kt, TT):
                        last = pe.transpose(bank[4 + kt][:, qb * P:(qb + 1) * P], ap[:, qb, kt * P:(kt + 1) * P], ident)
                    last.then_inc(pt_full, 1)
                if hd % 2 == 0 and hd >= 2:
                    pe.wait_ge(ol_ready, hd // 2)
                for kt in range(TT):
                    pe.wait_ge(pt_ready, 4 * hd + kt + 1)
                    last = pe.matmul(bank[3][r, kt * P:T], av[:, kt, hd * FOX_DIM:(hd + 1) * FOX_DIM],
                                     apt[:, kt, kt * P:T], start=(kt == 0), stop=(kt == TT - 1))
                last.then_inc(o_ready, 1)

            def conv_slot(n):
                c, kind = n // 3, n % 3
                if n < 3:
                    pe.wait_ge(a_evac, 12)
                elif kind == 0:
                    pe.wait_ge(gc_evac, c)
                elif kind == 1:
                    pe.wait_ge(z_ready, c)
                else:
                    pe.wait_ge(ut_ready, VALUE["a_gate"] + c)
                chunk(SLOT["a_conv"] + n, 0, bank[kind][:, :], u_hi, u_lo)

            pe.wait_ge(c_ready, 1)
            pe.wait_ge(a_evac, 12)
            for hd in range(FOX_HEADS):
                scores(hd)
                for n in range(hd * 12 // 8, (hd + 1) * 12 // 8):
                    conv_slot(n)
                attend(hd)

            def fox_ready(k):
                if k < 4:
                    pe.wait_ge(u_ready, SPLIT["a_gate"] + k + 1)
                else:
                    pe.wait_ge(ol_ready, k - 3)

            out_chunks("a_out", acat_hi, acat_lo, consumed("a_mix"), fox_ready)
            mean_square("a_post")
            feed_forward("a")
            mean_square("a_fpost")

            mean_square("b_pre")
            two_chunks(SLOT["b_in"], bank[0:2], u_hi, u_lo, normed_input("b_pre"))
            for n in range(2, 16):
                if n >= 4:
                    c = (n - 4) // 2
                    pe.wait_ge(b_a if n % 2 == 0 else b_sig, c + 1)
                chunk(SLOT["b_in"] + n, 0, bank[n % 4][:, :], u_hi, u_lo)
            for i, c in enumerate(PE_CHUNKS):
                pe.wait_ge(zl_ready, i + 1)
                for tap in range(LONG_TAPS):
                    n = LONG_TAPS * i + tap
                    pe.wait_ge(dg_ready, 2 * n + 2)
                    product(bank[5 + i][:, :], dg_hi[:, n % 4, :], dg_lo[:, n % 4, :], bz_hi[:, i, tap:tap + T],
                            bz_lo[:, i, tap:tap + T], tap == 0, tap == LONG_TAPS - 1).then_inc(dg_used, 1)
            for n, c in enumerate(range(KC)):
                if c in PE_CHUNKS:
                    pe.wait_ge(tap_evac, PE_CHUNKS.index(c) + 1)
                else:
                    pe.wait_ge(taps, TAP_DONE[c, LONG_TAPS - 1])
                last = pe.matmul(STAT[:, :], ones[:, :], by[:, c, :], start=(c == 0), stop=(c == KC - 1))
            last.then_inc(mean_full, 1)
            pe.wait_ge(mean_ready, 1)
            for c in range(KC):
                pe.wait_ge(sq_ready, SQ["b_var"] + c + 1)
                pe.matmul(STAT[:, :], ones[:, :], sq[:, c % 2, :], start=(c == 0), stop=(c == KC - 1)).then_inc(sq_used, 1)
            out_chunks("b_out", by_hi, by_lo, consumed("b_mix"), normed_input("b_ln"))
            mean_square("b_post")
            feed_forward("b")
            mean_square("b_fpost")

            mean_square("c_pre")
            two_chunks(SLOT["c_fq"], bank[0:2], u_hi, u_lo, normed_input("c_pre"))
            for n in range(2, 16):
                c = n // 2
                if n >= 4:
                    if n % 2 == 0:
                        pe.wait_ge(c_sig, 2 * c - 3)
                    else:
                        pe.wait_ge(c_qkf, 3 * (c - 1))
                chunk(SLOT["c_fq"] + n, 0, bank[n % 4][:, :], u_hi, u_lo)

            def value_slot(n):
                def free(t):
                    if n == 0:
                        pe.wait_ge(c_qkf, 3 * KC)
                    elif n == 4:
                        pe.wait_ge(i_evac, t + 1)
                token_major(SLOT["c_i"] + n, bank, n % 4, n % 4 == 3, free if n in (0, 4) else None)

            def gate_slot(n):
                if n < 2:
                    pe.wait_ge(co_evac, n + 1)
                else:
                    pe.wait_ge(g_ready, n - 1)
                chunk(SLOT["c_g"] + n, 0, bank[n % 2][:, :], u_hi, u_lo)

            def head_square(hd):
                pe.wait_ge(sq_ready, SQ["c_head"] + hd + 1)
                if hd < 4:
                    pe.wait_ge(co_evac, 4)
                    out = bank[2 + hd % 2]
                else:
                    pe.wait_ge(far_kept, 16)
                    out = bank[hd]
                after(pe, rs_ready, RS["c_head"] + hd - 1)
                pe.matmul(out[:, :], ones[:, :], sq[:, hd % 2, :], start=True, stop=True).then_inc(sq_used, 1)

            N_LEVEL = 1 + len(LEVELS)
            PER_HEAD = 1 + 3 * 8
            for g in range(2):
                for lv in range(N_LEVEL):
                    for e in range(4):
                        hd = 4 * g + e
                        if lv == 0:
                            after(pe, c_qkf, 3 * KC)
                            if g:
                                pe.wait_ge(far_kept, 8)
                        else:
                            pe.wait_ge(upd, upd_count(g, lv, e))
                            pe.wait_ge(level_kept, 4 * (N_LEVEL * g + lv - 1) + e + 1)
                        for t in range(TT):
                            s = slice(t * P, (t + 1) * P)
                            if lv == 0:
                                out, queries = bank[4 + e][:, s], cq[:, hd, s]
                            else:
                                out = bank[4 + e][:, t * P // 2:(t + 1) * P // 2]
                                queries = cq[:, hd, s].rearrange("p (b two s) -> p b two s", two=2, s=LEVELS[lv - 1])[:, :, 1, :]
                            last = pe.matmul(out, ck[:, hd, s], queries, start=True, stop=True)
                        last.then_inc(level_full, 1)
                    (gate_slot if g else value_slot)(lv)
                    if g and 1 <= lv <= 4:
                        head_square(lv - 1)
                for e in range(4):
                    hd = 4 * g + e
                    pe.wait_ge(level_kept, 4 * (N_LEVEL * g + N_LEVEL - 1) + e + 1)
                    if g == 0:
                        pe.wait_ge(i_evac, KC)
                    else:
                        pe.wait_ge(g_ready, KC)
                    for t in range(TT):
                        last = pe.matmul(bank[e][:, t * P:(t + 1) * P], cv[:, t, hd * P:(hd + 1) * P],
                                         ca[:, e, t * P:(t + 1) * P], start=(t == 0), stop=False, skip_group_check=True)
                    last.then_inc(pv_part, 1)
                for far in range(2):
                    for e in range(4):
                        hd = 4 * g + e
                        pe.wait_ge(upd, upd_count(g, N_LEVEL + far, e))
                        if far:
                            pe.wait_ge(far_kept, 8 * g + e + 1)
                        if far == 0:
                            for i in range(2):
                                last = pe.matmul(bank[4 + e][:, i * P:(i + 1) * P], ck[:, hd, 2 * i * P:(2 * i + 1) * P],
                                                 cq[:, hd, (2 * i + 1) * P:(2 * i + 2) * P], start=True, stop=True)
                        else:
                            for i in range(2):
                                last = pe.matmul(bank[4 + e][:, 2 * i * P:2 * (i + 1) * P], ck[:, hd, i * P:(i + 1) * P],
                                                 cq[:, hd, 2 * P:4 * P], start=True, stop=True)
                        last.then_inc(far_full, 1)
                    for e in range(4):
                        hd = 4 * g + e
                        pe.wait_ge(far_kept, 8 * g + 4 * far + e + 1)
                        for i in range(2):
                            if far == 0:
                                last = pe.matmul(bank[e][:, (2 * i + 1) * P:(2 * i + 2) * P],
                                                 cv[:, 2 * i, hd * P:(hd + 1) * P], ca[:, e, i * P:(i + 1) * P],
                                                 start=False, stop=False, skip_group_check=True)
                            else:
                                last = pe.matmul(bank[e][:, 2 * P:4 * P], cv[:, i, hd * P:(hd + 1) * P],
                                                 ca[:, e, 2 * i * P:2 * (i + 1) * P], start=False, stop=(i == 1),
                                                 skip_group_check=True)
                        last.then_inc(pv_part if far == 0 else co_full, 1)
            for hd in range(4, HG_HEADS):
                head_square(hd)
            out_chunks("c_out", ccat_hi, ccat_lo, added("c_mix"), normed_input("c_out"))
            feed_forward("c")

            mean_square("d_pre")
            chunk(SLOT["d_kv"], 0, bank[0][:, :], u_hi, u_lo, normed_input("d_kv"))
            jv = (SLOT["d_kv"] + 1) % RING
            pe.wait_ge(w_ready, SLOT["d_kv"] + 2)
            for t in range(TT):
                for k in range(KC):
                    ts = slice(t * P, (t + 1) * P)
                    last = product(bank[1][:, ts], u_hi[:, k, ts], u_lo[:, k, ts], weight(w_hi, jv, k), weight(w_lo, jv, k),
                                   k == 0, k == KC - 1)
            last.then_inc(slot_done, 1)

            def window_scores(c):
                kv = c // 4
                for n in range(TT):
                    lo = 0 if n else P
                    if c == 1:
                        pe.wait_ge(ds_ready, 8)
                    if c >= 2:
                        pe.wait_ge(dpt_ready, 4 * (c - 1))
                    for e in range(2):
                        r = slice(64 * e, 64 * e + 64)
                        last = pe.matmul(window_bank(n, e)[:, lo:],
                                         dq[r, c, n * P:(n + 1) * P], dk[r, kv, (n - 1) * P + lo:(n + 1) * P],
                                         start=True, stop=True)
                    last.then_inc(ds_full, 1)

            def window_attend(c):
                kv = c // 4
                pe.wait_ge(ds_ready, 8 * min(c + 2, KC))
                for n in range(TT):
                    pe.wait_ge(ds_p, 8 * c + 2 * n + 2)
                    for kt in range(0 if n else 1, 2):
                        for e in range(2):
                            last = pe.transpose(bank[4 + n][:, (2 * kt + e) * P:(2 * kt + e + 1) * P],
                                                ds_[:, c % 2, n, e, kt * P:(kt + 1) * P], ident)
                    last.then_inc(dpt_full, 1)
                if c >= 2:
                    pe.wait_ge(dol_ready, c - 1)
                o = bank[2 + c % 2]
                for n in range(TT):
                    pe.wait_ge(dpt_ready, 4 * c + n + 1)
                    for e in range(2):
                        first = 0 if n else 1
                        for kt in range(first, 2):
                            last = pe.matmul(o[64 * e:64 * e + 64, n * P:(n + 1) * P],
                                             dv[:, n - 1 + kt, 64 * kv:64 * kv + 64],
                                             dpt[:, n, (2 * kt + e) * P:(2 * kt + e + 1) * P],
                                             start=(kt == first), stop=(kt == 1))
                last.then_inc(do_ready, 1)

            def query_slot(n):
                pe.wait_ge(d_q_evac, n - 1)
                chunk(SLOT["d_q"] + n, 0, bank[n % 2][:, :], u_hi, u_lo)

            pe.wait_ge(d_kv_evac, 5)
            two_chunks(SLOT["d_q"], bank[0:2], u_hi, u_lo, normed_input("d_q"))
            pe.wait_ge(d_q_evac, 1)
            window_scores(0)
            for c in range(KC):
                if c + 1 < KC:
                    pe.wait_ge(d_q_evac, c + 2)
                    window_scores(c + 1)
                if c + 2 < KC:
                    query_slot(c + 2)
                window_attend(c)
            out_chunks("d_out", dcat_hi, dcat_lo, added("d_mix"), lambda k: pe.wait_ge(dol_ready, k + 1))
            feed_forward("d")
            mean_square("final")

        @block.scalar
        def _(act):
            def high_part(s, i=0):
                j = s % RING
                act.wait_ge(raw_landed[j], 16 * i + 16 * (s // RING + 1))
                act.activation(w_hi[:, j, :], raw[:, j, :], ACT.Copy).then_inc(hi_ready, 1)

            def slot_over(s, i=0):
                act.wait_ge(slot_done, s + RING * i + 1)
                if s + AHEAD < N_SLOTS:
                    high_part(s + AHEAD, i)

            def square(name, c, src):
                if c >= 2:
                    if name in DIRECT:
                        act.wait_ge(sq_used, USED[name] + c - 1)
                    else:
                        act.wait_ge(acc_ready, ACC[name] + max(c - 2, 1))
                act.activation(sq[:, c % 2, :], src, ACT.Square).then_inc(sq_ready, 1)

            def root(name, i=0, src=STAT, scale=1.0 / D, e=0):
                n = RS[name] + i
                if name in SUM:
                    act.wait_ge(sum_full, SUM[name] + 1)
                act.activation(rs[:, :], src[:, :], ACT.Ln, bias=eps[:, e:e + 1], scale=scale).then_inc(rs_ln, 1)
                act.wait_ge(rs_ln, n + 1)
                act.activation(rs[:, :], rs[:, :], ACT.Exp, scale=-0.5).then_inc(rs_ready, 1)

            def square_h(name, resid, chunks=range(KC)):
                for c in chunks:
                    act.wait_ge(x_landed[c] if resid is None else h_ready, 16 if resid is None else RESID[resid] + c + 1)
                    square(name, c, h[:, c, :])

            def scaled_input(l, resid, chunks=range(KC)):
                for c in chunks:
                    act.wait_ge(h_ready, RESID[resid] + c + 1)
                    act.activation(u_hi[:, c, :], h[:, c, :], ACT.Identity, scale=ffn_gain(l, c)).then_inc(uh_ready, 1)

            def high_of(name, c, dst):
                act.wait_ge(ut_ready, VALUE[name] + c + 1)
                act.activation(dst, ut[:, (VALUE[name] + c) % 2, :], ACT.Copy).then_inc(uh_ready, 1)

            def split_input(name):
                for c in range(KC):
                    high_of(name, c, u_hi[:, c, :])

            def square_out(part, stat, made):
                for n in range(KC):
                    slot_over(SLOT[part] + n)
                    act.wait_ge(made_ready, MADE[made] + n + 1)
                    square(stat, n, m[:, n, :])
                root(stat)

            def feed_forward(l, second):
                s0, s1 = SLOT[f"{l}_ffn_in"], SLOT[f"{l}_ffn_out"]

                def pair(i, b, over=True):
                    j = 2 * i + b
                    if over:
                        slot_over(s0 + 2 * b, i)
                    act.wait_ge(scaled_ready, HID[l] + j + 1)
                    if second is not None:
                        def one(name, at):
                            at += VEC[name] + b
                            return vec[:, at:at + 1] if isinstance(i, int) else vec[:, bass.ds(2 * i + at, 1)]
                        act.activation(gconv[:, b, :], ut[:, b, :], ACT.Identity, bias=one("ffn_conv_b", second * FC),
                                       scale=one("ffn_conv_w", (second * FFN_TAPS + 2) * FC)).then_inc(gconv0_ready, 1)
                        act.wait_ge(gconv_ready, CONVG[l] + 2 * j + 2)
                    act.activation(gconv[:, b, :], gconv[:, b, :], ACT.Silu).then_inc(gate_ready, 1)
                    if over:
                        slot_over(s0 + 2 * b + 1, i)

                slot_over(s0)
                slot_over(s0 + 1)
                slot_over(s0 + 2)
                root(f"{l}_fpre")
                pair(0, 0, False)
                slot_over(s0 + 3)
                pair(0, 1, False)
                with act.Fori(1, FC // 2) as i:
                    for b in range(2):
                        pair(i, b)

            def way_back(l, half):
                s = SLOT[f"{l}_ffn_out"] + HALF * half
                with act.Fori(0, 2) as i:
                    for n in range(RING):
                        slot_over(s + n, i)
                for n in range(2 * RING, HALF):
                    slot_over(s + n)

            def ffn_square_out(l, stat):
                for half in range(2):
                    way_back(l, half)
                    for n in range(4 * half, 4 * half + 4):
                        act.wait_ge(made_ready, MADE[f"{l}_ffn"] + n + 1)
                        square(stat, n, m[:, n, :])
                root(stat)

            act.wait_ge(consts_made, 2)

            square_h("a_pre", None)
            root("a_pre")
            for n in range(AHEAD):
                high_part(n)
            split_input("a_pre")
            act.activation(wf_hi[:, :, :, :], wf, ACT.Copy).then_inc(wf_ready, 1)
            for n in range(8):
                slot_over(n)
                act.activation((aq if n < 4 else ak)[:, n % 4, :], bank[n % 4][:, :], ACT.Copy,
                               scale=FOX_DIM ** -0.5 if n < 4 else 1.0).then_inc(a_evac, 1)
            act.wait_ge(f_read, 1)
            f8 = slice(0, FOX_HEADS)
            act.activation(ap[f8, 1, :], ap[f8, 0, :], ACT.Abs).then_inc(f_exp, 1)
            act.wait_ge(f_exp, 1)
            act.activation(ap[f8, 1, :], ap[f8, 1, :], ACT.Exp, scale=-1.0).then_inc(f_exp, 1)
            act.wait_ge(f_exp, 2)
            act.activation(ap[f8, 1, :], ap[f8, 1, :], ACT.Ln, bias=1.0).then_inc(f_ln, 1)
            for n in range(4):
                slot_over(SLOT["a_v"] + n)
            for t in range(TT):
                act.activation(av[:, t, :], bank[t][:, :], ACT.Copy).then_inc(a_evac, 1)
            nmax, rsum = small[:, 0:8], small[:, 8:16]
            for hd in range(FOX_HEADS):
                for qb in range(TT):
                    w, i = (qb + 1) * P, 4 * (hd % 2) + qb
                    act.wait_ge(max_ready, 4 * hd + qb + 1)
                    after(act, pt_full, 4 * hd)
                    act.activation(ap[:, qb, 0:w], bank[4 + qb][:, 0:w], ACT.Exp, bias=nmax[:, i:i + 1],
                                   accum_out=rsum[:, i:i + 1]).then_inc(exp_ready, 1)
                for n in range(hd * 12 // 8, (hd + 1) * 12 // 8):
                    c, kind = n // 3, n % 3
                    slot_over(SLOT["a_conv"] + n)
                    if kind == 0:
                        after(act, z_ready, c)
                        act.activation(agc[:, :], bank[0][:, :], ACT.Copy).then_inc(gc_evac, 1)
                    if kind == 2:
                        high_of("a_gate", c, acat_hi[:, c, :])
                for kt in range(TT):
                    act.wait_ge(pt_full, 4 * hd + kt + 1)
                    after(act, o_ready, hd)
                    act.activation(apt[:, kt, kt * P:T], bank[4 + kt][:, kt * P:T], ACT.Copy).then_inc(pt_ready, 1)
                if hd % 2:
                    act.wait_ge(o_ready, hd + 1)
                    act.activation(acat_hi[:, 4 + hd // 2, :], bank[3][:, :], ACT.Copy).then_inc(oh_ready, 1)
            square_out("a_out", "a_post", "a_mix")
            scaled_input("a", "a_mix")
            square_h("a_fpre", "a_mix")
            feed_forward("a", None)
            ffn_square_out("a", "a_fpost")

            square_h("b_pre", "a_ffn")
            root("b_pre")
            split_input("b_pre")
            act.activation(wt_hi[:, :], col("w_dw", 0, LONG_TAPS * KC), ACT.Copy).then_inc(wt_ready, 1)

            def high_gated(i):
                act.wait_ge(bz_ready, PE_CHUNKS[i] + 1)
                act.activation(bz_hi[:, i, :], bz[:, PE_CHUNKS[i], :], ACT.Copy).then_inc(zh_ready, 1)

            for n in range(16):
                c = n // 2
                slot_over(SLOT["b_in"] + n)
                after(act, bz_ready, c - 1)
                if n % 2 == 0:
                    act.activation(ba[:, c % 2, 0, :], bank[n % 4][:, :], ACT.Identity, bias=col("b_pw1", c)).then_inc(b_a, 1)
                else:
                    act.activation(ba[:, c % 2, 1, :], bank[n % 4][:, :], ACT.Sigmoid, bias=col("b_pw1", KC + c)).then_inc(b_sig, 1)
            act.wait_ge(wt_ready, 2)
            for i, c in enumerate(PE_CHUNKS):
                high_gated(i)
                for tap in range(LONG_TAPS):
                    n = LONG_TAPS * i + tap
                    after(act, dg_used, n - 3)
                    at = tap * KC + c
                    act.activation(dg_hi[:, n % 4, :], ident, ACT.Identity, scale=col("w_dw", at)).then_inc(dg_ready, 1)
                    act.activation(dg_lo[:, n % 4, :], ident, ACT.Identity, scale=wt_lo[:, at:at + 1]).then_inc(dg_ready, 1)
                act.wait_ge(dg_used, LONG_TAPS * (i + 1))
                act.activation(by[:, c, :], bank[5 + i][:, :], ACT.Identity, bias=col("b_dw", c)).then_inc(tap_evac, 1)
            act.wait_ge(mean_full, 1)
            act.activation(bmean[:, :], STAT[:, :], ACT.Copy, scale=1.0 / D).then_inc(mean_ready, 1)
            for c in range(KC):
                act.wait_ge(xc_ready, c + 1)
                square("b_var", c, by[:, c, :])
            act.wait_ge(sq_used, USED["b_var"] + KC)
            root("b_var", e=1)
            for c in range(KC):
                n, v = SPLIT["b_ln"] + c, VALUE["b_ln"] + c
                act.wait_ge(yn_ready, c + 1)
                act.wait_ge(u_ready, n - 1)
                act.activation(ut[:, v % 2, :], by[:, c, :], ACT.Silu, bias=col("ln_b", c), scale=col("ln_g", c))\
                   .then_inc(ut_ready, 1)
                act.wait_ge(ut_ready, v + 1)
                act.activation(by_hi[:, c, :], ut[:, v % 2, :], ACT.Copy).then_inc(uh_ready, 1)
            square_out("b_out", "b_post", "b_mix")
            scaled_input("b", "b_mix")
            square_h("b_fpre", "b_mix")
            feed_forward("b", None)
            ffn_square_out("b", "b_fpost")

            act.dma_start(cmask[:, :, :], masks_d).then_inc(mask_landed, 16)
            square_h("c_pre", "b_ffn")
            root("c_pre")
            split_input("c_pre")
            act.wait_ge(lb_step, 3)
            act.activation(small[:, 16:32], small[:, 16:32], ACT.Exp).then_inc(lb_step, 1)
            for n in range(16):
                slot_over(SLOT["c_fq"] + n)
                act.activation((cq if n % 2 else cf)[:, n // 2, :], bank[n % 4][:, :], ACT.Sigmoid).then_inc(c_sig, 1)

            def value_over(n):
                slot_over(SLOT["c_i"] + n)
                if n % 4 == 3:
                    half = slice(512 * (n // 4), 512 * (n // 4) + 512)
                    for t in range(TT):
                        act.activation(cv[:, t, half], bank[t][:, :], ACT.Copy).then_inc(i_evac, 1)

            def gate_over(n):
                slot_over(SLOT["c_g"] + n)
                act.activation(cg[:, n, :], bank[n % 2][:, :], ACT.Sigmoid).then_inc(g_sig, 1)

            def head_norm(hd):
                src = bank[2 + hd % 2] if hd < 4 else bank[hd]
                act.wait_ge(sq_used, USED["c_head"] + hd + 1)
                if hd:
                    act.wait_ge(ut_ready, VALUE["c_out"] + hd)
                root("c_head", hd, src, 1.0 / P)
                high_of("c_out", hd, ccat_hi[:, hd, :])

            for g in range(2):
                for lv in range(8):
                    if g and 1 <= lv <= 4:
                        square("c_head", lv - 1, cf[:, lv - 1, :])
                    (gate_over if g else value_over)(lv)
                    if g and 1 <= lv <= 4:
                        head_norm(lv - 1)
                for far in range(2):
                    for e in range(4):
                        w = T if far else 2 * P
                        act.wait_ge(far_full, 8 * g + 4 * far + e + 1)
                        act.wait_ge(pv_part, 8 * g + 4 * far + e + 1)
                        act.activation(ca[:, e, 0:w], bank[4 + e][:, 0:w], ACT.Copy).then_inc(far_kept, 1)
                for e in range(4):
                    act.wait_ge(co_full, 4 * g + e + 1)
                    act.activation(cf[:, 4 * g + e, :], bank[e][:, :], ACT.Copy).then_inc(co_evac, 1)
            for hd in range(4, HG_HEADS):
                act.wait_ge(co_evac, hd + 1)
                square("c_head", hd, cf[:, hd, :])
                if hd > 4:
                    head_norm(hd - 1)
            head_norm(HG_HEADS - 1)

            def add_over(l):
                for n in range(KC):
                    slot_over(SLOT[f"{l}_out"] + n)
                    scaled_input(l, f"{l}_mix", (n,))
                    square_h(f"{l}_fpre", f"{l}_mix", (n,))

            add_over("c")
            feed_forward("c", 0)
            for half in range(2):
                way_back("c", half)
                square_h("d_pre", "c_ffn", range(4 * half, 4 * half + 4))

            act.dma_start(dist[:, :], squares[:, 2 * P:]).then_inc(dist_landed, 16)
            root("d_pre")
            split_input("d_kv")
            slot_over(SLOT["d_kv"])
            for kv in range(2):
                for half in range(2):
                    act.activation(dk[64 * half:64 * half + 64, kv, :], bank[0][64 * kv:64 * kv + 64, :], ACT.Copy)\
                       .then_inc(d_kv_evac, 1)
            slot_over(SLOT["d_kv"] + 1)
            act.activation(dv[:, :, :], bank[1][:, :].rearrange("p (t n) -> p t n", t=TT), ACT.Copy).then_inc(d_kv_evac, 1)
            split_input("d_q")

            def query_over(n):
                slot_over(SLOT["d_q"] + n)
                act.activation(dq[:, n, :], bank[n % 2][:, :], ACT.Copy, scale=SWA_DIM ** -0.5).then_inc(d_q_evac, 1)

            def window_exp(c):
                _, nm, den, es = window_small(c)
                act.wait_ge(ds_nm, 2 * c + 2)
                act.activation(es, es, ACT.Exp).then_inc(ds_sink, 1)
                for n in range(TT):
                    lo = 0 if n else P
                    for e in range(2):
                        i, p = 2 * n + e, ds_[:, c % 2, n, e, lo:]
                        act.activation(p, p, ACT.Exp, bias=nm[:, i:i + 1], accum_out=den[:, i:i + 1]).then_inc(ds_exp, 1)

            query_over(0)
            query_over(1)
            window_exp(0)
            for c in range(KC):
                if c + 1 < KC:
                    window_exp(c + 1)
                if c + 2 < KC:
                    query_over(c + 2)
                for n in range(TT):
                    lo = 0 if n else 2 * P
                    act.wait_ge(dpt_full, 4 * c + n + 1)
                    after(act, do_ready, c)
                    act.activation(dpt[:, n, lo:], bank[4 + n][:, lo:], ACT.Copy).then_inc(dpt_ready, 1)
                act.wait_ge(do_ready, c + 1)
                act.activation(dcat_hi[:, c, :], bank[2 + c % 2][:, :], ACT.Copy).then_inc(doh_ready, 1)
            add_over("d")
            feed_forward("d", 1)
            for half in range(2):
                way_back("d", half)
                square_h("final", "d_ffn", range(4 * half, 4 * half + 4))
            root("final")

        @block.vector
        def _(dve):
            def split_value(name, c, make):
                if c >= 2:
                    dve.wait_ge(u_ready, SPLIT[name] + c - 1)
                make(ut[:, (VALUE[name] + c) % 2, :]).then_inc(ut_ready, 1)

            def low_of(name, c, dst, hi):
                dve.wait_ge(uh_ready, SPLIT[name] + c + 1)
                dve.tensor_tensor(dst, ut[:, (VALUE[name] + c) % 2, :], hi.bitcast(F32), ALU.subtract).then_inc(u_ready, 1)

            def norm_input(name, stat, gain, at):
                dve.wait_ge(rs_ready, RS[stat] + 1)
                for c in range(KC + 1):
                    if c < KC:
                        split_value(name, c, lambda dst: dve.scalar_tensor_tensor(
                            out=dst, in0=h[:, c, :], scalar=col(gain, at + c), in1=rs[:, :], op0=ALU.mult, op1=ALU.mult))
                    if c:
                        low_of(name, c - 1, u_lo[:, c - 1, :], u_hi[:, c - 1, :])

            def sum_squares(name, chunks=range(1, KC)):
                for c in chunks:
                    dve.wait_ge(sq_ready, SQ[name] + c + 1)
                    if c >= 2:
                        dve.wait_ge(acc_ready, ACC[name] + c - 1)
                    dve.tensor_tensor(acc[:, :], sq[:, 0, :] if c == 1 else acc[:, :], sq[:, c % 2, :], ALU.add).then_inc(acc_ready, 1)

            def scaled_low(l, c):
                dve.wait_ge(uh_ready, SPLIT[f"{l}_fpre"] + c + 1)
                dve.scalar_tensor_tensor(out=u_lo[:, c, :], in0=h[:, c, :], scalar=ffn_gain(l, c), in1=u_hi[:, c, :].bitcast(F32),
                                         op0=ALU.mult, op1=ALU.subtract).then_inc(u_ready, 1)

            def norm_add(made, resid, stat, gain, at, l=None):
                dve.wait_ge(rs_ready, RS[stat] + 1)
                for c in range(KC + 2):
                    if c < KC:
                        dve.wait_ge(made_ready, MADE[made] + c + 1)
                        dve.tensor_tensor(m[:, c, :], m[:, c, :], rs[:, :], ALU.mult).then_inc(normed, 1)
                    if 1 <= c <= KC:
                        dve.wait_ge(normed, MADE[made] + c)
                        dve.scalar_tensor_tensor(out=h[:, c - 1, :], in0=m[:, c - 1, :], scalar=col(gain, at + c - 1),
                                                 in1=h[:, c - 1, :], op0=ALU.mult, op1=ALU.add).then_inc(h_ready, 1)
                    if l and c >= 2:
                        scaled_low(l, c - 2)

            def keep_out(part, stat, bias=None):
                for n in range(KC):
                    dve.wait_ge(slot_done, SLOT[part] + n + 1)
                    if bias:
                        dve.tensor_scalar(m[:, n, :], bank[n % 4][:, :], bias(n), None, ALU.add).then_inc(made_ready, 1)
                    else:
                        dve.tensor_copy(m[:, n, :], bank[n % 4][:, :]).then_inc(made_ready, 1)
                    if n >= 2:
                        sum_squares(stat, (n - 1,))
                sum_squares(stat, (KC - 1,))

            def ffn_full(l, n):
                half, c = n // 4, n % 4
                if c < 3:
                    dve.wait_ge(out_full, FULL[l] + 3 * half + c + 1)
                else:
                    dve.wait_ge(slot_done, SLOT[f"{l}_ffn_out"] + HALF * (half + 1))
                return bank[4 * (1 - half) + c]

            def add_out(l):
                for n in range(KC + 1):
                    if n < KC:
                        dve.wait_ge(slot_done, SLOT[f"{l}_out"] + n + 1)
                        dve.tensor_tensor(h[:, n, :], h[:, n, :], bank[n % 4][:, :], ALU.add).then_inc(h_ready, 1)
                    if n:
                        scaled_low(l, n - 1)
                    if n >= 2:
                        sum_squares(f"{l}_fpre", (n - 1,))

            def add_ffn(l, stat):
                for half in range(2):
                    for n in range(4 * half, 4 * half + 4):
                        src = ffn_full(l, n)
                        dve.tensor_tensor(h[:, n, :], h[:, n, :], src[:, :], ALU.add).then_inc(h_ready, 1)
                        if n % 4 >= 2 or (half and n % 4 >= 1):
                            sum_squares(stat, (n - 1,))
                    sum_squares(stat, (4 * half + 3,))

            def feed_forward(l, second):
                s0 = SLOT[f"{l}_ffn_in"]

                def at(t, j, i):
                    return t[:, j, :] if isinstance(i, int) else t[:, bass.ds(j, 1), :].rearrange("p o t -> p (o t)")

                def pair(i, b):
                    j = 2 * i + b
                    scaled = gconv if second is None else ut
                    dve.wait_ge(slot_done, s0 + 2 * j + 1)
                    if not isinstance(i, int) or i:
                        dve.wait_ge(hid_ready, HID[l] + j - 1)
                    else:
                        dve.wait_ge(rs_ready, RS[f"{l}_fpre"] + 1)
                    dve.tensor_tensor(scaled[:, b, :], bank[2 * b][:, :], rs[:, :], ALU.mult).then_inc(scaled_ready, 1)
                    if second is not None:
                        dve.wait_ge(gconv0_ready, HID[l] - HID["c"] + j + 1)
                        for tap in (1, 0):
                            back = 2 - tap
                            base = VEC["ffn_conv_w"] + (second * FFN_TAPS + tap) * FC + b
                            w = vec[:, base:base + 1] if isinstance(i, int) else vec[:, bass.ds(2 * i + base, 1)]
                            if tap == 0:
                                dve.wait_ge(gconv_ready, CONVG[l] + 2 * j + 1)
                            dve.scalar_tensor_tensor(out=gconv[:, b, back:], in0=ut[:, b, 0:T - back], scalar=w,
                                                     in1=gconv[:, b, back:], op0=ALU.mult, op1=ALU.add).then_inc(gconv_ready, 1)
                    dve.wait_ge(slot_done, s0 + 2 * j + 2)
                    dve.wait_ge(gate_ready, HID[l] + j + 1)
                    dve.tensor_tensor(ut[:, b, :], gconv[:, b, :], bank[2 * b + 1][:, :], ALU.mult).then_inc(ht_ready, 1)
                    dve.wait_ge(ht_ready, HID[l] + j + 1)
                    dve.tensor_tensor(ut[:, b, :], ut[:, b, :], rs[:, :], ALU.mult).then_inc(t2_ready, 1)
                    dve.wait_ge(t2_ready, HID[l] + j + 1)
                    hi, lo = at(hid_hi, j, i), at(hid_lo, j, i)
                    dve.tensor_scalar(hi, ut[:, b, :], 1.0, None, ALU.mult).then_inc(hh_ready, 1)
                    dve.wait_ge(hh_ready, HID[l] + j + 1)
                    dve.tensor_tensor(lo, ut[:, b, :], hi.bitcast(F32), ALU.subtract).then_inc(hid_ready, 1)

                pair(0, 0)
                pair(0, 1)
                with dve.Fori(1, FC // 2) as i:
                    for b in range(2):
                        pair(i, b)

            def keep_ffn(l, stat):
                for half in range(2):
                    for n in range(4 * half, 4 * half + 4):
                        src = ffn_full(l, n)
                        dve.tensor_copy(m[:, n, :], src[:, :]).then_inc(made_ready, 1)
                        if n % 4 >= 2 or (half and n % 4 >= 1):
                            sum_squares(stat, (n - 1,))
                    sum_squares(stat, (4 * half + 3,))

            dve.memset(ones[:, :], 1.0).then_inc(consts_made, 1)
            dve.memset(eps[:, 0:1], RMS_EPS)
            dve.memset(eps[:, 1:2], LN_EPS).then_inc(consts_made, 1)
            dve.memset(az[:, :, 0:SHORT_TAPS - 1], 0.0)
            dve.wait_ge(vec_landed, 16)

            sum_squares("a_pre")
            norm_input("a_pre", "a_pre", "mix_pre", 0)
            dve.wait_ge(wf_ready, 1)
            dve.tensor_tensor(wf_lo[:, :, :, :], wf, wf_hi[:, :, :, :].bitcast(F32), ALU.subtract).then_inc(wf_ready, 1)
            f8 = slice(0, FOX_HEADS)
            dve.wait_ge(f_full, 1)
            dve.tensor_scalar(ap[f8, 0, :], bank[4][f8, :], vec[f8, VEC["b_forget"]:VEC["b_forget"] + 1], None, ALU.add)\
               .then_inc(f_read, 1)
            dve.wait_ge(f_ln, 1)
            dve.wait_ge(f_read, 1)
            dve.scalar_tensor_tensor(out=ap[f8, 2, :], in0=ap[f8, 0, :], scalar=0.0, in1=ap[f8, 1, :],
                                     op0=ALU.min, op1=ALU.subtract).then_inc(logf, 1)
            dve.memset(ap[f8, 3, :], 1.0).then_inc(logf, 1)
            dve.wait_ge(logf, 2)
            dve.tensor_tensor_scan(ac[:, :], ap[f8, 3, :], ap[f8, 2, :], 0.0, ALU.mult, ALU.add).then_inc(c_ready, 1)
            nmax, rsum, rinv = small[:, 0:8], small[:, 8:16], small[:, 48:56]
            dve.wait_ge(c_ready, 1)
            for hd in range(FOX_HEADS):
                o4 = 4 * (hd % 2)
                for qb in range(TT):
                    dve.wait_ge(scores_ready, 4 * hd + qb + 1)
                    dve.tensor_reduce(nmax[:, o4 + qb:o4 + qb + 1], bank[4 + qb][:, 0:(qb + 1) * P], AX_X, ALU.max,
                                      negate=True).then_inc(max_ready, 1)
                dve.wait_ge(exp_ready, 4 * hd + 4)
                dve.reciprocal(rinv[:, o4:o4 + 4], rsum[:, o4:o4 + 4]).then_inc(inv_ready, 1)
                dve.wait_ge(inv_ready, hd + 1)
                for qb in range(TT):
                    w = (qb + 1) * P
                    dve.tensor_scalar(ap[:, qb, 0:w], ap[:, qb, 0:w], rinv[:, o4 + qb:o4 + qb + 1], None, ALU.mult)\
                       .then_inc(p_ready, 1)
                for n in range(hd * 12 // 8, (hd + 1) * 12 // 8):
                    c, kind = n // 3, n % 3
                    dve.wait_ge(slot_done, SLOT["a_conv"] + n + 1)
                    if kind == 1:
                        dve.wait_ge(gc_evac, c + 1)
                        dve.tensor_tensor(az[:, c, SHORT_TAPS - 1:], agc[:, :], bank[1][:, :], ALU.mult).then_inc(z_ready, 1)
                        dve.wait_ge(z_ready, c + 1)
                        after(dve, ut_ready, VALUE["a_gate"] + c if c else 0)
                        for i, tap in enumerate((2, 1, 0)):
                            w = col("short_conv", tap * 4 + c)
                            if i == 0:
                                ins = dve.tensor_scalar(ay[:, :], az[:, c, tap:tap + T], w, None, ALU.mult)
                            else:
                                dve.wait_ge(sconv, 3 * c + i)
                                ins = dve.scalar_tensor_tensor(out=ay[:, :], in0=az[:, c, tap:tap + T], scalar=w,
                                                               in1=ay[:, :], op0=ALU.mult, op1=ALU.add)
                            ins.then_inc(sconv, 1)
                    if kind == 2:
                        dve.wait_ge(sconv, 3 * c + 3)
                        split_value("a_gate", c, lambda dst: dve.tensor_tensor(dst, ay[:, :], bank[2][:, :], ALU.mult))
                        low_of("a_gate", c, acat_lo[:, c, :], acat_hi[:, c, :])
                if hd % 2:
                    c = 4 + hd // 2
                    dve.wait_ge(oh_ready, hd // 2 + 1)
                    dve.tensor_tensor(acat_lo[:, c, :], bank[3][:, :], acat_hi[:, c, :].bitcast(F32), ALU.subtract)\
                       .then_inc(ol_ready, 1)
            keep_out("a_out", "a_post")
            norm_add("a_mix", "a_mix", "a_post", "mix_post", 0, "a")
            sum_squares("a_fpre")
            feed_forward("a", None)
            keep_ffn("a", "a_fpost")
            norm_add("a_ffn", "a_ffn", "a_fpost", "ffn_post", 0)

            sum_squares("b_pre")
            dve.memset(bz[:, :, 0:LONG_TAPS - 1], 0.0)
            norm_input("b_pre", "b_pre", "mix_pre", KC)
            dve.wait_ge(wt_ready, 1)
            dve.tensor_tensor(wt_lo[:, :], col("w_dw", 0, LONG_TAPS * KC), wt_hi[:, :].bitcast(F32), ALU.subtract)\
               .then_inc(wt_ready, 1)
            for item in TAP_ITEMS:
                c = item[1]
                if item[0] == "gated":
                    dve.wait_ge(b_a, c + 1)
                    dve.wait_ge(b_sig, c + 1)
                    dve.tensor_tensor(bz[:, c, LONG_TAPS - 1:], ba[:, c % 2, 0, :], ba[:, c % 2, 1, :], ALU.mult).then_inc(bz_ready, 1)
                    continue
                if item[0] == "low":
                    i = PE_CHUNKS.index(c)
                    dve.wait_ge(zh_ready, i + 1)
                    dve.tensor_tensor(bz_lo[:, i, :], bz[:, c, :], bz_hi[:, i, :].bitcast(F32), ALU.subtract).then_inc(zl_ready, 1)
                    continue
                tap = item[2]
                w = col("w_dw", tap * KC + c)
                if tap == 0:
                    dve.wait_ge(bz_ready, c + 1)
                    ins = dve.tensor_scalar(by[:, c, :], bz[:, c, 0:T], w, col("b_dw", c), ALU.mult, ALU.add)
                else:
                    dve.wait_ge(taps, TAP_DONE[c, tap - 1])
                    ins = dve.scalar_tensor_tensor(out=by[:, c, :], in0=bz[:, c, tap:tap + T], scalar=w, in1=by[:, c, :],
                                                   op0=ALU.mult, op1=ALU.add)
                ins.then_inc(taps, 1)
            dve.wait_ge(mean_ready, 1)
            for c in range(KC):
                dve.tensor_tensor(by[:, c, :], by[:, c, :], bmean[:, :], ALU.subtract).then_inc(xc_ready, 1)
            dve.wait_ge(rs_ready, RS["b_var"] + 1)
            for c in range(KC + 2):
                if c < KC:
                    dve.tensor_tensor(by[:, c, :], by[:, c, :], rs[:, :], ALU.mult).then_inc(yn_ready, 1)
                if c >= 2:
                    low_of("b_ln", c - 2, by_lo[:, c - 2, :], by_hi[:, c - 2, :])
            keep_out("b_out", "b_post", lambda n: col("b_pw2", n))
            norm_add("b_mix", "b_mix", "b_post", "mix_post", KC, "b")
            sum_squares("b_fpre")
            feed_forward("b", None)
            keep_ffn("b", "b_fpost")
            norm_add("b_ffn", "b_ffn", "b_fpost", "ffn_post", KC)

            l0, l1, e0, e1 = col("lb_logits", 0, KC), col("lb_logits", KC, KC), small[:, 16:24], small[:, 24:32]
            lb, rest, top = small[:, 0:8], small[:, 8:16], small[:, 32:40]
            dve.tensor_tensor(top, l0, l1, ALU.max).then_inc(lb_step, 1)
            dve.wait_ge(lb_step, 1)
            dve.tensor_tensor(e0, l0, top, ALU.subtract).then_inc(lb_step, 1)
            dve.tensor_tensor(e1, l1, top, ALU.subtract).then_inc(lb_step, 1)
            sum_squares("c_pre")
            norm_input("c_pre", "c_pre", "hg_norm", 0)
            dve.wait_ge(lb_step, 4)
            dve.tensor_tensor(top, e0, e1, ALU.add).then_inc(lb_step, 1)
            dve.wait_ge(lb_step, 5)
            dve.reciprocal(top, top).then_inc(lb_step, 1)
            dve.wait_ge(lb_step, 6)
            dve.tensor_tensor(lb, e0, top, ALU.mult).then_inc(lb_step, 1)
            dve.wait_ge(lb_step, 7)
            dve.tensor_scalar(rest, lb, -1.0, 1.0, ALU.mult, ALU.add).then_inc(lb_step, 1)
            dve.wait_ge(lb_step, 8)
            for c in range(KC):
                dve.wait_ge(c_sig, 2 * c + 1)
                dve.tensor_scalar(cf[:, c, :], cf[:, c, :], rest[:, c:c + 1], lb[:, c:c + 1], ALU.mult, ALU.add)\
                   .then_inc(c_qkf, 1)
                dve.wait_ge(c_qkf, 3 * c + 1)
                dve.tensor_scalar(ck[:, c, :], cf[:, c, :], -1.0, 1.0, ALU.mult, ALU.add).then_inc(c_qkf, 1)
                dve.wait_ge(c_sig, 2 * c + 2)
                dve.scalar_tensor_tensor(out=cq[:, c, :], in0=cq[:, c, :], scalar=P ** -0.5, in1=bank[(2 * c + 1) % 4][:, :],
                                         op0=ALU.mult, op1=ALU.mult).then_inc(c_qkf, 1)
            dve.wait_ge(c_qkf, 3 * KC)
            dve.wait_ge(mask_landed, 16)

            def keep_level(g, lv, e):
                dve.wait_ge(level_full, 4 * (8 * g + lv) + e + 1)
                if g and lv == 0:
                    dve.wait_ge(co_full, e + 1)
                if lv == 0:
                    kept = ca[:, e, :].rearrange("p (t s) -> p t s", t=TT)
                    found = bank[4 + e][:, :].rearrange("p (t s) -> p t s", t=TT)
                    mask = ident.unsqueeze(1).to_broadcast([P, TT, P])
                    dve.tensor_tensor(kept, found, mask, ALU.mult).then_inc(level_kept, 1)
                else:
                    dve.wait_ge(level_kept, 4 * (8 * g + lv - 1) + e + 1)
                    mm = LEVELS[lv - 1]
                    nb = P // (2 * mm)
                    kept = ca[:, e, :].rearrange("p (t b two s) -> p t b two s", t=TT, two=2, s=mm)[:, :, :, 1, :]
                    found = bank[4 + e][:, 0:T // 2].rearrange("p (t b s) -> p t b s", t=TT, s=mm)
                    mask = cmask[:, lv - 1, :].bitcast(U32).rearrange("p (b s) -> p b s", s=mm)\
                        .unsqueeze(1).to_broadcast([P, TT, nb, mm])
                    dve.copy_predicated(kept, mask, found).then_inc(level_kept, 1)

            def products(level, hd, e):
                if level == 0:
                    return cf[:, hd, :]
                return (ct1 if level % 2 else ct2)[:, e, 0:T >> level]

            def decay(g, lv, e):
                hd = 4 * g + e
                if lv == 1:
                    dve.tensor_tensor(cq[:, hd, :], cq[:, hd, :], cf[:, hd, :], ALU.mult).then_inc(upd, 1)
                    return
                mm = 1 << (lv - 2)
                nb = T // (2 * mm)
                dve.wait_ge(upd, upd_count(g, lv - 1, e) + (0 if lv == 2 else 1))
                prod = products(lv - 2, hd, e).rearrange("p (b two) -> p b two", two=2)
                q = cq[:, hd, :].rearrange("p (b two s) -> p b two s", two=2, s=mm)[:, :, 1, :]
                k = ck[:, hd, :].rearrange("p (b two s) -> p b two s", two=2, s=mm)[:, :, 0, :]
                even = prod[:, :, 0].unsqueeze(2).to_broadcast([P, nb, mm])
                odd = prod[:, :, 1].unsqueeze(2).to_broadcast([P, nb, mm])
                dve.tensor_tensor(q, q, even, ALU.mult).then_inc(upd, 1)
                dve.tensor_tensor(k, k, odd, ALU.mult).then_inc(upd, 1)
                dve.tensor_tensor(products(lv - 1, hd, e), prod[:, :, 0], prod[:, :, 1], ALU.mult).then_inc(upd, 1)

            def gate_product(n):
                dve.wait_ge(g_sig, n + 1)
                dve.tensor_tensor(cg[:, n, :], cg[:, n, :], bank[n % 2][:, :], ALU.mult).then_inc(g_ready, 1)

            def head_value(hd):
                dve.wait_ge(co_evac, hd + 1)
                dve.wait_ge(g_ready, hd + 1)
                dve.scalar_tensor_tensor(out=cg[:, hd, :], in0=cf[:, hd, :], scalar=col("hg_out_norm"), in1=cg[:, hd, :],
                                         op0=ALU.mult, op1=ALU.mult).then_inc(cg_mul, 1)
                dve.wait_ge(cg_mul, hd + 1)
                dve.wait_ge(rs_ready, RS["c_head"] + hd + 1)
                split_value("c_out", hd, lambda dst: dve.tensor_tensor(dst, cg[:, hd, :], rs[:, :], ALU.mult))

            def head_low(hd):
                low_of("c_out", hd, ccat_lo[:, hd, :], ccat_hi[:, hd, :])

            for g in range(2):
                for lv in range(1, 9):
                    for e in range(4):
                        keep_level(g, lv - 1, e)
                        decay(g, lv, e)
                    if g:
                        if 3 <= lv <= 6:
                            head_low(lv - 3)
                        gate_product(lv - 1)
                        if 2 <= lv <= 5:
                            head_value(lv - 2)
                for e in range(4):
                    dve.wait_ge(far_full, 8 * g + e + 1)
                    decay(g, 9, e)
            for hd in range(4, HG_HEADS):
                head_value(hd)
                if hd > 4:
                    head_low(hd - 1)
            head_low(HG_HEADS - 1)
            add_out("c")
            feed_forward("c", 0)
            add_ffn("c", "d_pre")

            norm_input("d_kv", "d_pre", "kv_norm", 0)
            dve.wait_ge(slot_done, SLOT["d_q"])
            norm_input("d_q", "d_pre", "attn_norm", 0)
            dve.wait_ge(dist_landed, 16)

            def pairs_of(x):
                return x.rearrange("p (n e) -> p n e", e=2)

            def window_max(c):
                top, nm, _, es = window_small(c)
                sink2 = col("sinks", 2 * c, 2).unsqueeze(1).to_broadcast([P, TT, 2])
                if c >= 2:
                    dve.wait_ge(dpt_full, 4 * (c - 1))
                for n in range(TT):
                    lo = 0 if n else P
                    dve.wait_ge(ds_full, 4 * c + 2 * (n // 2) + 2)
                    for e in range(2):
                        slope = 2.0 ** (-8.0 * (2 * c + e + 1) / SWA_HEADS)
                        dve.scalar_tensor_tensor(out=ds_[:, c % 2, n, e, lo:], in0=dist[:, lo:], scalar=-slope,
                                                 in1=window_bank(n, e)[:, lo:], op0=ALU.mult, op1=ALU.add).then_inc(ds_ready, 1)
                for n in range(TT):
                    lo = 0 if n else P
                    dve.wait_ge(ds_ready, 8 * c + 2 * n + 2)
                    dve.tensor_reduce(top[:, 2 * n:2 * n + 2], ds_[:, c % 2, n, :, lo:], AX_X, ALU.max).then_inc(ds_max, 1)
                dve.wait_ge(ds_max, 4 * c + 4)
                dve.tensor_tensor(pairs_of(top), pairs_of(top), sink2, ALU.max).then_inc(ds_m, 1)
                dve.wait_ge(ds_m, c + 1)
                dve.tensor_scalar(nm, top, -1.0, None, ALU.mult).then_inc(ds_nm, 1)
                dve.tensor_tensor(pairs_of(es), sink2, pairs_of(top), ALU.subtract).then_inc(ds_nm, 1)

            def window_probs(c):
                _, _, den, es = window_small(c)
                dve.wait_ge(ds_sink, c + 1)
                dve.wait_ge(ds_exp, 8 * c + 8)
                dve.tensor_tensor(den, den, es, ALU.add).then_inc(ds_den, 1)
                dve.wait_ge(ds_den, 2 * c + 1)
                dve.reciprocal(den, den).then_inc(ds_den, 1)
                dve.wait_ge(ds_den, 2 * c + 2)
                for n in range(TT):
                    lo = 0 if n else P
                    for e in range(2):
                        i, p = 2 * n + e, ds_[:, c % 2, n, e, lo:]
                        dve.tensor_scalar(p, p, den[:, i:i + 1], None, ALU.mult).then_inc(ds_p, 1)

            def window_low(c):
                dve.wait_ge(doh_ready, c + 1)
                dve.tensor_tensor(dcat_lo[:, c, :], bank[2 + c % 2][:, :], dcat_hi[:, c, :].bitcast(F32), ALU.subtract)\
                   .then_inc(dol_ready, 1)

            window_max(0)
            for c in range(KC):
                if c + 1 < KC:
                    window_max(c + 1)
                window_probs(c)
                if c:
                    window_low(c - 1)
            window_low(KC - 1)
            add_out("d")
            feed_forward("d", 1)
            add_ffn("d", "final")
            dve.wait_ge(rs_ready, RS["final"] + 1)
            for c in range(KC):
                dve.scalar_tensor_tensor(out=m[:, c, :], in0=h[:, c, :], scalar=col("final_norm", c), in1=rs[:, :],
                                         op0=ALU.mult, op1=ALU.mult).then_inc(y_ready, 1)


def upd_count(g, lv, e):
    per_group = 4 + 8 * 12
    before = 0 if lv <= 1 else 4 + 12 * (lv - 2)
    return per_group * g + before + (e + 1 if lv == 1 else 3 * e + 2)


def kernel(**inputs):
    import numpy as np
    import concourse.bacc as bacc
    from concourse.bass_utils import run_bass_kernel_spmd

    a = {k: np.ascontiguousarray(v) for k, v in inputs.items()}

    def feature_slots(w):
        return w.reshape(KC, P, -1, P).transpose(2, 1, 0, 3).reshape(-1, P, D)

    def token_slots(w):
        return w.reshape(4, 2, P, -1, 512).transpose(3, 0, 2, 1, 4).reshape(-1, P, D)

    def woven(*parts):
        return np.stack(parts, 1).reshape(-1, P, D)

    def ffn(w_in, w_out):
        back = w_out.reshape(HALF, 2, P, 2, 512).transpose(3, 0, 2, 1, 4).reshape(-1, P, D)
        return [woven(feature_slots(w_in[:, :FF]), feature_slots(w_in[:, FF:])), back]

    w_in, w_hg, w_kv = a["w_in"][0], a["hg_w_in_2"][0], a["w_kv_2"]
    w_pw1 = a["w_pw1"][0]
    part = [w_in[:, 512 * i:512 * (i + 1)] for i in range(6)]
    hg = [w_hg[:, D * i:D * (i + 1)] for i in range(4)]
    slots = [feature_slots(part[3]), feature_slots(part[4]), token_slots(part[5]),
             woven(feature_slots(part[1]), feature_slots(part[2]), feature_slots(part[0])),
             feature_slots(a["w_out"][0]), *ffn(a["w_ffn_in"][0], a["w_ffn_out"][0]),
             woven(feature_slots(w_pw1[:, :D]), feature_slots(w_pw1[:, D:])), feature_slots(a["w_pw2"][0]),
             *ffn(a["w_ffn_in"][1], a["w_ffn_out"][1]),
             woven(feature_slots(hg[1]), feature_slots(hg[0])), token_slots(hg[2]), feature_slots(hg[3]),
             feature_slots(a["hg_w_out_2"][0]), *ffn(a["ffn_w_up_2"][0], a["ffn_w_down_2"][0]),
             feature_slots(w_kv), feature_slots(a["attn_w_q_2"][0]), feature_slots(a["attn_w_o_2"][0]),
             *ffn(a["ffn_w_up_2"][1], a["ffn_w_down_2"][1])]
    weights = np.concatenate(slots)
    assert weights.shape == (N_SLOTS, P, D)

    def columns(v):
        return v.reshape(-1, P).T

    forget = w_in[:, 3072:].reshape(KC, P, FOX_HEADS).transpose(1, 0, 2).reshape(P, -1)
    b_forget = np.zeros((P, 1), np.float32)
    b_forget[:FOX_HEADS, 0] = a["b_forget"][0]
    vectors = np.concatenate([
        columns(a["norm_mix_pre"]), columns(a["norm_mix_post"]), columns(a["norm_ffn_pre"]), columns(a["norm_ffn_post"]),
        forget, b_forget, columns(a["w_short_conv"][0]), columns(a["b_pw1"]), columns(a["w_dw"][0]), columns(a["b_dw"]),
        columns(a["ln_g"]), columns(a["ln_b"]), columns(a["b_pw2"]), columns(a["hg_norm_2"]), columns(a["hg_lb_logits_2"]),
        columns(a["hg_out_norm_2"]), columns(a["kv_norm_2"]), columns(a["attn_norm_2"]),
        np.broadcast_to(a["attn_sinks_2"], (P, SWA_HEADS)), columns(a["ffn_norm_2"]), columns(a["ffn_conv_w_2"]),
        columns(a["ffn_conv_b_2"]), columns(a["final_norm_2"])], 1)
    assert vectors.shape == (P, N_VEC)

    row, colm = np.arange(P)[:, None], np.arange(P)[None, :]
    far = row + WINDOW - np.arange(2 * WINDOW)[None, :]
    squares = np.concatenate([np.eye(P), np.where(colm <= row, 0.0, NEVER),
                              np.where((far >= 0) & (far < WINDOW), far, -NEVER)], 1).astype(np.float32)
    select = np.zeros((FOX_HEADS, FOX_HEADS, P), np.float32)
    for hd in range(FOX_HEADS):
        select[hd, hd] = -1.0
    second = [np.arange(P).reshape(-1, 2, n)[:, 1].reshape(1, -1) for n in LEVELS]
    masks = np.stack([(row // (2 * n) == q // (2 * n)) & (row // n % 2 == 0) for n, q in zip(LEVELS, second)], 1)
    arrays = {
        "weights": weights, "vectors": vectors, "squares": squares, "select": select, "masks": masks.astype(np.float32),
        "x_t": a["x"][0].T.reshape(KC, P, T).transpose(1, 0, 2),
    }
    nc = bacc.Bacc("TRN2", target_bir_lowering=False, num_devices=1)
    args = []
    for name, v in arrays.items():
        arrays[name] = v = np.ascontiguousarray(v)
        args.append(nc.dram_tensor(f"{name}_dram", v.shape, mybir.dt.from_np(v.dtype), kind="ExternalInput").ap())
    args.append(nc.dram_tensor("out_dram", (P, KC, T), F32, kind="ExternalOutput").ap())
    build(nc, *args)
    r = run_bass_kernel_spmd(nc, [{f"{k}_dram": v for k, v in arrays.items()}], core_ids=[0])
    out = r.results[0]["out_dram"]
    return np.ascontiguousarray(out.transpose(1, 0, 2).reshape(D, T).T)[None]
```

```python
from contextlib import ExitStack

import concourse.bass as bass
from concourse import mybir

F32 = mybir.dt.float32
F32R = mybir.dt.float32r
U32 = mybir.dt.uint32
ALU = mybir.AluOpType
ACT = mybir.ActivationFunctionType
AX_X = mybir.AxisListType.X

P = 128
T = 512
D = 1024
KC = D // P
TT = T // P
FF = 2816
FC = FF // P
FOX_HEADS, FOX_DIM = 8, 64
HG_HEADS = 8
SWA_HEADS, SWA_DIM, WINDOW = 16, 64, 128
SHORT_TAPS, LONG_TAPS, FFN_TAPS = 3, 31, 3
RMS_EPS, LN_EPS = 1e-6, 1e-5
LOW_ROW = 32
NEVER = -1e30
LEVELS = (1, 2, 4, 8, 16, 32, 64)
RING = 4
AHEAD = 3
HALF = FC // 2
DVE_CHUNKS, POOL_CHUNK, PE_CHUNKS = (0, 2, 3, 4, 5), 1, (6, 7)
SHARED, SHARED_FROM = 5, 23
PROD_SLOT = 6
PROD_TAPS = 2 * (2 * KC - PROD_SLOT)
DVE_LAST, POOL_LAST = (0, 1, 3, 4, 6), (2, 5, 7)
FIRST_TAPS = 3
DVE_SLOTS = 2
DVE_NORMS = 2
CONV_ORDER = (0, 2, 3, 4, 6, 1, 7, 5)

SLOT_PARTS = (
    ("a_q", 4), ("a_k", 4), ("a_v", 4), ("a_conv", 12), ("a_out", 8), ("a_ffn_in", 2 * FC), ("a_ffn_out", FC),
    ("b_in", 16), ("b_out", 8), ("b_ffn_in", 2 * FC), ("b_ffn_out", FC),
    ("c_fq", 16), ("c_i", 8), ("c_g", 8), ("c_out", 8), ("c_ffn_in", 2 * FC), ("c_ffn_out", FC),
    ("d_kv", 2), ("d_q", 8), ("d_out", 8), ("d_ffn_in", 2 * FC), ("d_ffn_out", FC),
)


def starts(parts):
    at, out = 0, {}
    for name, n in parts:
        out[name] = at
        at += n
    return out, at


SLOT, N_SLOTS = starts(SLOT_PARTS)

VEC_PARTS = (
    ("mix_pre", 16), ("mix_post", 16), ("ffn_pre", 16), ("ffn_post", 16),
    ("w_forget", KC * FOX_HEADS), ("b_forget", 1), ("short_conv", SHORT_TAPS * 4),
    ("b_pw1", 16), ("w_dw", LONG_TAPS * KC), ("b_dw", KC), ("ln_g", KC), ("ln_b", KC), ("b_pw2", KC),
    ("hg_norm", KC), ("lb_logits", 2 * KC), ("hg_out_norm", 1), ("kv_norm", KC), ("attn_norm", KC),
    ("sinks", SWA_HEADS), ("ffn_norm_2", 2 * KC), ("ffn_conv_w", 2 * FFN_TAPS * FC), ("ffn_conv_b", 2 * FC),
    ("final_norm", KC),
)
VEC, N_VEC = starts(VEC_PARTS)

STATS = ("a_pre", "a_post", "a_fpre", "a_fpost", "b_pre", "b_post", "b_fpre", "b_fpost",
         "c_pre", "c_fpre", "d_pre", "d_fpre", "final")
DIRECT = ("b_var", "c_head")
ORDER = STATS[:5] + ("b_var",) + STATS[5:9] + ("c_head",) + STATS[9:]
SQ, _ = starts([(s, KC) for s in ORDER])
LATE = ("a_post", "a_fpost", "b_post", "b_fpost", "final")
ACC, _ = starts([(s, KC - 2 if s in LATE else KC - 1) for s in STATS])
POST, _ = starts([(s, DVE_NORMS) for s in LATE[:4]])
SUM, _ = starts([(s, 1) for s in STATS])
USED, _ = starts([(s, KC) for s in DIRECT])
RS, _ = starts([(s, HG_HEADS if s == "c_head" else 1) for s in ORDER])
SPLITS = ("a_pre", "a_gate", "a_fpre", "b_pre", "b_ln", "b_fpre", "c_pre", "c_out", "c_fpre", "d_kv", "d_q", "d_fpre")
SPLIT, _ = starts([(s, 4 if s == "a_gate" else KC) for s in SPLITS])
VALUE, _ = starts([("a_gate", 4), ("b_ln", KC), ("c_out", KC)])
TOK, _ = starts([(s, 1) for s in ("a_pre", "c_pre")])
RESID, _ = starts([(s, KC) for s in ("a_mix", "a_ffn", "b_mix", "b_ffn", "c_mix", "c_ffn", "d_mix", "d_ffn")])
NORMED, _ = starts([(s, KC - DVE_NORMS) for s in ("a_mix", "a_ffn", "b_mix", "b_ffn")])
MADE, _ = starts([(s, KC) for s in ("a_mix", "a_ffn", "b_mix", "b_ffn")])
FULL, _ = starts([(s, 6) for s in "abcd"])
HID, _ = starts([(s, FC) for s in "abcd"])
CONVG, _ = starts([(s, 2 * FC) for s in "cd"])


def tap_order():
    items, done, made = [], {}, 0
    left = {c: 0 for c in DVE_CHUNKS}

    def taps(n):
        for _ in range(n):
            live = [c for c in DVE_CHUNKS if c < made and left[c] < (SHARED_FROM if c == SHARED else LONG_TAPS)][:2]
            if live:
                c = min(live, key=lambda c: done.get((c, left[c] - 1), 0))
                items.append(("tap", c, left[c]))
                done[c, left[c]] = len(done) + 1
                left[c] += 1

    for n in range(2 * KC):
        per_slot = 0 if n < FIRST_TAPS else 6 + n % 2
        items.append(("slot", n))
        taps(min(per_slot, 2))
        if n % 2:
            items.append(("gated", n // 2))
            made += 1
        taps(per_slot - 2)
    taps(KC * LONG_TAPS)
    for c in PE_CHUNKS:
        last, n = (("slot", 2 * c + 2), 2) if c < KC - 1 else (("gated", c), 12)
        items.insert(items.index(last) + n, ("low", c))
    return items, done


def build(nc, weights, vectors, squares, select_d, masks_d, x_t, out_t):
    with ExitStack() as ctx:
        def sb(name, shape, dt, where=ctx):
            return where.enter_context(nc.sbuf_tensor(name, shape, dt))

        def sem(name):
            return ctx.enter_context(nc.semaphore(name))

        h = sb("h", [P, KC, T], F32)
        with ExitStack() as one:
            m = sb("m", [P, KC, T], F32, one)
        u_hi = sb("u_hi", [P, KC, T], F32R)
        u_lo = sb("u_lo", [P, KC, T], F32R)
        with ExitStack() as landing:
            raw = sb("raw", [P, RING, D], F32, landing)
        w_lo = sb("w_lo", [P, RING, D], F32R)
        w_hi = sb("w_hi", [P, RING, D], F32R)
        sq = sb("sq", [P, 2, T], F32)
        ut = sb("ut", [P, 2, T], F32)
        acc = sb("acc", [P, T], F32)
        rs = sb("rs", [P, T], F32)
        vec = sb("vec", [P, N_VEC], F32)
        identity = sb("identity", [P, P], F32)
        ident = identity[:, :]
        ones = sb("ones", [P, P], F32)
        small = sb("small", [P, 64], F32)
        spare = sb("spare", [P, 16], F32)
        rs_tok = sb("rs_tok", [P, TT], F32)
        eps = sb("eps", [P, 2], F32)

        with ExitStack() as fox:
            aq_hi = sb("aq_hi", [P, 4, T], F32R, fox)
            aq_lo = sb("aq_lo", [P, 4, T], F32R, fox)
            ak_hi = sb("ak_hi", [P, 4, T], F32R, fox)
            ak_lo = sb("ak_lo", [P, 4, T], F32R, fox)
            av = sb("av", [P, TT, 512], F32, fox)
            az = sb("az", [P, T + SHORT_TAPS - 1], F32, fox)
            agc = sb("agc", [P, T], F32, fox)
            ay = sb("ay", [P, T], F32, fox)
            ap = sb("ap", [P, TT, T], F32, fox)
            with ExitStack() as early:
                wf_hi = sb("wf_hi", [P, KC, P // FOX_HEADS, FOX_HEADS], F32R, early)
                wf_lo = sb("wf_lo", [P, KC, P // FOX_HEADS, FOX_HEADS], F32R, early)
            apt = sb("apt", [P, TT, T], F32, fox)
            ac = sb("ac", [FOX_HEADS, T], F32, fox)
            ac2 = sb("ac2", [P, T], F32R, fox)
            causal = sb("causal", [P, P], F32R, fox)
            ident_r = sb("ident_r", [P, P], F32R, fox)
            select = sb("select", [P, FOX_HEADS, P], F32R, fox)
            acat_hi = sb("acat_hi", [P, KC, T], F32R, fox)
            acat_lo = sb("acat_lo", [P, KC, T], F32R, fox)
        with ExitStack() as conf:
            bz = sb("bz", [P, KC, T + LONG_TAPS - 1], F32, conf)
            ba = sb("ba", [P, 2, 2, T], F32, conf)
            bz_hi = sb("bz_hi", [P, len(PE_CHUNKS), T + LONG_TAPS - 1], F32R, conf)
            bz_lo = sb("bz_lo", [P, len(PE_CHUNKS), T + LONG_TAPS - 1], F32R, conf)
            dg_hi = sb("dg_hi", [P, 4, P], F32R, conf)
            dg_lo = sb("dg_lo", [P, 4, P], F32R, conf)
            wt_hi = sb("wt_hi", [P, LONG_TAPS * KC], F32R, conf)
            wt_lo = sb("wt_lo", [P, LONG_TAPS * KC], F32, conf)
            by = sb("by", [P, KC, T], F32, conf)
            bprod = sb("bprod", [P, 2, T], F32, conf)
            bown = sb("bown", [P, T], F32, conf)
            bpart = sb("bpart", [P, T], F32, conf)
            bmean = sb("bmean", [P, T], F32, conf)
            by_hi = sb("by_hi", [P, KC, T], F32R, conf)
            by_lo = sb("by_lo", [P, KC, T], F32R, conf)
        with ExitStack() as hgrn:
            with ExitStack() as qk:
                cq = sb("cq", [P, HG_HEADS, T], F32, qk)
                ck = sb("ck", [P, HG_HEADS, T], F32, qk)
            ccat_hi = sb("ccat_hi", [P, KC, T], F32R, hgrn)
            ccat_lo = sb("ccat_lo", [P, KC, T], F32R, hgrn)
            cf = sb("cf", [P, HG_HEADS, T], F32, hgrn)
            cv = sb("cv", [P, TT, D], F32, hgrn)
            cg = sb("cg", [P, KC, T], F32, hgrn)
            ca = sb("ca", [P, 4, T], F32, hgrn)
            ct1 = sb("ct1", [P, 4, T // 2], F32, hgrn)
            ct2 = sb("ct2", [P, 4, T // 4], F32, hgrn)
            rs_head = sb("rs_head", [P, T], F32, hgrn)
            cmask = sb("cmask", [P, len(LEVELS), P // 2], F32, hgrn)
        with ExitStack() as swa:
            dq = sb("dq", [P, 2, 2, T], F32R, swa)
            dk_hi = sb("dk_hi", [P, 2, T], F32R, swa)
            dk_lo = sb("dk_lo", [P, 2, T], F32R, swa)
            dv = sb("dv", [P, TT, P], F32, swa)
            ds_ = sb("ds", [P, 2, TT, 2, 2 * WINDOW], F32, swa)
            dist = sb("dist", [P, 2 * WINDOW], F32, swa)
            dpt = sb("dpt", [P, TT, T], F32, swa)
            dcat_hi = sb("dcat_hi", [P, KC, T], F32R, swa)
            dcat_lo = sb("dcat_lo", [P, KC, T], F32R, swa)
        with ExitStack() as ffn:
            hid_hi = sb("hid_hi", [P, FC, T], F32R, ffn)
            hid_lo = sb("hid_lo", [P, FC, T], F32R, ffn)
            gconv = sb("gconv", [P, 2, T], F32, ffn)

        bank = [ctx.enter_context(nc.psum_tensor(f"bank{i}", [P, T], F32)) for i in range(8)]
        STAT, TOK_STAT = bank[4], bank[5]

        raw_landed = [sem(f"raw_landed{j}") for j in range(RING)]
        hi_ready, w_ready, slot_done = sem("hi_ready"), sem("w_ready"), sem("slot_done")
        x_landed = [sem(f"x_landed{c}") for c in range(KC)]
        gain_landed, vec_landed, consts_landed, mask_landed, dist_landed = (sem(n) for n in (
            "gain_landed", "vec_landed", "consts_landed", "mask_landed", "dist_landed"))
        acc_ready, sum_full, scaled_ready, t2_ready = sem("acc_ready"), sem("sum_full"), sem("scaled_ready"), sem("t2_ready")
        wf_ready, wt_ready, zh_ready, zl_ready, dg_ready, dg_used, tap_full, tap_evac = (sem(n) for n in (
            "wf_ready", "wt_ready", "zh_ready", "zl_ready", "dg_ready", "dg_used", "tap_full", "tap_evac"))
        consts_made = sem("consts_made")
        sq_ready, sq_used, rs_ln, rs_ready = sem("sq_ready"), sem("sq_used"), sem("rs_ln"), sem("rs_ready")
        ut_ready, uh_ready, u_ready = sem("ut_ready"), sem("uh_ready"), sem("u_ready")
        made_ready, normed_0, normed, h_ready = (sem(n) for n in ("made_ready", "normed_0", "normed", "h_ready"))
        out_full = sem("out_full")
        gate_ready, ht_ready, hh_ready, hid_ready = sem("gate_ready"), sem("ht_ready"), sem("hh_ready"), sem("hid_ready")
        gconv0_ready, gconv_ready = sem("gconv0_ready"), sem("gconv_ready")
        scaled_out, y_ready, yp_ready, y_stored = (sem(n) for n in ("scaled_out", "y_ready", "yp_ready", "y_stored"))
        a_evac, f_full, f_read, f_exp, f_ln, logf, c_ready = (sem(n) for n in (
            "a_evac", "f_full", "f_read", "f_exp", "f_ln", "logf", "c_ready"))
        gc_evac, gc_ready, z_ready, sconv = sem("gc_evac"), sem("gc_ready"), sem("z_ready"), sem("sconv")
        qk_evac, qkh_ready, qkl_ready, f_evac, c_high, c_low, zeroed, rounded = (sem(n) for n in ("qk_evac", "qkh_ready", "qkl_ready", "f_evac", "c_high", "c_low", "zeroed", "rounded"))
        tok_full, tok_ln, tok_ready = sem("tok_full"), sem("tok_ln"), sem("tok_ready")
        scores_ready, max_ready, exp_ready, inv_ready, p_ready = (sem(n) for n in (
            "scores_ready", "max_ready", "exp_ready", "inv_ready", "p_ready"))
        pt_full, pt_ready, o_ready, oh_ready, ol_ready = (sem(n) for n in (
            "pt_full", "pt_ready", "o_ready", "oh_ready", "ol_ready"))
        b_evac, b_sig, bz_ready, taps, pool_taps, pool_prod, prod_ready, shared_taps, mean_full, mean_ready, xc_ready, yn_ready = (sem(n) for n in (
            "b_evac", "b_sig", "bz_ready", "taps", "pool_taps", "pool_prod", "prod_ready", "shared_taps", "mean_full", "mean_ready", "xc_ready", "yn_ready"))
        lb_step, c_evac, c_sig, c_qkf, i_evac, g_evac, g_ready = (sem(n) for n in (
            "lb_step", "c_evac", "c_sig", "c_qkf", "i_evac", "g_evac", "g_ready"))
        level_full, level_kept, upd, pv_part, far_full, far_kept, co_full, co_evac, cg_mul = (sem(n) for n in (
            "level_full", "level_kept", "upd", "pv_part", "far_full", "far_kept", "co_full", "co_evac", "cg_mul"))
        d_kv_evac, d_vt_full, d_kv_ready, dk_low, d_q_evac, dq_high, dq_low = (sem(n) for n in (
            "d_kv_evac", "d_vt_full", "d_kv_ready", "dk_low", "d_q_evac", "dq_high", "dq_low"))
        ds_full, ds_ready, ds_max, ds_m, ds_nm, ds_exp, ds_sink, ds_den, ds_p = (sem(n) for n in (
            "ds_full", "ds_ready", "ds_max", "ds_m", "ds_nm", "ds_exp", "ds_sink", "ds_den", "ds_p"))
        dpt_full, dpt_ready, do_ready, doh_ready, dol_ready = (sem(n) for n in (
            "dpt_full", "dpt_ready", "do_ready", "doh_ready", "dol_ready"))

        def col(name, i=0, n=1):
            return vec[:, VEC[name] + i:VEC[name] + i + n]

        def window_bank(n, e):
            return bank[4 + 2 * e + n // 2][:, 2 * WINDOW * (n % 2):2 * WINDOW * (n % 2 + 1)]

        def rows_of(e):
            return slice(64 * e, 64 * e + 64)

        def window_small(c):
            at = 32 * (c % 2)
            return tuple(small[:, at + 8 * i:at + 8 * i + 8] for i in range(4))

        def pre_gain(split, c):
            name, at = {"a_pre": ("mix_pre", 0), "b_pre": ("mix_pre", KC), "c_pre": ("hg_norm", 0), "d_kv": ("kv_norm", 0),
                        "d_q": ("attn_norm", 0), "a_fpre": ("ffn_pre", 0), "b_fpre": ("ffn_pre", KC),
                        "c_fpre": ("ffn_norm_2", 0), "d_fpre": ("ffn_norm_2", KC)}[split]
            return col(name, at + c)

        wf = vec[:, VEC["w_forget"]:VEC["w_forget"] + KC * FOX_HEADS].rearrange("p (k n) -> p k n", k=KC)\
            .unsqueeze(2).to_broadcast([P, KC, P // FOX_HEADS, FOX_HEADS])
        select_raw = ap[:, 2:4, :].rearrange("p a (b n) -> p (a b) n", n=P)
        TAP_ITEMS, TAP_DONE = tap_order()

        def after(eng, s, n):
            if not (isinstance(n, int) and n <= 0):
                eng.wait_ge(s, n)

        def ffn_full(eng, l, n):
            half, c = n // 4, n % 4
            if c < 3:
                eng.wait_ge(out_full, FULL[l] + 3 * half + c + 1)
            else:
                eng.wait_ge(slot_done, SLOT[f"{l}_ffn_out"] + HALF * (half + 1))
            return bank[4 * (1 - half) + c]

        block = ctx.enter_context(nc.Block())

        @block.sync
        def _(sp):
            def load(s, j, n):
                sp.dma_start(raw[:, j, :], weights[n]).then_inc(raw_landed[j], 16)

            def load_x(c):
                sp.dma_start(h[:, c, :], x_t[:, c, :]).then_inc(x_landed[c], 16)

            sp.dma_start(vec[:, 0:KC], vectors[:, 0:KC]).then_inc(gain_landed, 16)
            load(0, 0, 0)
            load_x(0)
            load(1, 1, 1)
            for c in range(1, KC):
                load_x(c)
            load(2, 2, 2)
            sp.dma_start(vec[:, KC:], vectors[:, KC:]).then_inc(vec_landed, 16)
            load(3, 3, 3)
            sp.dma_start(identity[:, :], squares[:, 0:P]).then_inc(consts_landed, 16)
            sp.dma_start(ap[:, 0, 0:P], squares[:, P:2 * P]).then_inc(consts_landed, 16)
            sp.dma_start(select_raw, select_d).then_inc(consts_landed, 16)
            with sp.Fori(1, N_SLOTS // RING) as i:
                for j in range(RING):
                    sp.wait_ge(slot_done, RING * (i - 1) + j + 1)
                    sp.dma_start(raw[:, j, :], weights[bass.ds(RING * i + j, 1)].rearrange("o p n -> p (o n)"))\
                      .then_inc(raw_landed[j], 16)
            for n in range(N_SLOTS - N_SLOTS % RING, N_SLOTS):
                sp.wait_ge(slot_done, n - RING + 1)
                load(n, n % RING, n)
            for c in range(KC):
                if c in POOL_LAST:
                    sp.wait_ge(yp_ready, POOL_LAST.index(c) + 1)
                else:
                    sp.wait_ge(y_ready, DVE_LAST.index(c) + 1)
                sp.dma_start(out_t[:, c, :], m[:, c, :]).then_inc(y_stored, 16)
            sp.wait_ge(y_stored, 16 * KC)

        @block.gpsimd
        def _(pool):
            def low_part(s, j):
                pool.wait_ge(hi_ready, s + 1)
                pool.tensor_tensor(w_lo[:, j, :], raw[:, j, :], w_hi[:, j, :].bitcast(F32), ALU.subtract)\
                    .then_inc(w_ready, 1)

            def low_parts(a, b):
                if b - a >= RING:
                    with pool.Fori(0, (b - a) // RING) as i:
                        for n in range(RING):
                            low_part(RING * i + a + n, (a + n) % RING)
                for s in range(b - (b - a) % RING, b):
                    low_part(s, s % RING)

            def norm_output(stat):
                pool.wait_ge(rs_ready, RS[stat] + 1)
                pool.wait_ge(made_ready, MADE[f"{stat[0]}_{'ffn' if 'f' in stat else 'mix'}"] + KC)
                for c in range(DVE_NORMS, KC):
                    pool.tensor_tensor(m[:, c, :], m[:, c, :], rs[:, :], ALU.mult).then_inc(normed, 1)

            def add_product(tap):
                c = POOL_CHUNK
                pool.wait_ge(prod_ready, tap + 1)
                after(pool, pool_taps, tap - 1)
                pool.tensor_tensor(by[:, c, :], by[:, c, :], bprod[:, tap % 2, :], ALU.add).then_inc(pool_taps, 1)

            own = []

            def own_tap(c, tap, to, count, n):
                w = col("w_dw", tap * KC + c).to_broadcast([P, T])
                if n == 0:
                    pool.wait_ge(bz_ready, c + 1)
                    pool.tensor_tensor(to, bz[:, c, tap:tap + T], w, ALU.mult).then_inc(count, 1)
                    return
                pool.wait_ge(count, n)
                pool.tensor_tensor(bown[:, :], bz[:, c, tap:tap + T], w, ALU.mult).then_inc(pool_prod, 1)
                own.append(tap)
                pool.wait_ge(pool_prod, len(own))
                pool.tensor_tensor(to, to, bown[:, :], ALU.add).then_inc(count, 1)

            pool.wait_ge(w_ready, DVE_SLOTS)
            low_parts(DVE_SLOTS, SLOT["a_ffn_in"] + AHEAD - 1)
            norm_output("a_post")
            low_parts(SLOT["a_ffn_in"] + AHEAD - 1, SLOT["b_in"] + AHEAD - 1)
            norm_output("a_fpost")
            low_parts(SLOT["b_in"] + AHEAD - 1, SLOT["b_in"] + AHEAD)
            for n in range(2 * KC):
                s = SLOT["b_in"] + AHEAD + n
                low_part(s, s % RING)
                if n >= PROD_SLOT:
                    first = 2 * (n - PROD_SLOT) + 1
                    add_product(first)
                    add_product(first + 1)
            for tap in range(PROD_TAPS + 1, LONG_TAPS):
                own_tap(POOL_CHUNK, tap, by[:, POOL_CHUNK, :], pool_taps, tap - 1)
            pool.wait_ge(pool_taps, LONG_TAPS - 1)
            for n, tap in enumerate(range(SHARED_FROM, LONG_TAPS)):
                own_tap(SHARED, tap, bpart[:, :], shared_taps, n)
            low_parts(SLOT["b_out"] + AHEAD, SLOT["b_ffn_in"] + AHEAD - 1)
            norm_output("b_post")
            low_parts(SLOT["b_ffn_in"] + AHEAD - 1, SLOT["c_fq"] + AHEAD - 1)
            norm_output("b_fpost")
            low_parts(SLOT["c_fq"] + AHEAD - 1, N_SLOTS)
            pool.wait_ge(rs_ready, RS["final"] + 1)
            for c in POOL_LAST:
                pool.wait_ge(scaled_out, c + 1)
                pool.tensor_tensor(m[:, c, :], m[:, c, :], rs[:, :], ALU.mult).then_inc(yp_ready, 1)

        @block.tensor
        def _(pe):
            def product(out, wh, wl, xh, xl, start, stop):
                pe.matmul(out, wh, xh, start=start, stop=False)
                pe.matmul(out, wh, xl, start=False, stop=False)
                return pe.matmul(out, wl, xh, start=False, stop=stop)

            def weight(part, j, k, n=P):
                return part[:, j, k * n:(k + 1) * n]

            def chunk(s, i, out, xh, xl, ready=None, ks=range(KC)):
                j = s % RING
                pe.wait_ge(w_ready, s + RING * i + 1)
                for k in ks:
                    if ready:
                        ready(k)
                    last = product(out, weight(w_hi, j, k), weight(w_lo, j, k), xh[:, k, :], xl[:, k, :],
                                   k == 0, k == KC - 1)
                if ks[-1] == KC - 1:
                    last.then_inc(slot_done, 1)

            def two_chunks(s, outs, xh, xl, ready, ready_hi=None):
                pe.wait_ge(w_ready, s + 2)
                for k in range(KC):
                    if k == 0 and ready_hi:
                        ready_hi()
                        for w in (w_hi, w_lo):
                            for e in range(2):
                                pe.matmul(outs[e][:, :], weight(w, (s + e) % RING, 0), xh[:, 0, :], start=w is w_hi, stop=False)
                        ready(0)
                        for e in range(2):
                            pe.matmul(outs[e][:, :], weight(w_hi, (s + e) % RING, 0), xl[:, 0, :], start=False, stop=False)
                        continue
                    ready(k)
                    for e in range(2):
                        j = (s + e) % RING
                        last = product(outs[e][:, :], weight(w_hi, j, k), weight(w_lo, j, k), xh[:, k, :], xl[:, k, :],
                                       k == 0, k == KC - 1)
                        if k == KC - 1:
                            last.then_inc(slot_done, 1)

            def token_major(s, banks, first, final, free=None):
                j = s % RING
                pe.wait_ge(w_ready, s + 1)
                for t in range(TT):
                    if free:
                        free(t)
                    for k in range(2):
                        xs = slice(t * P, (t + 1) * P)
                        kk = 2 * first + k
                        last = product(banks[t][:, :], u_hi[:, kk, xs], u_lo[:, kk, xs],
                                       weight(w_hi, j, k, 512), weight(w_lo, j, k, 512),
                                       kk == 0, final and k == 1)
                last.then_inc(slot_done, 1)

            def mean_square(name):
                if name in LATE:
                    pe.wait_ge(acc_ready, ACC[name] + KC - 2)
                    pe.matmul(STAT[:, :], ones[:, :], acc[:, :], start=True, stop=False)
                    pe.wait_ge(sq_ready, SQ[name] + KC)
                    pe.matmul(STAT[:, :], ones[:, :], sq[:, (KC - 1) % 2, :], start=False, stop=True).then_inc(sum_full, 1)
                else:
                    pe.wait_ge(acc_ready, ACC[name] + KC - 1)
                    pe.matmul(STAT[:, :], ones[:, :], acc[:, :], start=True, stop=True).then_inc(sum_full, 1)
                if name in TOK:
                    for t in range(TT):
                        last = pe.matmul(TOK_STAT[:, t:t + 1], acc[:, t * P:(t + 1) * P], ones[:, 0:1], start=True, stop=True)
                    last.then_inc(tok_full, 1)

            def normed_input(name):
                return lambda k: pe.wait_ge(u_ready, SPLIT[name] + k + 1)

            def high_input(name):
                return lambda: pe.wait_ge(uh_ready, SPLIT[name] + 1)

            def keep_warm(s, n):
                pe.wait_ge(w_ready, s + 1)
                for _ in range(n):
                    pe.matmul(bank[7][:, :], w_hi[:, s % RING, 0:P], w_hi[:, s % RING, 0:T], start=True, stop=True)

            def post_norm(stat, s):
                mean_square(stat)
                pe.wait_ge(rs_ln, RS[stat] + 1)
                keep_warm(s, 6)
                pe.wait_ge(rs_ready, RS[stat] + 1)
                keep_warm(s, 4)

            def out_chunks(part, xh, xl, free, ready, ready_hi=None):
                s = SLOT[part]
                two_chunks(s, bank[0:2], xh, xl, ready, ready_hi)
                for n in range(2, KC):
                    free(n)
                    chunk(s + n, 0, bank[n % 4][:, :], xh, xl)

            def consumed(made):
                def free(n):
                    if n >= 4:
                        pe.wait_ge(made_ready, MADE[made] + n - 3)
                return free

            def added(resid):
                def free(n):
                    if n >= 4:
                        pe.wait_ge(h_ready, RESID[resid] + n - 3)
                return free

            def feed_forward(l):
                s0, s1 = SLOT[f"{l}_ffn_in"], SLOT[f"{l}_ffn_out"]

                def gates(i, b):
                    after(pe, scaled_ready, HID[l] + 2 * i + b - 1 if not isinstance(i, int) or i else 0)
                    chunk(s0 + 2 * b, i, bank[2 * b][:, :], u_hi, u_lo)

                def values(i, b):
                    after(pe, ht_ready, HID[l] + 2 * i + b - 1 if not isinstance(i, int) or i else 0)
                    chunk(s0 + 2 * b + 1, i, bank[2 * b + 1][:, :], u_hi, u_lo)

                two_chunks(s0, bank[0:2], u_hi, u_lo, normed_input(f"{l}_fpre"), high_input(f"{l}_fpre"))
                gates(0, 1)
                mean_square(f"{l}_fpre")
                values(0, 1)
                with pe.Fori(1, FC // 2) as i:
                    for b in range(2):
                        gates(i, b)
                        values(i, b)

                def back(half, n, i=0, first=False, final=False):
                    s = s1 + HALF * half + n
                    j = s % RING
                    pe.wait_ge(w_ready, s + RING * i + 1)
                    if half == 0:
                        pe.wait_ge(hid_ready, HID[l] + 2 * n + 2 * RING * i + 2)
                    for c in range(4):
                        for kk in range(2):
                            xs = [x[:, 2 * n + kk, :] if isinstance(i, int) else
                                  x[:, bass.ds(2 * RING * i + 2 * n + kk, 1), :].rearrange("p o t -> p (o t)")
                                  for x in (hid_hi, hid_lo)]
                            ws = [w[:, j, 512 * kk + P * c:512 * kk + P * (c + 1)] for w in (w_hi, w_lo)]
                            last = product(bank[4 * (1 - half) + c][:, :], *ws, *xs, first and kk == 0, final and kk == 1)
                        if final and c < 3:
                            last.then_inc(out_full, 1)
                    last.then_inc(slot_done, 1)

                for half in range(2):
                    if half:
                        pe.wait_ge(ht_ready, HID[l] + FC)
                    back(half, 0, first=True)
                    with pe.Fori(0, 2) as i:
                        for n in range(1, 1 + RING):
                            back(half, n, i)
                    back(half, 9)
                    back(half, 10, final=True)

            pe.wait_ge(consts_made, 2)

            two_chunks(0, bank[0:2], u_hi, u_lo, normed_input("a_pre"), high_input("a_pre"))
            for n in range(2, 8):
                if n >= 4:
                    pe.wait_ge(qk_evac, n - 3)
                chunk(n, 0, bank[n % 4][:, :], u_hi, u_lo)
                if n == 2:
                    mean_square("a_pre")
            pe.wait_ge(wf_ready, 2)
            pe.wait_ge(rs_ready, RS["a_pre"] + 1)
            for k in range(KC):
                wide = [w[:, k, :, :].rearrange("p r n -> p (r n)") for w in (wf_hi, wf_lo)]
                last = product(bank[4][:, :], *wide, u_hi[:, k, :], u_lo[:, k, :], k == 0, k == KC - 1)
            last.then_inc(f_full, 1)
            for n in range(4):
                token_major(SLOT["a_v"] + n, bank, n, n == 3, (lambda t: pe.wait_ge(qk_evac, 5 + t)) if n == 0 else None)
            pe.wait_ge(consts_landed, 48)
            pe.wait_ge(rounded, 3)

            def scores(hd):
                r, c = slice(64 * (hd % 2), 64 * (hd % 2) + 64), hd // 2
                for qb in range(TT):
                    w = (qb + 1) * P
                    if hd > 0:
                        pe.wait_ge(pt_ready, 4 * hd)
                    s = bank[4 + qb]
                    product(s[:, 0:w], aq_hi[r, c, qb * P:w], aq_lo[r, c, qb * P:w], ak_hi[r, c, 0:w], ak_lo[r, c, 0:w],
                            True, False)
                    pe.matmul(s[:, 0:w], select[:, hd, :], ac2[:, 0:w], start=False, stop=False)
                    pe.matmul(s[:, qb * P:w], ident_r[:, :], causal[:, :], start=False, stop=True).then_inc(scores_ready, 1)

            def attend(hd, between):
                r = slice(64 * (hd % 2), 64 * (hd % 2) + 64)
                pe.wait_ge(p_ready, 4 * hd + 4)
                for kt in range(TT):
                    for qb in range(kt, TT):
                        last = pe.transpose(bank[4 + kt][:, qb * P:(qb + 1) * P], ap[:, qb, kt * P:(kt + 1) * P], ident)
                    last.then_inc(pt_full, 1)
                between()
                if hd % 2 == 0 and hd >= 2:
                    pe.wait_ge(ol_ready, hd // 2)
                for kt in range(TT):
                    pe.wait_ge(pt_ready, 4 * hd + kt + 1)
                    last = pe.matmul(bank[3][r, kt * P:T], av[:, kt, hd * FOX_DIM:(hd + 1) * FOX_DIM],
                                     apt[:, kt, kt * P:T], start=(kt == 0), stop=(kt == TT - 1))
                last.then_inc(o_ready, 1)

            def conv_slot(n, ks=range(KC)):
                c, kind = n // 3, n % 3
                if ks[0] > 0:
                    pass
                elif n < 3:
                    pe.wait_ge(a_evac, TT)
                elif kind == 0:
                    pe.wait_ge(gc_evac, c)
                elif kind == 1:
                    pe.wait_ge(z_ready, c)
                else:
                    pe.wait_ge(ut_ready, VALUE["a_gate"] + c)
                chunk(SLOT["a_conv"] + n, 0, bank[kind][:, :], u_hi, u_lo, ks=ks)

            pe.wait_ge(c_low, 1)
            pe.wait_ge(qkl_ready, 8)
            for hd in range(FOX_HEADS):
                scores(hd)
                slots = range(hd * 12 // 8, (hd + 1) * 12 // 8)
                for n in slots[:-1]:
                    conv_slot(n)
                conv_slot(slots[-1], range(KC - 2))
                attend(hd, lambda: conv_slot(slots[-1], range(KC - 2, KC)))

            def fox_ready(k):
                if k < 4:
                    pe.wait_ge(u_ready, SPLIT["a_gate"] + k + 1)
                else:
                    pe.wait_ge(ol_ready, k - 3)

            pe.wait_ge(z_ready, 4)
            out_chunks("a_out", acat_hi, acat_lo, consumed("a_mix"), fox_ready)
            post_norm("a_post", SLOT["a_ffn_in"])
            feed_forward("a")
            post_norm("a_fpost", SLOT["b_in"])

            two_chunks(SLOT["b_in"], bank[0:2], u_hi, u_lo, normed_input("b_pre"), high_input("b_pre"))
            for n in range(2, 16):
                if n >= 4:
                    pe.wait_ge(b_evac, n - 3)
                chunk(SLOT["b_in"] + n, 0, bank[n % 4][:, :], u_hi, u_lo)
                if n == 2:
                    mean_square("b_pre")
            for i, c in enumerate(PE_CHUNKS):
                pe.wait_ge(zl_ready, i + 1)
                for tap in range(LONG_TAPS):
                    n = LONG_TAPS * i + tap
                    pe.wait_ge(dg_ready, 2 * n + 2)
                    product(bank[5 + i][:, :], dg_hi[:, n % 4, :], dg_lo[:, n % 4, :], bz_hi[:, i, tap:tap + T],
                            bz_lo[:, i, tap:tap + T], tap == 0, tap == LONG_TAPS - 1).then_inc(dg_used, 1)
            for n, c in enumerate(CONV_ORDER):
                if c in PE_CHUNKS:
                    pe.wait_ge(tap_evac, PE_CHUNKS.index(c) + 1)
                elif c == POOL_CHUNK:
                    pe.wait_ge(pool_taps, LONG_TAPS - 1)
                elif c == SHARED:
                    pe.wait_ge(taps, len(TAP_DONE) + 1)
                else:
                    pe.wait_ge(taps, TAP_DONE[c, LONG_TAPS - 1])
                last = pe.matmul(STAT[:, :], ones[:, :], by[:, c, :], start=(n == 0), stop=(n == KC - 1))
            last.then_inc(mean_full, 1)
            pe.wait_ge(mean_ready, 1)
            for c in range(KC):
                pe.wait_ge(sq_ready, SQ["b_var"] + c + 1)
                pe.matmul(STAT[:, :], ones[:, :], sq[:, c % 2, :], start=(c == 0), stop=(c == KC - 1)).then_inc(sq_used, 1)
            out_chunks("b_out", by_hi, by_lo, consumed("b_mix"), normed_input("b_ln"), high_input("b_ln"))
            post_norm("b_post", SLOT["b_ffn_in"])
            feed_forward("b")
            post_norm("b_fpost", SLOT["c_fq"])

            two_chunks(SLOT["c_fq"], bank[0:2], u_hi, u_lo, normed_input("c_pre"), high_input("c_pre"))
            for n in range(2, 16):
                if n >= 4:
                    pe.wait_ge(c_evac, n - 3)
                chunk(SLOT["c_fq"] + n, 0, bank[n % 4][:, :], u_hi, u_lo)
                if n == 2:
                    mean_square("c_pre")

            def value_slot(n):
                def free(t):
                    if n == 0:
                        pe.wait_ge(c_evac, 2 * KC)
                    elif n == 4:
                        pe.wait_ge(i_evac, t + 1)
                token_major(SLOT["c_i"] + n, bank, n % 4, n % 4 == 3, free if n in (0, 4) else None)

            def gate_slot(n):
                if n < 2:
                    pe.wait_ge(co_evac, n + 1)
                else:
                    pe.wait_ge(g_evac, n - 1)
                chunk(SLOT["c_g"] + n, 0, bank[n % 2][:, :], u_hi, u_lo)

            def head_square(hd):
                pe.wait_ge(sq_ready, SQ["c_head"] + hd + 1)
                if hd < 4:
                    pe.wait_ge(co_evac, 4)
                    out = bank[2 + hd % 2]
                else:
                    pe.wait_ge(far_kept, 16)
                    out = bank[hd]
                if hd in (2, 3):
                    pe.wait_ge(rs_ln, RS["c_head"] + hd - 1)
                pe.matmul(out[:, :], ones[:, :], sq[:, hd % 2, :], start=True, stop=True).then_inc(sq_used, 1)

            N_LEVEL = 1 + len(LEVELS)
            PER_HEAD = 1 + 3 * 8
            for g in range(2):
                for lv in range(N_LEVEL):
                    last_first = g == 0 and lv == N_LEVEL - 1
                    if last_first:
                        value_slot(lv)
                    for e in range(4):
                        hd = 4 * g + e
                        if lv == 0:
                            pe.wait_ge(c_qkf, 3 * (hd + 1))
                            if g:
                                pe.wait_ge(far_kept, 8)
                        else:
                            pe.wait_ge(upd, upd_count(g, lv, e))
                            pe.wait_ge(level_kept, 4 * (N_LEVEL * g + lv - 1) + e + 1)
                        for t in range(TT):
                            s = slice(t * P, (t + 1) * P)
                            if lv == 0:
                                out, queries = bank[4 + e][:, s], cq[:, hd, s]
                            else:
                                out = bank[4 + e][:, t * P // 2:(t + 1) * P // 2]
                                queries = cq[:, hd, s].rearrange("p (b two s) -> p b two s", two=2, s=LEVELS[lv - 1])[:, :, 1, :]
                            last = pe.matmul(out, ck[:, hd, s], queries, start=True, stop=True)
                        last.then_inc(level_full, 1)
                    if g:
                        gate_slot(lv)
                    elif not last_first:
                        value_slot(lv)
                    if g and 1 <= lv <= 4:
                        head_square(lv - 1)
                for e in range(4):
                    hd = 4 * g + e
                    pe.wait_ge(level_kept, 4 * (N_LEVEL * g + N_LEVEL - 1) + e + 1)
                    if g == 0:
                        pe.wait_ge(i_evac, KC)
                    else:
                        pe.wait_ge(g_evac, KC)
                    for t in range(TT):
                        last = pe.matmul(bank[e][:, t * P:(t + 1) * P], cv[:, t, hd * P:(hd + 1) * P],
                                         ca[:, e, t * P:(t + 1) * P], start=(t == 0), stop=False, skip_group_check=True)
                    last.then_inc(pv_part, 1)
                for far in range(2):
                    for e in range(4):
                        hd = 4 * g + e
                        pe.wait_ge(upd, upd_count(g, N_LEVEL + far, e))
                        if far:
                            pe.wait_ge(far_kept, 8 * g + e + 1)
                        if far == 0:
                            for i in range(2):
                                last = pe.matmul(bank[4 + e][:, i * P:(i + 1) * P], ck[:, hd, 2 * i * P:(2 * i + 1) * P],
                                                 cq[:, hd, (2 * i + 1) * P:(2 * i + 2) * P], start=True, stop=True)
                        else:
                            for i in range(2):
                                last = pe.matmul(bank[4 + e][:, 2 * i * P:2 * (i + 1) * P], ck[:, hd, i * P:(i + 1) * P],
                                                 cq[:, hd, 2 * P:4 * P], start=True, stop=True)
                        last.then_inc(far_full, 1)
                    for e in range(4):
                        hd = 4 * g + e
                        pe.wait_ge(far_kept, 8 * g + 4 * far + e + 1)
                        for i in range(2):
                            if far == 0:
                                last = pe.matmul(bank[e][:, (2 * i + 1) * P:(2 * i + 2) * P],
                                                 cv[:, 2 * i, hd * P:(hd + 1) * P], ca[:, e, i * P:(i + 1) * P],
                                                 start=False, stop=False, skip_group_check=True)
                            else:
                                last = pe.matmul(bank[e][:, 2 * P:4 * P], cv[:, i, hd * P:(hd + 1) * P],
                                                 ca[:, e, 2 * i * P:2 * (i + 1) * P], start=False, stop=(i == 1),
                                                 skip_group_check=True)
                        last.then_inc(pv_part if far == 0 else co_full, 1)

            def heads_ready(k):
                if k == 0:
                    head_square(4)
                    head_square(5)
                    pe.wait_ge(cg_mul, 6)
                if k in (1, 2):
                    head_square(5 + k)
                pe.wait_ge(u_ready, SPLIT["c_out"] + k + 1)

            out_chunks("c_out", ccat_hi, ccat_lo, added("c_mix"), heads_ready)
            feed_forward("c")

            pe.wait_ge(h_ready, RESID["c_ffn"] + 6)
            two_chunks(SLOT["d_kv"], bank[0:2], u_hi, u_lo, normed_input("d_kv"))
            mean_square("d_pre")

            def window_scores(c):
                kv = c // 4
                pe.wait_ge(dq_low, 2 * c + 2)
                for n in range(TT):
                    lo = 0 if n else P
                    if c == 1:
                        pe.wait_ge(ds_ready, 8)
                    if c >= 2:
                        pe.wait_ge(dpt_ready, 4 * (c - 1))
                    keys = slice((n - 1) * P + lo, (n + 1) * P)
                    for e in range(2):
                        r, out, queries = rows_of(e), window_bank(n, e)[:, lo:], dq[:, c % 2, e, n * P:(n + 1) * P]
                        pe.matmul(out, queries, dk_hi[:, kv, keys], start=True, stop=False)
                        last = pe.matmul(out, queries[r], dk_lo[r, kv, keys], start=False, stop=True)
                    last.then_inc(ds_full, 1)

            def window_transpose(c):
                pe.wait_ge(ds_ready, 8 * min(c + 2, KC))
                for n in range(TT):
                    pe.wait_ge(ds_p, 8 * c + 2 * n + 2)
                    for kt in range(0 if n else 1, 2):
                        for e in range(2):
                            last = pe.transpose(bank[4 + n][:, (2 * kt + e) * P:(2 * kt + e + 1) * P],
                                                ds_[:, c % 2, n, e, kt * P:(kt + 1) * P], ident)
                    last.then_inc(dpt_full, 1)

            def window_values(c):
                kv = c // 4
                if c >= 2:
                    pe.wait_ge(dol_ready, c - 1)
                o = bank[2 + c % 2]
                for n in range(TT):
                    pe.wait_ge(dpt_ready, 4 * c + n + 1)
                    for e in range(2):
                        first = 0 if n else 1
                        for kt in range(first, 2):
                            last = pe.matmul(o[64 * e:64 * e + 64, n * P:(n + 1) * P],
                                             dv[:, n - 1 + kt, 64 * kv:64 * kv + 64],
                                             dpt[:, n, (2 * kt + e) * P:(2 * kt + e + 1) * P],
                                             start=(kt == first), stop=(kt == 1))
                last.then_inc(do_ready, 1)

            def query_slot(n, ks):
                if n >= 4 and not ks[0]:
                    pe.wait_ge(d_q_evac, n - 1)
                chunk(SLOT["d_q"] + n, 0, bank[n % 2][:, :], u_hi, u_lo, ks=ks)

            two_chunks(SLOT["d_q"], bank[2:4], u_hi, u_lo, normed_input("d_q"), high_input("d_q"))
            pe.wait_ge(d_kv_evac, 2)
            for t in range(TT):
                last = pe.transpose(bank[0][:, t * P:(t + 1) * P], ut[:, 1, t * P:(t + 1) * P], ident)
            last.then_inc(d_vt_full, 1)
            pe.wait_ge(d_kv_ready, 5)
            pe.wait_ge(dk_low, 4)
            window_scores(0)
            query_slot(2, range(KC))
            for c in range(KC - 2):
                window_scores(c + 1)
                if c:
                    window_values(c - 1)
                if c + 3 < KC:
                    query_slot(c + 3, range(KC - 2))
                window_transpose(c)
                if c + 3 < KC:
                    query_slot(c + 3, range(KC - 2, KC))
            window_scores(KC - 1)
            window_values(KC - 3)

            def window_ready(k):
                if k in (2, 5):
                    window_transpose(KC - 2 if k == 2 else KC - 1)
                elif k in (3, 6):
                    window_values(KC - 2 if k == 3 else KC - 1)
                pe.wait_ge(dol_ready, k + 1)

            out_chunks("d_out", dcat_hi, dcat_lo, added("d_mix"), window_ready)
            feed_forward("d")
            mean_square("final")

        @block.scalar
        def _(act):
            def log_table(n):
                act.activation(spare[:, n:n + 1], ones[:, 0:1], ACT.Ln)

            def high_part(s, i=0):
                j = s % RING
                act.wait_ge(raw_landed[j], 16 * i + 16 * (s // RING + 1))
                act.activation(w_hi[:, j, :], raw[:, j, :], ACT.Copy).then_inc(hi_ready, 1)

            def slot_over(s, i=0):
                act.wait_ge(slot_done, s + RING * i + 1)
                if s + AHEAD < N_SLOTS:
                    high_part(s + AHEAD, i)

            def square(name, c, src, bias=0.0):
                if c >= 2:
                    if name in DIRECT:
                        act.wait_ge(sq_used, USED[name] + c - 1)
                    else:
                        act.wait_ge(acc_ready, ACC[name] + max(c - 2, 1))
                act.activation(sq[:, c % 2, :], src, ACT.Square, bias=bias).then_inc(sq_ready, 1)

            def root(name, i=0, src=STAT, scale=1.0 / D, e=0, to=rs):
                n = RS[name] + i
                if name in SUM:
                    act.wait_ge(sum_full, SUM[name] + 1)
                act.activation(to[:, :], src[:, :], ACT.Ln, bias=eps[:, e:e + 1], scale=scale).then_inc(rs_ln, 1)
                if name in TOK:
                    act.wait_ge(tok_full, TOK[name] + 1)
                    act.activation(rs_tok[:, :], TOK_STAT[:, 0:TT], ACT.Ln, bias=eps[:, e:e + 1], scale=scale).then_inc(tok_ln, 1)
                act.wait_ge(rs_ln, n + 1)
                act.activation(to[:, :], to[:, :], ACT.Exp, scale=-0.5).then_inc(rs_ready, 1)
                if name in TOK:
                    act.wait_ge(tok_ln, TOK[name] + 1)
                    act.activation(rs_tok[:, :], rs_tok[:, :], ACT.Exp, scale=-0.5).then_inc(tok_ready, 1)

            def square_h(name, resid, chunks=range(KC)):
                for c in chunks:
                    act.wait_ge(x_landed[c] if resid is None else h_ready, 16 if resid is None else RESID[resid] + c + 1)
                    square(name, c, h[:, c, :])

            def scaled_input(split, resid, chunks=range(KC)):
                for c in chunks:
                    act.wait_ge(x_landed[c] if resid is None else h_ready, 16 if resid is None else RESID[resid] + c + 1)
                    act.activation(u_hi[:, c, :], h[:, c, :], ACT.Identity, scale=pre_gain(split, c)).then_inc(uh_ready, 1)

            def first_slots(s, stat):
                for n in range(3):
                    slot_over(s + n)
                root(stat)

            def high_of(name, c, dst):
                act.wait_ge(ut_ready, VALUE[name] + c + 1)
                act.activation(dst, ut[:, (VALUE[name] + c) % 2, :], ACT.Copy).then_inc(uh_ready, 1)

            def square_out(part, stat, bias=None):
                for n in range(KC):
                    act.wait_ge(slot_done, SLOT[part] + n + 1)
                    square(stat, n, bank[n % 4][:, :], bias(n) if bias else 0.0)
                    if n < KC - 1:
                        high_part(SLOT[part] + n + AHEAD)
                root(stat)
                high_part(SLOT[part] + KC - 1 + AHEAD)

            def feed_forward(l, second):
                s0, s1 = SLOT[f"{l}_ffn_in"], SLOT[f"{l}_ffn_out"]

                def pair(i, b, over=True):
                    j = 2 * i + b
                    if over:
                        slot_over(s0 + 2 * b, i)
                    act.wait_ge(scaled_ready, HID[l] + j + 1)
                    if second is not None:
                        def one(name, at):
                            at += VEC[name] + b
                            return vec[:, at:at + 1] if isinstance(i, int) else vec[:, bass.ds(2 * i + at, 1)]
                        act.activation(gconv[:, b, :], ut[:, b, :], ACT.Identity, bias=one("ffn_conv_b", second * FC),
                                       scale=one("ffn_conv_w", (second * FFN_TAPS + 2) * FC)).then_inc(gconv0_ready, 1)
                        act.wait_ge(gconv_ready, CONVG[l] + 2 * j + 2)
                    act.activation(gconv[:, b, :], gconv[:, b, :], ACT.Silu).then_inc(gate_ready, 1)
                    if over:
                        slot_over(s0 + 2 * b + 1, i)

                first_slots(s0, f"{l}_fpre")
                pair(0, 0, False)
                slot_over(s0 + 3)
                pair(0, 1, False)
                with act.Fori(1, FC // 2) as i:
                    for b in range(2):
                        pair(i, b)
                log_table("abcd".index(l))

            def way_back(l, half):
                s = SLOT[f"{l}_ffn_out"] + HALF * half
                with act.Fori(0, 2) as i:
                    for n in range(RING):
                        slot_over(s + n, i)
                for n in range(2 * RING, HALF - 1):
                    slot_over(s + n)

            def last_back(l, half):
                slot_over(SLOT[f"{l}_ffn_out"] + HALF * (half + 1) - 1)

            def ffn_square_out(l, stat):
                for half in range(2):
                    way_back(l, half)
                    for n in range(4 * half, 4 * half + 4):
                        square(stat, n, ffn_full(act, l, n)[:, :])
                    if half:
                        root(stat)
                    last_back(l, half)

            act.wait_ge(consts_made, 2)

            log_table(4)
            act.wait_ge(gain_landed, 16)
            high_part(0)
            scaled_input("a_pre", None, (0,))
            high_part(1)
            scaled_input("a_pre", None, range(1, KC))
            high_part(2)
            square_h("a_pre", None)
            act.wait_ge(vec_landed, 16)
            act.activation(wf_hi[:, :, :, :], wf, ACT.Copy).then_inc(wf_ready, 1)
            act.wait_ge(consts_landed, 48)
            for dst, src in ((ident_r[:, :], ident), (causal[:, :], ap[:, 0, 0:P]), (select[:, :, :], select_raw)):
                act.activation(dst, src, ACT.Copy).then_inc(rounded, 1)
            act.activation(ac2[:, :], ones[:, 0:1].to_broadcast([P, T]), ACT.Copy, scale=0.0).then_inc(zeroed, 1)
            first_slots(0, "a_pre")
            for n in range(8):
                if n >= 3:
                    slot_over(n)
                act.wait_ge(qk_evac, n + 1)
                act.activation((aq_hi if n < 4 else ak_hi)[:, n % 4, :], ut[:, n % 2, :], ACT.Copy).then_inc(qkh_ready, 1)
            act.wait_ge(f_read, 1)
            f8 = slice(0, FOX_HEADS)
            act.activation(ap[f8, 1, :], ap[f8, 0, :], ACT.Abs).then_inc(f_exp, 1)
            act.wait_ge(f_exp, 1)
            act.activation(ap[f8, 1, :], ap[f8, 1, :], ACT.Exp, scale=-1.0).then_inc(f_exp, 1)
            act.wait_ge(f_exp, 2)
            act.activation(ap[f8, 1, :], ap[f8, 1, :], ACT.Ln, bias=1.0).then_inc(f_ln, 1)
            slot_over(SLOT["a_v"])
            act.wait_ge(c_ready, 1)
            act.wait_ge(zeroed, 1)
            act.activation(ac2[0:FOX_HEADS, :], ac[:, :], ACT.Copy).then_inc(c_high, 1)
            for n in range(1, 4):
                slot_over(SLOT["a_v"] + n)
            for t in range(TT):
                if t == 0:
                    act.wait_ge(tok_ready, TOK["a_pre"] + 1)
                act.activation(av[:, t, :], bank[t][:, :], ACT.Copy, scale=rs_tok[:, t:t + 1]).then_inc(a_evac, 1)
            nmax, rsum = small[:, 0:8], small[:, 8:16]
            for hd in range(FOX_HEADS):
                for qb in range(TT):
                    w, i = (qb + 1) * P, 4 * (hd % 2) + qb
                    act.wait_ge(max_ready, 4 * hd + qb + 1)
                    after(act, pt_full, 4 * hd)
                    act.activation(ap[:, qb, 0:w], bank[4 + qb][:, 0:w], ACT.Exp, bias=nmax[:, i:i + 1],
                                   accum_out=rsum[:, i:i + 1]).then_inc(exp_ready, 1)

                def conv_over(n):
                    slot_over(SLOT["a_conv"] + n)
                    if n % 3 == 2:
                        high_of("a_gate", n // 3, acat_hi[:, n // 3, :])

                slots = range(hd * 12 // 8, (hd + 1) * 12 // 8)
                for n in slots[:-1]:
                    conv_over(n)
                for kt in range(TT):
                    act.wait_ge(pt_full, 4 * hd + kt + 1)
                    after(act, o_ready, hd)
                    act.activation(apt[:, kt, kt * P:T], bank[4 + kt][:, kt * P:T], ACT.Copy).then_inc(pt_ready, 1)
                conv_over(slots[-1])
                if hd % 2:
                    act.wait_ge(o_ready, hd + 1)
                    act.activation(acat_hi[:, 4 + hd // 2, :], bank[3][:, :], ACT.Copy).then_inc(oh_ready, 1)
            log_table(6)
            square_out("a_out", "a_post")
            scaled_input("a_fpre", "a_mix")
            square_h("a_fpre", "a_mix")
            feed_forward("a", None)
            ffn_square_out("a", "a_fpost")

            scaled_input("b_pre", "a_ffn")
            square_h("b_pre", "a_ffn")
            act.activation(wt_hi[:, :], col("w_dw", 0, LONG_TAPS * KC), ACT.Copy).then_inc(wt_ready, 1)

            def high_gated(i):
                act.wait_ge(bz_ready, PE_CHUNKS[i] + 1)
                act.activation(bz_hi[:, i, :], bz[:, PE_CHUNKS[i], :], ACT.Copy).then_inc(zh_ready, 1)

            def diagonal(i, tap):
                n, at = LONG_TAPS * i + tap, tap * KC + PE_CHUNKS[i]
                after(act, dg_used, n - 3)
                act.activation(dg_hi[:, n % 4, :], ident, ACT.Identity, scale=col("w_dw", at)).then_inc(dg_ready, 1)
                act.activation(dg_lo[:, n % 4, :], ident, ACT.Identity, scale=wt_lo[:, at:at + 1]).then_inc(dg_ready, 1)

            first_slots(SLOT["b_in"], "b_pre")
            for n in range(16):
                c = n // 2
                if n >= 3:
                    slot_over(SLOT["b_in"] + n)
                if n % 2:
                    act.wait_ge(b_evac, n + 1)
                    act.activation(ba[:, c % 2, 1, :], ba[:, c % 2, 1, :], ACT.Sigmoid, bias=col("b_pw1", KC + c)).then_inc(b_sig, 1)
                if n >= PROD_SLOT:
                    for tap in range(0 if n == PROD_SLOT else 2 * (n - PROD_SLOT) + 1, 2 * (n - PROD_SLOT) + 3):
                        at = tap * KC + POOL_CHUNK
                        if tap == 0:
                            act.wait_ge(bz_ready, POOL_CHUNK + 1)
                            act.activation(by[:, POOL_CHUNK, :], bz[:, POOL_CHUNK, 0:T], ACT.Identity, scale=col("w_dw", at),
                                           bias=col("b_dw", POOL_CHUNK)).then_inc(prod_ready, 1)
                        else:
                            after(act, pool_taps, tap - 2)
                            act.activation(bprod[:, tap % 2, :], bz[:, POOL_CHUNK, tap:tap + T], ACT.Copy,
                                           scale=col("w_dw", at)).then_inc(prod_ready, 1)
                if n % 2 and c in PE_CHUNKS[:-1]:
                    high_gated(PE_CHUNKS.index(c))
                if n == 2 * KC - 2:
                    act.wait_ge(wt_ready, 2)
                    for tap in range(4):
                        diagonal(0, tap)

            def tap_over(i):
                act.wait_ge(dg_used, LONG_TAPS * (i + 1))
                act.activation(by[:, PE_CHUNKS[i], :], bank[5 + i][:, :], ACT.Identity, bias=col("b_dw", PE_CHUNKS[i]))\
                   .then_inc(tap_evac, 1)

            for i, c in enumerate(PE_CHUNKS):
                for tap in range(0 if i else 4, LONG_TAPS):
                    if tap == 6 and i == 0:
                        high_gated(PE_CHUNKS.index(KC - 1))
                    elif tap == 6:
                        tap_over(i - 1)
                    diagonal(i, tap)
                if i == len(PE_CHUNKS) - 1:
                    tap_over(i)
            log_table(5)
            act.wait_ge(mean_full, 1)
            act.activation(bmean[:, :], STAT[:, :], ACT.Copy, scale=1.0 / D).then_inc(mean_ready, 1)
            for c in range(KC):
                act.wait_ge(xc_ready, c + 1)
                square("b_var", c, by[:, c, :])
            act.wait_ge(sq_used, USED["b_var"] + KC)
            root("b_var", e=1)
            for c in range(KC):
                n, v = SPLIT["b_ln"] + c, VALUE["b_ln"] + c
                act.wait_ge(yn_ready, c + 1)
                act.wait_ge(u_ready, n - 1)
                for dst, done in ((by_hi[:, c, :], uh_ready), (ut[:, v % 2, :], ut_ready)):
                    act.activation(dst, by[:, c, :], ACT.Silu, bias=col("ln_b", c), scale=col("ln_g", c)).then_inc(done, 1)
            log_table(7)
            square_out("b_out", "b_post", lambda n: col("b_pw2", n))
            scaled_input("b_fpre", "b_mix")
            square_h("b_fpre", "b_mix")
            feed_forward("b", None)
            ffn_square_out("b", "b_fpost")

            act.dma_start(cmask[:, :, :], masks_d).then_inc(mask_landed, 16)
            scaled_input("c_pre", "b_ffn")
            square_h("c_pre", "b_ffn")
            act.wait_ge(lb_step, 3)
            act.activation(small[:, 16:32], small[:, 16:32], ACT.Exp).then_inc(lb_step, 1)
            first_slots(SLOT["c_fq"], "c_pre")
            for n in range(16):
                c = n // 2
                if 3 <= n < 15:
                    slot_over(SLOT["c_fq"] + n)
                act.wait_ge(c_evac, n + 1)
                if n % 2:
                    act.activation(cq[:, c, :], ut[:, c % 2, :], ACT.Sigmoid).then_inc(c_sig, 1)
                else:
                    act.activation(cf[:, c, :], cf[:, c, :], ACT.Sigmoid).then_inc(c_sig, 1)
            slot_over(SLOT["c_fq"] + 15)

            def value_over(n):
                if n % 4 < 3:
                    slot_over(SLOT["c_i"] + n)
                else:
                    half = slice(512 * (n // 4), 512 * (n // 4) + 512)
                    act.wait_ge(slot_done, SLOT["c_i"] + n + 1)
                    for t in range(TT):
                        act.activation(cv[:, t, half], bank[t][:, :], ACT.Copy, scale=rs_tok[:, t:t + 1]).then_inc(i_evac, 1)
                    slot_over(SLOT["c_i"] + n)

            def gate_over(n):
                slot_over(SLOT["c_g"] + n)
                act.wait_ge(g_evac, n + 1)
                act.activation(cg[:, n, :], cg[:, n, :], ACT.Silu).then_inc(g_ready, 1)

            def head_norm(hd):
                src = bank[2 + hd % 2] if hd < 4 else bank[hd]
                act.wait_ge(sq_used, USED["c_head"] + hd + 1)
                if hd:
                    act.wait_ge(ut_ready, VALUE["c_out"] + hd)
                root("c_head", hd, src, 1.0 / P, to=rs_head)
                high_of("c_out", hd, ccat_hi[:, hd, :])

            for g in range(2):
                for lv in range(8):
                    if g and 1 <= lv <= 4:
                        square("c_head", lv - 1, cf[:, lv - 1, :])
                    (gate_over if g else value_over)(lv)
                    if g and 1 <= lv <= 4:
                        head_norm(lv - 1)
                if g:
                    log_table(8)
                for far in range(2):
                    for e in range(4):
                        w = T if far else 2 * P
                        act.wait_ge(far_full, 8 * g + 4 * far + e + 1)
                        act.wait_ge(pv_part, 8 * g + 4 * far + e + 1)
                        act.activation(ca[:, e, 0:w], bank[4 + e][:, 0:w], ACT.Copy).then_inc(far_kept, 1)
                for e in range(4 if g == 0 else 0):
                    act.wait_ge(co_full, e + 1)
                    act.activation(cf[:, e, :], bank[e][:, :], ACT.Copy).then_inc(co_evac, 1)
            for hd in range(4, HG_HEADS + 2):
                if hd < HG_HEADS:
                    act.wait_ge(co_full, hd + 1)
                    square("c_head", hd, bank[hd - 4][:, :])
                if hd >= 6:
                    act.wait_ge(sq_used, USED["c_head"] + hd - 1)
                    act.activation(ca[:, hd - 6, :], bank[hd - 2][:, :], ACT.Ln, bias=eps[:, 0:1], scale=1.0 / P).then_inc(rs_ln, 1)
            for hd in range(4, HG_HEADS + 1):
                if hd < HG_HEADS:
                    act.wait_ge(rs_ln, RS["c_head"] + hd + 1)
                    act.activation(ca[:, hd - 4, :], ca[:, hd - 4, :], ACT.Exp, scale=-0.5).then_inc(rs_ready, 1)
                if hd > 4:
                    high_of("c_out", hd - 1, ccat_hi[:, hd - 1, :])

            def add_over(l):
                for n in range(KC):
                    slot_over(SLOT[f"{l}_out"] + n)
                    scaled_input(f"{l}_fpre", f"{l}_mix", (n,))
                    square_h(f"{l}_fpre", f"{l}_mix", (n,))

            add_over("c")
            feed_forward("c", 0)
            for half in range(2):
                way_back("c", half)
                scaled_input("d_kv", "c_ffn", range(4 * half, 4 * half + 4))
                square_h("d_pre", "c_ffn", range(4 * half, 4 * half + 4))
                last_back("c", half)

            act.dma_start(dist[:, :], squares[:, 2 * P:]).then_inc(dist_landed, 16)
            slot_over(SLOT["d_kv"])
            act.wait_ge(slot_done, SLOT["d_kv"] + 2)
            scaled_input("d_q", "c_ffn")
            slot_over(SLOT["d_kv"] + 1)
            root("d_pre")
            act.wait_ge(d_kv_evac, 1)
            for kv in range(2):
                for e in range(2):
                    act.activation(dk_hi[rows_of(e), kv, :], ut[rows_of(kv), 0, :], ACT.Copy).then_inc(d_kv_ready, 1)

            def query_high(n):
                act.wait_ge(d_q_evac, n + 1)
                for e in range(2):
                    act.activation(dq[rows_of(e), n % 2, e, :], ut[rows_of(e), n % 2, :], ACT.Copy).then_inc(dq_high, 1)

            act.wait_ge(d_vt_full, 1)
            act.activation(dv[:, :, :], bank[0][:, :].rearrange("p (t n) -> p t n", t=TT), ACT.Copy).then_inc(d_kv_ready, 1)

            def window_exp(c):
                _, nm, den, es = window_small(c)
                act.wait_ge(ds_nm, 2 * c + 2)
                act.activation(es, es, ACT.Exp).then_inc(ds_sink, 1)
                for n in range(TT):
                    lo = 0 if n else P
                    for e in range(2):
                        i, p = 2 * n + e, ds_[:, c % 2, n, e, lo:]
                        act.activation(p, p, ACT.Exp, bias=nm[:, i:i + 1], accum_out=den[:, i:i + 1]).then_inc(ds_exp, 1)

            query_high(0)
            query_high(1)
            slot_over(SLOT["d_q"])
            slot_over(SLOT["d_q"] + 1)
            window_exp(0)
            slot_over(SLOT["d_q"] + 2)
            query_high(2)

            def window_out(c):
                act.wait_ge(do_ready, c + 1)
                act.activation(dcat_hi[:, c, :], bank[2 + c % 2][:, :], ACT.Copy).then_inc(doh_ready, 1)

            for c in range(KC):
                if c:
                    window_out(c - 1)
                for n in range(TT):
                    lo = 0 if n else 2 * P
                    act.wait_ge(dpt_full, 4 * c + n + 1)
                    after(act, do_ready, c)
                    act.activation(dpt[:, n, lo:], bank[4 + n][:, lo:], ACT.Copy).then_inc(dpt_ready, 1)
                if c + 1 < KC:
                    window_exp(c + 1)
                if c + 3 < KC:
                    slot_over(SLOT["d_q"] + c + 3)
                    query_high(c + 3)
            window_out(KC - 1)
            add_over("d")
            feed_forward("d", 1)
            for half in range(2):
                way_back("d", half)
                square_h("final", "d_ffn", range(4 * half, 4 * half + 4))
                if half:
                    root("final")
                for c in range(4 * half, 4 * half + 4):
                    act.activation(m[:, c, :], h[:, c, :], ACT.Identity, scale=col("final_norm", c)).then_inc(scaled_out, 1)
                last_back("d", half)

        @block.vector
        def _(dve):
            def split_value(name, c, make):
                if c >= 2:
                    dve.wait_ge(u_ready, SPLIT[name] + c - 1)
                make(ut[:, (VALUE[name] + c) % 2, :]).then_inc(ut_ready, 1)

            def low_of(name, c, dst, hi):
                dve.wait_ge(uh_ready, SPLIT[name] + c + 1)
                dve.wait_ge(ut_ready, VALUE[name] + c + 1)
                dve.tensor_tensor(dst, ut[:, (VALUE[name] + c) % 2, :], hi.bitcast(F32), ALU.subtract).then_inc(u_ready, 1)

            def sum_squares(name, chunks=range(1, KC)):
                for c in chunks:
                    dve.wait_ge(sq_ready, SQ[name] + c + 1)
                    if c >= 2:
                        dve.wait_ge(acc_ready, ACC[name] + c - 1)
                    dve.tensor_tensor(acc[:, :], sq[:, 0, :] if c == 1 else acc[:, :], sq[:, c % 2, :], ALU.add).then_inc(acc_ready, 1)

            def scaled_low(split, c):
                dve.wait_ge(uh_ready, SPLIT[split] + c + 1)
                dve.scalar_tensor_tensor(out=u_lo[:, c, :], in0=h[:, c, :], scalar=pre_gain(split, c), in1=u_hi[:, c, :].bitcast(F32),
                                         op0=ALU.mult, op1=ALU.subtract).then_inc(u_ready, 1)

            stat_of = {"a_mix": "a_post", "a_ffn": "a_fpost", "b_mix": "b_post", "b_ffn": "b_fpost"}

            def norm_add(made, gain, at, split, stat):
                def norm(c):
                    dve.tensor_tensor(m[:, c, :], m[:, c, :], rs[:, :], ALU.mult).then_inc(normed_0, 1)

                dve.wait_ge(rs_ready, RS[stat_of[made]] + 1)
                norm(0)
                for c in range(KC + 1):
                    if c < DVE_NORMS:
                        dve.wait_ge(normed_0, POST[stat_of[made]] + c + 1)
                    elif c < KC:
                        dve.wait_ge(normed, NORMED[made] + c + 1 - DVE_NORMS)
                    if c < KC:
                        dve.scalar_tensor_tensor(out=h[:, c, :], in0=m[:, c, :], scalar=col(gain, at + c), in1=h[:, c, :],
                                                 op0=ALU.mult, op1=ALU.add).then_inc(h_ready, 1)
                    if c + 1 < DVE_NORMS:
                        norm(c + 1)
                        scaled_low(split, c)
                    elif c >= DVE_NORMS:
                        scaled_low(split, c - 1)
                sum_squares(stat)

            def keep_chunk(stat, n, src, bias=None):
                dve.wait_ge(sq_ready, SQ[stat] + n + 1)
                if bias is not None:
                    dve.tensor_scalar(m[:, n, :], src[:, :], bias, None, ALU.add).then_inc(made_ready, 1)
                else:
                    dve.tensor_copy(m[:, n, :], src[:, :]).then_inc(made_ready, 1)
                if 1 <= n < KC - 1:
                    sum_squares(stat, (n,))

            def keep_out(part, stat, bias=None):
                for n in range(KC):
                    dve.wait_ge(slot_done, SLOT[part] + n + 1)
                    keep_chunk(stat, n, bank[n % 4], bias(n) if bias else None)

            def add_out(l):
                for n in range(KC + 1):
                    if n < KC:
                        dve.wait_ge(slot_done, SLOT[f"{l}_out"] + n + 1)
                        dve.tensor_tensor(h[:, n, :], h[:, n, :], bank[n % 4][:, :], ALU.add).then_inc(h_ready, 1)
                    if n:
                        scaled_low(f"{l}_fpre", n - 1)
                    if n >= 2:
                        sum_squares(f"{l}_fpre", (n - 1,))

            def add_ffn(l, stat, split=None):
                for half in range(2):
                    for n in range(4 * half, 4 * half + 4):
                        src = ffn_full(dve, l, n)
                        dve.tensor_tensor(h[:, n, :], h[:, n, :], src[:, :], ALU.add).then_inc(h_ready, 1)
                        if split and n % 4:
                            scaled_low(split, n - 1)
                        elif not split and n >= 2:
                            sum_squares(stat, (n - 1,))
                    if split:
                        scaled_low(split, 4 * half + 3)
                        sum_squares(stat, range(max(4 * half, 1), 4 * half + 4))

            def feed_forward(l, second):
                s0 = SLOT[f"{l}_ffn_in"]

                def at(t, j, i):
                    return t[:, j, :] if isinstance(i, int) else t[:, bass.ds(j, 1), :].rearrange("p o t -> p (o t)")

                def pair(i, b):
                    j = 2 * i + b
                    scaled = gconv if second is None else ut
                    dve.wait_ge(slot_done, s0 + 2 * j + 1)
                    if not isinstance(i, int) or i:
                        dve.wait_ge(hid_ready, HID[l] + j - 1)
                    else:
                        dve.wait_ge(rs_ready, RS[f"{l}_fpre"] + 1)
                    dve.tensor_tensor(scaled[:, b, :], bank[2 * b][:, :], rs[:, :], ALU.mult).then_inc(scaled_ready, 1)
                    if second is not None:
                        dve.wait_ge(gconv0_ready, HID[l] - HID["c"] + j + 1)
                        for tap in (1, 0):
                            back = 2 - tap
                            base = VEC["ffn_conv_w"] + (second * FFN_TAPS + tap) * FC + b
                            w = vec[:, base:base + 1] if isinstance(i, int) else vec[:, bass.ds(2 * i + base, 1)]
                            if tap == 0:
                                dve.wait_ge(gconv_ready, CONVG[l] + 2 * j + 1)
                            dve.scalar_tensor_tensor(out=gconv[:, b, back:], in0=ut[:, b, 0:T - back], scalar=w,
                                                     in1=gconv[:, b, back:], op0=ALU.mult, op1=ALU.add).then_inc(gconv_ready, 1)
                    dve.wait_ge(slot_done, s0 + 2 * j + 2)
                    dve.wait_ge(gate_ready, HID[l] + j + 1)
                    dve.tensor_tensor(ut[:, b, :], gconv[:, b, :], bank[2 * b + 1][:, :], ALU.mult).then_inc(ht_ready, 1)
                    dve.wait_ge(ht_ready, HID[l] + j + 1)
                    dve.tensor_tensor(ut[:, b, :], ut[:, b, :], rs[:, :], ALU.mult).then_inc(t2_ready, 1)
                    dve.wait_ge(t2_ready, HID[l] + j + 1)
                    hi, lo = at(hid_hi, j, i), at(hid_lo, j, i)
                    dve.tensor_scalar(hi, ut[:, b, :], 1.0, None, ALU.mult).then_inc(hh_ready, 1)
                    dve.wait_ge(hh_ready, HID[l] + j + 1)
                    dve.tensor_tensor(lo, ut[:, b, :], hi.bitcast(F32), ALU.subtract).then_inc(hid_ready, 1)

                pair(0, 0)
                pair(0, 1)
                with dve.Fori(1, FC // 2) as i:
                    for b in range(2):
                        pair(i, b)

            def keep_ffn(l, stat):
                for n in range(KC):
                    keep_chunk(stat, n, ffn_full(dve, l, n))

            dve.memset(ones[:, :], 1.0).then_inc(consts_made, 1)
            dve.memset(eps[:, 0:1], RMS_EPS)
            dve.memset(eps[:, 1:2], LN_EPS).then_inc(consts_made, 1)
            dve.memset(az[:, 0:SHORT_TAPS - 1], 0.0)

            for c in range(KC):
                if c < DVE_SLOTS:
                    dve.wait_ge(hi_ready, c + 1)
                    dve.tensor_tensor(w_lo[:, c, :], raw[:, c, :], w_hi[:, c, :].bitcast(F32), ALU.subtract).then_inc(w_ready, 1)
                scaled_low("a_pre", c)
            sum_squares("a_pre")
            dve.wait_ge(wf_ready, 1)
            dve.tensor_tensor(wf_lo[:, :, :, :], wf, wf_hi[:, :, :, :].bitcast(F32), ALU.subtract).then_inc(wf_ready, 1)
            dve.wait_ge(rs_ready, RS["a_pre"] + 1)

            def low_qk(n):
                dve.wait_ge(qkh_ready, n + 1)
                hi, lo = (aq_hi, aq_lo) if n < 4 else (ak_hi, ak_lo)
                dve.tensor_tensor(lo[:, n % 4, :], ut[:, n % 2, :], hi[:, n % 4, :].bitcast(F32), ALU.subtract).then_inc(qkl_ready, 1)

            for n in range(8):
                dve.wait_ge(slot_done, n + 1)
                if n >= 2:
                    dve.wait_ge(qkl_ready, n - 1)
                dve.scalar_tensor_tensor(out=ut[:, n % 2, :], in0=bank[n % 4][:, :], scalar=FOX_DIM ** -0.5 if n < 4 else 1.0,
                                         in1=rs[:, :], op0=ALU.mult, op1=ALU.mult).then_inc(qk_evac, 1)
                if n:
                    low_qk(n - 1)
            low_qk(7)
            f8 = slice(0, FOX_HEADS)
            dve.wait_ge(f_full, 1)
            dve.tensor_tensor(ap[f8, 0, :], bank[4][f8, :], rs[f8, :], ALU.mult).then_inc(f_evac, 1)
            dve.wait_ge(f_evac, 1)
            dve.tensor_scalar(ap[f8, 0, :], ap[f8, 0, :], vec[f8, VEC["b_forget"]:VEC["b_forget"] + 1], None, ALU.add)\
               .then_inc(f_read, 1)
            dve.wait_ge(f_ln, 1)
            dve.wait_ge(f_read, 1)
            dve.scalar_tensor_tensor(out=ap[f8, 2, :], in0=ap[f8, 0, :], scalar=0.0, in1=ap[f8, 1, :],
                                     op0=ALU.min, op1=ALU.subtract).then_inc(logf, 1)
            dve.memset(ap[f8, 3, :], 1.0).then_inc(logf, 1)
            dve.wait_ge(logf, 2)
            dve.tensor_tensor_scan(ac[:, :], ap[f8, 3, :], ap[f8, 2, :], 0.0, ALU.mult, ALU.add).then_inc(c_ready, 1)
            dve.wait_ge(zeroed, 1)
            dve.wait_ge(c_high, 1)
            dve.tensor_tensor(ac2[LOW_ROW:LOW_ROW + FOX_HEADS, :], ac[:, :], ac2[f8, :].bitcast(F32), ALU.subtract).then_inc(c_low, 1)
            nmax, rsum, rinv = small[:, 0:8], small[:, 8:16], small[:, 48:56]
            for hd in range(FOX_HEADS):
                o4 = 4 * (hd % 2)
                for qb in range(TT):
                    dve.wait_ge(scores_ready, 4 * hd + qb + 1)
                    dve.tensor_reduce(nmax[:, o4 + qb:o4 + qb + 1], bank[4 + qb][:, 0:(qb + 1) * P], AX_X, ALU.max,
                                      negate=True).then_inc(max_ready, 1)
                dve.wait_ge(exp_ready, 4 * hd + 4)
                dve.reciprocal(rinv[:, o4:o4 + 4], rsum[:, o4:o4 + 4]).then_inc(inv_ready, 1)
                dve.wait_ge(inv_ready, hd + 1)
                for qb in range(TT):
                    w = (qb + 1) * P
                    dve.tensor_scalar(ap[:, qb, 0:w], ap[:, qb, 0:w], rinv[:, o4 + qb:o4 + qb + 1], None, ALU.mult)\
                       .then_inc(p_ready, 1)
                for n in range(hd * 12 // 8, (hd + 1) * 12 // 8):
                    c, kind = n // 3, n % 3
                    dve.wait_ge(slot_done, SLOT["a_conv"] + n + 1)
                    if kind == 0:
                        after(dve, z_ready, c)
                        dve.tensor_tensor(agc[:, :], bank[0][:, :], rs[:, :], ALU.mult).then_inc(gc_evac, 1)
                        dve.wait_ge(gc_evac, c + 1)
                        dve.tensor_tensor(agc[:, :], agc[:, :], rs[:, :], ALU.mult).then_inc(gc_ready, 1)
                    if kind == 1:
                        dve.wait_ge(gc_ready, c + 1)
                        after(dve, sconv, 4 * c)
                        dve.tensor_tensor(az[:, SHORT_TAPS - 1:], agc[:, :], bank[1][:, :], ALU.mult).then_inc(z_ready, 1)
                        dve.wait_ge(z_ready, c + 1)
                        after(dve, ut_ready, VALUE["a_gate"] + c if c else 0)
                        for i, tap in enumerate((2, 1, 0)):
                            w = col("short_conv", tap * 4 + c)
                            if i == 0:
                                ins = dve.tensor_scalar(ay[:, :], az[:, tap:tap + T], w, None, ALU.mult)
                            else:
                                dve.wait_ge(sconv, 4 * c + i)
                                ins = dve.scalar_tensor_tensor(out=ay[:, :], in0=az[:, tap:tap + T], scalar=w,
                                                               in1=ay[:, :], op0=ALU.mult, op1=ALU.add)
                            ins.then_inc(sconv, 1)
                        dve.wait_ge(sconv, 4 * c + 3)
                        dve.tensor_tensor(ay[:, :], ay[:, :], rs[:, :], ALU.mult).then_inc(sconv, 1)
                    if kind == 2:
                        dve.wait_ge(sconv, 4 * c + 4)
                        split_value("a_gate", c, lambda dst: dve.tensor_tensor(dst, ay[:, :], bank[2][:, :], ALU.mult))
                        low_of("a_gate", c, acat_lo[:, c, :], acat_hi[:, c, :])
                if hd % 2:
                    c = 4 + hd // 2
                    dve.wait_ge(oh_ready, hd // 2 + 1)
                    dve.tensor_tensor(acat_lo[:, c, :], bank[3][:, :], acat_hi[:, c, :].bitcast(F32), ALU.subtract)\
                       .then_inc(ol_ready, 1)
            keep_out("a_out", "a_post")
            norm_add("a_mix", "mix_post", 0, "a_fpre", "a_fpre")
            feed_forward("a", None)
            keep_ffn("a", "a_fpost")
            norm_add("a_ffn", "ffn_post", 0, "b_pre", "b_pre")

            dve.memset(bz[:, :, 0:LONG_TAPS - 1], 0.0)
            dve.wait_ge(wt_ready, 1)
            dve.tensor_tensor(wt_lo[:, :], col("w_dw", 0, LONG_TAPS * KC), wt_hi[:, :].bitcast(F32), ALU.subtract)\
               .then_inc(wt_ready, 1)
            dve.wait_ge(rs_ready, RS["b_pre"] + 1)
            for item in TAP_ITEMS:
                c = item[1]
                if item[0] == "slot":
                    n = item[1]
                    dve.wait_ge(slot_done, SLOT["b_in"] + n + 1)
                    after(dve, bz_ready, n // 2 - 1)
                    dve.tensor_tensor(ba[:, n // 2 % 2, n % 2, :], bank[n % 4][:, :], rs[:, :], ALU.mult).then_inc(b_evac, 1)
                elif item[0] == "gated":
                    dve.wait_ge(b_evac, 2 * c + 1)
                    dve.wait_ge(b_sig, c + 1)
                    dve.scalar_tensor_tensor(out=bz[:, c, LONG_TAPS - 1:], in0=ba[:, c % 2, 0, :], scalar=col("b_pw1", c),
                                             in1=ba[:, c % 2, 1, :], op0=ALU.add, op1=ALU.mult).then_inc(bz_ready, 1)
                elif item[0] == "low":
                    i = PE_CHUNKS.index(c)
                    dve.wait_ge(zh_ready, i + 1)
                    dve.tensor_tensor(bz_lo[:, i, :], bz[:, c, :], bz_hi[:, i, :].bitcast(F32), ALU.subtract).then_inc(zl_ready, 1)
                else:
                    tap = item[2]
                    w = col("w_dw", tap * KC + c)
                    if tap == 0:
                        dve.wait_ge(bz_ready, c + 1)
                        ins = dve.tensor_scalar(by[:, c, :], bz[:, c, 0:T], w, col("b_dw", c), ALU.mult, ALU.add)
                    else:
                        dve.wait_ge(taps, TAP_DONE[c, tap - 1])
                        ins = dve.scalar_tensor_tensor(out=by[:, c, :], in0=bz[:, c, tap:tap + T], scalar=w, in1=by[:, c, :],
                                                       op0=ALU.mult, op1=ALU.add)
                    ins.then_inc(taps, 1)
            dve.wait_ge(taps, len(TAP_DONE))
            dve.wait_ge(shared_taps, LONG_TAPS - SHARED_FROM)
            dve.tensor_tensor(by[:, SHARED, :], by[:, SHARED, :], bpart[:, :], ALU.add).then_inc(taps, 1)
            dve.wait_ge(mean_ready, 1)
            for c in range(KC):
                dve.tensor_tensor(by[:, c, :], by[:, c, :], bmean[:, :], ALU.subtract).then_inc(xc_ready, 1)
            dve.wait_ge(rs_ready, RS["b_var"] + 1)
            for c in range(KC + 2):
                if c < KC:
                    dve.tensor_tensor(by[:, c, :], by[:, c, :], rs[:, :], ALU.mult).then_inc(yn_ready, 1)
                if c >= 2:
                    low_of("b_ln", c - 2, by_lo[:, c - 2, :], by_hi[:, c - 2, :])
            keep_out("b_out", "b_post", lambda n: col("b_pw2", n))
            norm_add("b_mix", "mix_post", KC, "b_fpre", "b_fpre")
            feed_forward("b", None)
            keep_ffn("b", "b_fpost")
            norm_add("b_ffn", "ffn_post", KC, "c_pre", "c_pre")

            l0, l1, e0, e1 = col("lb_logits", 0, KC), col("lb_logits", KC, KC), small[:, 16:24], small[:, 24:32]
            lb, rest, top = small[:, 0:8], small[:, 8:16], small[:, 32:40]
            dve.tensor_tensor(top, l0, l1, ALU.max).then_inc(lb_step, 1)
            dve.wait_ge(lb_step, 1)
            dve.tensor_tensor(e0, l0, top, ALU.subtract).then_inc(lb_step, 1)
            dve.tensor_tensor(e1, l1, top, ALU.subtract).then_inc(lb_step, 1)
            dve.wait_ge(lb_step, 4)
            dve.tensor_tensor(top, e0, e1, ALU.add).then_inc(lb_step, 1)
            dve.wait_ge(lb_step, 5)
            dve.reciprocal(top, top).then_inc(lb_step, 1)
            dve.wait_ge(lb_step, 6)
            dve.tensor_tensor(lb, e0, top, ALU.mult).then_inc(lb_step, 1)
            dve.wait_ge(lb_step, 7)
            dve.tensor_scalar(rest, lb, -1.0, 1.0, ALU.mult, ALU.add).then_inc(lb_step, 1)
            dve.wait_ge(lb_step, 8)
            dve.wait_ge(rs_ready, RS["c_pre"] + 1)
            for n in range(17):
                if n < 16:
                    c = n // 2
                    dve.wait_ge(slot_done, SLOT["c_fq"] + n + 1)
                    if n % 2 and c >= 2:
                        dve.wait_ge(c_qkf, 3 * (c - 1))
                    dve.tensor_tensor(ut[:, c % 2, :] if n % 2 else cf[:, c, :], bank[n % 4][:, :], rs[:, :], ALU.mult)\
                       .then_inc(c_evac, 1)
                if n == 0:
                    continue
                c = (n - 1) // 2
                dve.wait_ge(c_sig, n)
                if n % 2:
                    dve.tensor_scalar(cf[:, c, :], cf[:, c, :], rest[:, c:c + 1], lb[:, c:c + 1], ALU.mult, ALU.add)\
                       .then_inc(c_qkf, 1)
                    dve.wait_ge(c_qkf, 3 * c + 1)
                    dve.tensor_scalar(ck[:, c, :], cf[:, c, :], -1.0, 1.0, ALU.mult, ALU.add).then_inc(c_qkf, 1)
                else:
                    dve.scalar_tensor_tensor(out=cq[:, c, :], in0=cq[:, c, :], scalar=P ** -0.5, in1=ut[:, c % 2, :],
                                             op0=ALU.mult, op1=ALU.mult).then_inc(c_qkf, 1)
            dve.wait_ge(c_qkf, 3 * KC)
            dve.wait_ge(mask_landed, 16)

            def keep_level(g, lv, e):
                dve.wait_ge(level_full, 4 * (8 * g + lv) + e + 1)
                if g and lv == 0:
                    dve.wait_ge(co_full, e + 1)
                if lv == 0:
                    kept = ca[:, e, :].rearrange("p (t s) -> p t s", t=TT)
                    found = bank[4 + e][:, :].rearrange("p (t s) -> p t s", t=TT)
                    mask = ident.unsqueeze(1).to_broadcast([P, TT, P])
                    dve.tensor_tensor(kept, found, mask, ALU.mult).then_inc(level_kept, 1)
                else:
                    dve.wait_ge(level_kept, 4 * (8 * g + lv - 1) + e + 1)
                    mm = LEVELS[lv - 1]
                    nb = P // (2 * mm)
                    kept = ca[:, e, :].rearrange("p (t b two s) -> p t b two s", t=TT, two=2, s=mm)[:, :, :, 1, :]
                    found = bank[4 + e][:, 0:T // 2].rearrange("p (t b s) -> p t b s", t=TT, s=mm)
                    mask = cmask[:, lv - 1, :].bitcast(U32).rearrange("p (b s) -> p b s", s=mm)\
                        .unsqueeze(1).to_broadcast([P, TT, nb, mm])
                    dve.copy_predicated(kept, mask, found).then_inc(level_kept, 1)

            def products(level, hd, e):
                if level == 0:
                    return cf[:, hd, :]
                return (ct1 if level % 2 else ct2)[:, e, 0:T >> level]

            def decay(g, lv, e):
                hd = 4 * g + e
                if lv == 1:
                    dve.tensor_tensor(cq[:, hd, :], cq[:, hd, :], cf[:, hd, :], ALU.mult).then_inc(upd, 1)
                    return
                mm = 1 << (lv - 2)
                nb = T // (2 * mm)
                dve.wait_ge(upd, upd_count(g, lv - 1, e) + (0 if lv == 2 else 1))
                prod = products(lv - 2, hd, e).rearrange("p (b two) -> p b two", two=2)
                q = cq[:, hd, :].rearrange("p (b two s) -> p b two s", two=2, s=mm)[:, :, 1, :]
                k = ck[:, hd, :].rearrange("p (b two s) -> p b two s", two=2, s=mm)[:, :, 0, :]
                even = prod[:, :, 0].unsqueeze(2).to_broadcast([P, nb, mm])
                odd = prod[:, :, 1].unsqueeze(2).to_broadcast([P, nb, mm])
                dve.tensor_tensor(q, q, even, ALU.mult).then_inc(upd, 1)
                dve.tensor_tensor(k, k, odd, ALU.mult).then_inc(upd, 1)
                dve.tensor_tensor(products(lv - 1, hd, e), prod[:, :, 0], prod[:, :, 1], ALU.mult).then_inc(upd, 1)

            def gate_evac(n):
                dve.wait_ge(slot_done, SLOT["c_g"] + n + 1)
                dve.tensor_tensor(cg[:, n, :], bank[n % 2][:, :], rs[:, :], ALU.mult).then_inc(g_evac, 1)

            def head_value(hd):
                if hd < 4:
                    dve.wait_ge(co_evac, hd + 1)
                    src = cf[:, hd, :]
                else:
                    dve.wait_ge(co_full, hd + 1)
                    dve.wait_ge(sq_ready, SQ["c_head"] + hd + 1)
                    src = bank[hd - 4][:, :]
                dve.wait_ge(g_ready, hd + 1)
                dve.scalar_tensor_tensor(out=cg[:, hd, :], in0=src, scalar=col("hg_out_norm"), in1=cg[:, hd, :],
                                         op0=ALU.mult, op1=ALU.mult).then_inc(cg_mul, 1)

            def head_norm(hd):
                dve.wait_ge(cg_mul, hd + 1)
                dve.wait_ge(rs_ready, RS["c_head"] + hd + 1)
                split_value("c_out", hd, lambda dst: dve.tensor_tensor(
                    dst, cg[:, hd, :], rs_head[:, :] if hd < 4 else ca[:, hd - 4, :], ALU.mult))

            def head_low(hd):
                low_of("c_out", hd, ccat_lo[:, hd, :], ccat_hi[:, hd, :])

            for g in range(2):
                for lv in range(1, 9):
                    for e in range(4):
                        keep_level(g, lv - 1, e)
                        decay(g, lv, e)
                    if g:
                        if 3 <= lv <= 6:
                            head_low(lv - 3)
                        gate_evac(lv - 1)
                        if 2 <= lv <= 5:
                            head_value(lv - 2)
                            head_norm(lv - 2)
                for e in range(4):
                    dve.wait_ge(far_full, 8 * g + e + 1)
                    decay(g, 9, e)
            for hd in range(4, HG_HEADS):
                head_value(hd)
            for hd in range(4, HG_HEADS):
                head_norm(hd)
                if hd > 4:
                    head_low(hd - 1)
            head_low(HG_HEADS - 1)
            add_out("c")
            feed_forward("c", 0)
            add_ffn("c", "d_pre", "d_kv")

            for c in range(KC):
                scaled_low("d_q", c)
            dve.wait_ge(rs_ready, RS["d_pre"] + 1)
            for i in range(2):
                dve.tensor_tensor(ut[:, i, :], bank[i][:, :], rs[:, :], ALU.mult).then_inc(d_kv_evac, 1)

            for kv in range(2):
                for e in range(2):
                    dve.wait_ge(d_kv_ready, 2 * kv + kv + 1)
                    dve.tensor_tensor(dk_lo[rows_of(e), kv, :], ut[rows_of(kv), 0, :], dk_hi[rows_of(kv), kv, :].bitcast(F32), ALU.subtract)\
                       .then_inc(dk_low, 1)

            def query_evac(n):
                dve.wait_ge(slot_done, SLOT["d_q"] + n + 1)
                if n == 0:
                    dve.wait_ge(dk_low, 4)
                elif n == 1:
                    dve.wait_ge(d_vt_full, 1)
                else:
                    dve.wait_ge(dq_low, 2 * n - 2)
                dve.scalar_tensor_tensor(out=ut[:, n % 2, :], in0=bank[2 + n if n < 2 else n % 2][:, :], scalar=SWA_DIM ** -0.5,
                                         in1=rs[:, :], op0=ALU.mult, op1=ALU.mult).then_inc(d_q_evac, 1)

            def query_low(n):
                for e in range(2):
                    dve.wait_ge(dq_high, 2 * n + e + 1)
                    dve.tensor_tensor(dq[rows_of(1 - e), n % 2, e, :], ut[rows_of(e), n % 2, :],
                                      dq[rows_of(e), n % 2, e, :].bitcast(F32), ALU.subtract).then_inc(dq_low, 1)

            query_evac(0)
            query_evac(1)
            query_low(0)
            query_low(1)
            dve.wait_ge(dist_landed, 16)

            def pairs_of(x):
                return x.rearrange("p (n e) -> p n e", e=2)

            def window_add(c):
                if c >= 2:
                    dve.wait_ge(dpt_full, 4 * (c - 1))
                for n in range(TT):
                    lo = 0 if n else P
                    dve.wait_ge(ds_full, 4 * c + 2 * (n // 2) + 2)
                    for e in range(2):
                        slope = 2.0 ** (-8.0 * (2 * c + e + 1) / SWA_HEADS)
                        dve.scalar_tensor_tensor(out=ds_[:, c % 2, n, e, lo:], in0=dist[:, lo:], scalar=-slope,
                                                 in1=window_bank(n, e)[:, lo:], op0=ALU.mult, op1=ALU.add).then_inc(ds_ready, 1)

            def window_max(c):
                top, nm, _, es = window_small(c)
                sink2 = col("sinks", 2 * c, 2).unsqueeze(1).to_broadcast([P, TT, 2])
                for n in range(TT):
                    lo = 0 if n else P
                    dve.wait_ge(ds_ready, 8 * c + 2 * n + 2)
                    dve.tensor_reduce(top[:, 2 * n:2 * n + 2], ds_[:, c % 2, n, :, lo:], AX_X, ALU.max).then_inc(ds_max, 1)
                dve.wait_ge(ds_max, 4 * c + 4)
                dve.tensor_tensor(pairs_of(top), pairs_of(top), sink2, ALU.max).then_inc(ds_m, 1)
                dve.wait_ge(ds_m, c + 1)
                dve.tensor_scalar(nm, top, -1.0, None, ALU.mult).then_inc(ds_nm, 1)
                dve.tensor_tensor(pairs_of(es), sink2, pairs_of(top), ALU.subtract).then_inc(ds_nm, 1)

            def window_probs(c):
                _, _, den, es = window_small(c)
                dve.wait_ge(ds_sink, c + 1)
                dve.wait_ge(ds_exp, 8 * c + 8)
                dve.tensor_tensor(den, den, es, ALU.add).then_inc(ds_den, 1)
                dve.wait_ge(ds_den, 2 * c + 1)
                dve.reciprocal(den, den).then_inc(ds_den, 1)
                dve.wait_ge(ds_den, 2 * c + 2)
                for n in range(TT):
                    lo = 0 if n else P
                    for e in range(2):
                        i, p = 2 * n + e, ds_[:, c % 2, n, e, lo:]
                        dve.tensor_scalar(p, p, den[:, i:i + 1], None, ALU.mult).then_inc(ds_p, 1)

            def window_low(c):
                dve.wait_ge(doh_ready, c + 1)
                dve.tensor_tensor(dcat_lo[:, c, :], bank[2 + c % 2][:, :], dcat_hi[:, c, :].bitcast(F32), ALU.subtract)\
                   .then_inc(dol_ready, 1)

            window_add(0)
            window_max(0)
            query_evac(2)
            for c in range(KC):
                if c + 1 < KC:
                    window_add(c + 1)
                window_probs(c)
                if c + 2 < KC:
                    query_low(c + 2)
                if c + 1 < KC:
                    window_max(c + 1)
                if c:
                    window_low(c - 1)
                if c + 3 < KC:
                    query_evac(c + 3)
            window_low(KC - 1)
            add_out("d")
            feed_forward("d", 1)
            add_ffn("d", "final")
            dve.wait_ge(rs_ready, RS["final"] + 1)
            for i, c in enumerate(DVE_LAST):
                dve.wait_ge(scaled_out, c + 1)
                dve.tensor_tensor(m[:, c, :], m[:, c, :], rs[:, :], ALU.mult).then_inc(y_ready, 1)


def upd_count(g, lv, e):
    per_group = 4 + 8 * 12
    before = 0 if lv <= 1 else 4 + 12 * (lv - 2)
    return per_group * g + before + (e + 1 if lv == 1 else 3 * e + 2)


def kernel(**inputs):
    import numpy as np
    import concourse.bacc as bacc
    from concourse.bass_utils import run_bass_kernel_spmd

    a = {k: np.ascontiguousarray(v) for k, v in inputs.items()}

    def feature_slots(w):
        return w.reshape(KC, P, -1, P).transpose(2, 1, 0, 3).reshape(-1, P, D)

    def token_slots(w):
        return w.reshape(4, 2, P, -1, 512).transpose(3, 0, 2, 1, 4).reshape(-1, P, D)

    def woven(*parts):
        return np.stack(parts, 1).reshape(-1, P, D)

    def ffn(w_in, w_out):
        back = w_out.reshape(HALF, 2, P, 2, 512).transpose(3, 0, 2, 1, 4).reshape(-1, P, D)
        return [woven(feature_slots(w_in[:, :FF]), feature_slots(w_in[:, FF:])), back]

    w_in, w_hg, w_kv = a["w_in"][0], a["hg_w_in_2"][0], a["w_kv_2"]
    w_pw1 = a["w_pw1"][0]
    part = [w_in[:, 512 * i:512 * (i + 1)] for i in range(6)]
    hg = [w_hg[:, D * i:D * (i + 1)] for i in range(4)]
    slots = [feature_slots(part[3]), feature_slots(part[4]), token_slots(part[5]),
             woven(feature_slots(part[1]), feature_slots(part[2]), feature_slots(part[0])),
             feature_slots(a["w_out"][0]), *ffn(a["w_ffn_in"][0], a["w_ffn_out"][0]),
             woven(feature_slots(w_pw1[:, :D]), feature_slots(w_pw1[:, D:])), feature_slots(a["w_pw2"][0]),
             *ffn(a["w_ffn_in"][1], a["w_ffn_out"][1]),
             woven(feature_slots(hg[1]), feature_slots(hg[0])), token_slots(hg[2]), feature_slots(hg[3]),
             feature_slots(a["hg_w_out_2"][0]), *ffn(a["ffn_w_up_2"][0], a["ffn_w_down_2"][0]),
             feature_slots(w_kv), feature_slots(a["attn_w_q_2"][0]), feature_slots(a["attn_w_o_2"][0]),
             *ffn(a["ffn_w_up_2"][1], a["ffn_w_down_2"][1])]
    weights = np.concatenate(slots)
    assert weights.shape == (N_SLOTS, P, D)

    def columns(v):
        return v.reshape(-1, P).T

    forget = w_in[:, 3072:].reshape(KC, P, FOX_HEADS).transpose(1, 0, 2).reshape(P, -1)
    b_forget = np.zeros((P, 1), np.float32)
    b_forget[:FOX_HEADS, 0] = a["b_forget"][0]
    vectors = np.concatenate([
        columns(a["norm_mix_pre"]), columns(a["norm_mix_post"]), columns(a["norm_ffn_pre"]), columns(a["norm_ffn_post"]),
        forget, b_forget, columns(a["w_short_conv"][0]), columns(a["b_pw1"]), columns(a["w_dw"][0]), columns(a["b_dw"]),
        columns(a["ln_g"]), columns(a["ln_b"]), columns(a["b_pw2"]), columns(a["hg_norm_2"]), columns(a["hg_lb_logits_2"]),
        columns(a["hg_out_norm_2"]), columns(a["kv_norm_2"]), columns(a["attn_norm_2"]),
        np.broadcast_to(a["attn_sinks_2"], (P, SWA_HEADS)), columns(a["ffn_norm_2"]), columns(a["ffn_conv_w_2"]),
        columns(a["ffn_conv_b_2"]), columns(a["final_norm_2"])], 1)
    assert vectors.shape == (P, N_VEC)

    row, colm = np.arange(P)[:, None], np.arange(P)[None, :]
    far = row + WINDOW - np.arange(2 * WINDOW)[None, :]
    squares = np.concatenate([np.eye(P), np.where(colm <= row, 0.0, NEVER),
                              np.where((far >= 0) & (far < WINDOW), far, -NEVER)], 1).astype(np.float32)
    select = np.zeros((P, FOX_HEADS, P), np.float32)
    for hd in range(FOX_HEADS):
        select[[hd, LOW_ROW + hd], hd] = -1.0
    second = [np.arange(P).reshape(-1, 2, n)[:, 1].reshape(1, -1) for n in LEVELS]
    masks = np.stack([(row // (2 * n) == q // (2 * n)) & (row // n % 2 == 0) for n, q in zip(LEVELS, second)], 1)
    arrays = {
        "weights": weights, "vectors": vectors, "squares": squares, "select": select, "masks": masks.astype(np.float32),
        "x_t": a["x"][0].T.reshape(KC, P, T).transpose(1, 0, 2),
    }
    nc = bacc.Bacc("TRN2", target_bir_lowering=False, num_devices=1)
    args = []
    for name, v in arrays.items():
        arrays[name] = v = np.ascontiguousarray(v)
        args.append(nc.dram_tensor(f"{name}_dram", v.shape, mybir.dt.from_np(v.dtype), kind="ExternalInput").ap())
    args.append(nc.dram_tensor("out_dram", (P, KC, T), F32, kind="ExternalOutput").ap())
    build(nc, *args)
    r = run_bass_kernel_spmd(nc, [{f"{k}_dram": v for k, v in arrays.items()}], core_ids=[0])
    out = r.results[0]["out_dram"]
    return np.ascontiguousarray(out.transpose(1, 0, 2).reshape(D, T).T)[None]
```
